# Optimizing a Trainium2 kernel written in Bass

```python
import jax, jax.numpy as jnp
from jax import lax
import numpy as np
import math

D_MODEL = 1024
BATCH = 1
SEQ = 512
DEPTH = 1

D_RNN = 1280
RNN_BLOCKS = 10
RNN_BW = D_RNN // RNN_BLOCKS
CONV_W = 4
LRU_C = 8.0
N_HEADS = 8
HEAD_DIM = 128
D_ATT = N_HEADS * HEAD_DIM
KV_RANK = 256
IDX_HEADS = 8
IDX_DIM = 64
TOPK_MAX = 256
Q_BLOCK = 128
IDX_SCALE = IDX_DIM ** -0.5 * IDX_HEADS ** -0.5
ATT_SCALE = HEAD_DIM ** -0.5
N_GROUPS = 4
EXP_PER_GROUP = 8
N_EXPERTS = N_GROUPS * EXP_PER_GROUP
TOP_K_INNER = 2
D_EXPERT = 512
MOE_BLOCK = 128
N_BRANCH = 2
EPS = 1e-6

SPLITS = (D_RNN, D_RNN, D_ATT, KV_RANK, IDX_HEADS * IDX_DIM, IDX_DIM, IDX_HEADS, N_BRANCH * D_MODEL)
D_IN = sum(SPLITS)


def rmsnorm(x, g):
    xf = x.astype(jnp.float32)
    y = xf * lax.rsqrt(jnp.mean(xf * xf, axis=-1, keepdims=True) + EPS)
    return (y * g.astype(jnp.float32)).astype(x.dtype)

def modulate(x, g, shift, scale):
    return rmsnorm(x, g) * (1 + scale[:, None, :]) + shift[:, None, :]

def causal_dwconv(x, w, b):
    y = lax.conv_general_dilated(x, w[:, None, :], window_strides=(1,), padding=[(CONV_W - 1, 0)],
                                 dimension_numbers=('NWC', 'WIO', 'NWC'), feature_group_count=x.shape[-1])
    return y + b

def rg_lru(x, w_a, b_a, w_x, b_x, lam):
    B_, S_, _ = x.shape
    xb = x.reshape(B_, S_, RNN_BLOCKS, RNN_BW)
    r = jax.nn.sigmoid(jnp.einsum('bsnc,ncd->bsnd', xb, w_a).reshape(B_, S_, D_RNN) + b_a)
    i = jax.nn.sigmoid(jnp.einsum('bsnc,ncd->bsnd', xb, w_x).reshape(B_, S_, D_RNN) + b_x)
    log_a = -LRU_C * jax.nn.softplus(-lam.astype(jnp.float32)) * r.astype(jnp.float32)
    a = jnp.exp(log_a)
    inp = jnp.sqrt(-jnp.expm1(2.0 * log_a)) * (i * x).astype(jnp.float32)

    def combine(lhs, rhs):
        a1, b1 = lhs
        a2, b2 = rhs
        return a1 * a2, a2 * b1 + b2

    _, h = lax.associative_scan(combine, (a, inp), axis=1)
    return h.astype(x.dtype)

def dsa_attention(q, c_kv, q_idx, k_idx, w_idx, w_uk, w_uv):
    B_, S_ = q.shape[0], q.shape[1]
    topk = min(TOPK_MAX, S_ // 4)
    nblk = S_ // Q_BLOCK
    slopes = 2.0 ** (-8.0 * jnp.arange(1, N_HEADS + 1, dtype=jnp.float32) / N_HEADS)
    key_pos = jnp.arange(S_)

    def to_blocks(t):
        return jnp.moveaxis(t.reshape((B_, nblk, Q_BLOCK) + t.shape[2:]), 1, 0)

    def one_block(args):
        qb, qib, wib, q0 = args
        qpos = q0 + jnp.arange(Q_BLOCK)
        causal = key_pos[None, :] <= qpos[:, None]
        rel = jax.nn.relu(jnp.einsum('bqhd,bsd->bqhs', qib, k_idx).astype(jnp.float32))
        score = jnp.einsum('bqh,bqhs->bqs', wib.astype(jnp.float32), rel) * IDX_SCALE
        score = jnp.where(causal[None], score, -jnp.inf)
        _, sel = lax.top_k(score, topk)
        c_sel = jax.vmap(lambda cb, ib: cb[ib])(c_kv, sel)
        q_lat = jnp.einsum('bqhd,rhd->bqhr', qb, w_uk)
        logits = jnp.einsum('bqhr,bqkr->bqhk', q_lat, c_sel).astype(jnp.float32) * ATT_SCALE
        dist = (qpos[None, :, None] - sel).astype(jnp.float32)
        logits = logits - slopes[None, None, :, None] * dist[:, :, None, :]
        valid = sel <= qpos[None, :, None]
        logits = jnp.where(valid[:, :, None, :], logits, -jnp.inf)
        p = jax.nn.softmax(logits, axis=-1).astype(c_sel.dtype)
        o_lat = jnp.einsum('bqhk,bqkr->bqhr', p, c_sel)
        return jnp.einsum('bqhr,rhd->bqhd', o_lat, w_uv)

    out = lax.map(one_block, (to_blocks(q), to_blocks(q_idx), to_blocks(w_idx), jnp.arange(nblk) * Q_BLOCK))
    return jnp.moveaxis(out, 0, 1).reshape(B_, S_, N_HEADS * HEAD_DIM)

def hier_moe(x, w_group, b_group, w_expert, b_expert, w1, w3, w2):
    B_, S_, D_ = x.shape
    T = B_ * S_
    xf = x.reshape(T, D_)
    g_logits = (xf @ w_group + b_group).astype(jnp.float32)
    g_sel = jnp.argmax(g_logits, axis=-1)
    g_w = jnp.take_along_axis(jax.nn.softmax(g_logits, axis=-1), g_sel[:, None], axis=-1)
    e_logits = (xf @ w_expert + b_expert).astype(jnp.float32).reshape(T, N_GROUPS, EXP_PER_GROUP)
    e_logits = jnp.take_along_axis(e_logits, g_sel[:, None, None], axis=1)[:, 0]
    e_top, e_loc = lax.top_k(e_logits, TOP_K_INNER)
    gate = (g_w * jax.nn.softmax(e_top, axis=-1)).reshape(-1)
    eid = (g_sel[:, None] * EXP_PER_GROUP + e_loc).reshape(-1)
    tok = jnp.repeat(jnp.arange(T, dtype=jnp.int32), TOP_K_INNER)
    A = T * TOP_K_INNER
    order = jnp.argsort(eid)
    eid_s = eid[order]
    counts = jnp.bincount(eid, length=N_EXPERTS)
    padded = (counts + MOE_BLOCK - 1) // MOE_BLOCK * MOE_BLOCK
    start = jnp.cumsum(counts) - counts
    pstart = jnp.cumsum(padded) - padded
    dest = pstart[eid_s] + jnp.arange(A) - start[eid_s]
    n_rows = A + N_EXPERTS * MOE_BLOCK
    n_blk = n_rows // MOE_BLOCK
    row_tok = jnp.zeros((n_rows,), jnp.int32).at[dest].set(tok[order])
    row_gate = jnp.zeros((n_rows,), x.dtype).at[dest].set(gate[order].astype(x.dtype))
    blk_exp = jnp.minimum(jnp.searchsorted(jnp.cumsum(padded), jnp.arange(n_blk) * MOE_BLOCK, side='right'),
                          N_EXPERTS - 1)
    xs = xf[row_tok].reshape(n_blk, MOE_BLOCK, D_)

    def expert_block(args):
        xb, e = args
        hid = jax.nn.silu(xb @ w1[e]) * (xb @ w3[e])
        return hid @ w2[e]

    ys = lax.map(expert_block, (xs, blk_exp)).reshape(n_rows, D_)
    out = jax.ops.segment_sum(ys * row_gate[:, None], row_tok, num_segments=T)
    return out.reshape(B_, S_, D_)

def _w(k, shape, fan_in, mult=1.0):
    return jax.random.normal(k, shape, jnp.float32) * (mult * fan_in ** -0.5)

def _small(k, shape):
    return 0.01 * jax.random.normal(k, shape, jnp.float32)

def _gain(k, shape):
    return 1.0 + 0.01 * jax.random.normal(k, shape, jnp.float32)

def first_inputs(seed: int = 0) -> dict:
    key = jax.random.key(seed)
    ks = list(jax.random.split(key, 32))
    L = DEPTH
    u = jax.random.uniform(ks.pop(), (L, D_RNN), jnp.float32, minval=0.9, maxval=0.999)
    a0 = u ** (1.0 / LRU_C)
    lru_lambda = jnp.log(a0) - jnp.log1p(-a0)
    return {
        'x': jax.random.normal(ks.pop(), (BATCH, SEQ, D_MODEL), jnp.float32),
        'c': jax.random.normal(ks.pop(), (BATCH, D_MODEL), jnp.float32),
        'w_mod': _w(ks.pop(), (L, D_MODEL, 6 * D_MODEL), D_MODEL, 0.5),
        'b_mod': _small(ks.pop(), (L, 6 * D_MODEL)),
        'norm1_g': _gain(ks.pop(), (L, D_MODEL)),
        'w_in': _w(ks.pop(), (L, D_MODEL, D_IN), D_MODEL),
        'conv_w': _w(ks.pop(), (L, CONV_W, D_RNN), CONV_W),
        'conv_b': _small(ks.pop(), (L, D_RNN)),
        'w_rg_a': _w(ks.pop(), (L, RNN_BLOCKS, RNN_BW, RNN_BW), RNN_BW),
        'b_rg_a': _small(ks.pop(), (L, D_RNN)),
        'w_rg_x': _w(ks.pop(), (L, RNN_BLOCKS, RNN_BW, RNN_BW), RNN_BW),
        'b_rg_x': _small(ks.pop(), (L, D_RNN)),
        'lru_lambda': lru_lambda,
        'kv_norm_g': _gain(ks.pop(), (L, KV_RANK)),
        'w_uk': _w(ks.pop(), (L, KV_RANK, N_HEADS, HEAD_DIM), KV_RANK),
        'w_uv': _w(ks.pop(), (L, KV_RANK, N_HEADS, HEAD_DIM), KV_RANK),
        'w_rnn_out': _w(ks.pop(), (L, D_RNN, D_MODEL), D_RNN),
        'w_att_out': _w(ks.pop(), (L, D_ATT, D_MODEL), D_ATT),
        'w_out': _w(ks.pop(), (L, D_MODEL, D_MODEL), D_MODEL),
        'norm2_g': _gain(ks.pop(), (L, D_MODEL)),
        'w_group': _w(ks.pop(), (L, D_MODEL, N_GROUPS), D_MODEL),
        'b_group': _small(ks.pop(), (L, N_GROUPS)),
        'w_expert': _w(ks.pop(), (L, D_MODEL, N_EXPERTS), D_MODEL),
        'b_expert': _small(ks.pop(), (L, N_EXPERTS)),
        'moe_w1': _w(ks.pop(), (L, N_EXPERTS, D_MODEL, D_EXPERT), D_MODEL),
        'moe_w3': _w(ks.pop(), (L, N_EXPERTS, D_MODEL, D_EXPERT), D_MODEL),
        'moe_w2': _w(ks.pop(), (L, N_EXPERTS, D_EXPERT, D_MODEL), D_EXPERT),
        'final_g': _gain(ks.pop(), (D_MODEL,)),
    }

def first_block(x, c, w_mod, b_mod, norm1_g, w_in, conv_w, conv_b, w_rg_a, b_rg_a, w_rg_x, b_rg_x,
              lru_lambda, kv_norm_g, w_uk, w_uv, w_rnn_out, w_att_out, w_out, norm2_g, w_group, b_group,
              w_expert, b_expert, moe_w1, moe_w3, moe_w2, final_g):
    B_, S_, _ = x.shape
    split_pts = [int(v) for v in np.cumsum(SPLITS)[:-1]]
    h = x
    for l in range(DEPTH):
        mod = jax.nn.silu(c) @ w_mod[l] + b_mod[l]
        sh1, sc1, g1, sh2, sc2, g2 = jnp.split(mod, 6, axis=-1)
        u = modulate(h, norm1_g[l], sh1, sc1)
        proj = u @ w_in[l]
        xr, gr, q, ckv, qi, ki, wi, mg = jnp.split(proj, split_pts, axis=-1)
        hr = rg_lru(causal_dwconv(xr, conv_w[l], conv_b[l]), w_rg_a[l], b_rg_a[l], w_rg_x[l], b_rg_x[l],
                    lru_lambda[l])
        y_a = (jax.nn.gelu(gr) * hr) @ w_rnn_out[l]
        att = dsa_attention(q.reshape(B_, S_, N_HEADS, HEAD_DIM), rmsnorm(ckv, kv_norm_g[l]),
                            qi.reshape(B_, S_, IDX_HEADS, IDX_DIM), ki, wi, w_uk[l], w_uv[l])
        y_b = att @ w_att_out[l]
        ga, gb = jnp.split(jax.nn.sigmoid(mg), N_BRANCH, axis=-1)
        mix = (ga * y_a + gb * y_b) @ w_out[l]
        h = h + g1[:, None, :] * mix
        u2 = modulate(h, norm2_g[l], sh2, sc2)
        h = h + g2[:, None, :] * hier_moe(u2, w_group[l], b_group[l], w_expert[l], b_expert[l],
                                          moe_w1[l], moe_w3[l], moe_w2[l])
    return rmsnorm(h, final_g)


DEPTH_2 = 2

GRID_W = 64
NA_HEADS = 8
NA_HEAD_DIM = 64
NA_WIDTH = NA_HEADS * NA_HEAD_DIM
NA_WIN_ROWS = 8
NA_WIN_COLS = 16
NA_COL_BLOCK = NA_WIN_COLS
NA_KEY_COL_BLOCK = 2 * NA_WIN_COLS
DIFF_HEADS = 4
DIFF_HEAD_DIM = 64
DIFF_QK_WIDTH = DIFF_HEADS * 2 * DIFF_HEAD_DIM
DIFF_V_WIDTH = DIFF_HEADS * 2 * DIFF_HEAD_DIM
MLA_HEADS = 8
MLA_NOPE_DIM = 64
MLA_ROPE_DIM = 32
MLA_V_DIM = 64
MLA_Q_RANK = 384
MLA_KV_RANK = 256
MLA_WIDTH = MLA_HEADS * MLA_V_DIM
N_BRANCH_2 = 3
BRANCH_WIDTH = 512
D_IN_2 = 3 * NA_WIDTH + 2 * DIFF_QK_WIDTH + DIFF_V_WIDTH + MLA_Q_RANK + MLA_KV_RANK + MLA_ROPE_DIM + N_BRANCH_2 * D_MODEL
D_FF = -(-8 * D_MODEL // (3 * 256)) * 256
ROPE_THETA = 500000.0
DIFF_ROT_DIM = DIFF_HEAD_DIM // 4
DN_ALPHA = (2 * DEPTH_2) ** 0.25
DN_BETA = (8 * DEPTH_2) ** -0.25
LN_EPS = 1e-5
RMS_EPS = 1e-6


def layer_norm(x, g, b):
    xf = x.astype(jnp.float32)
    mu = jnp.mean(xf, -1, keepdims=True)
    var = jnp.mean(jnp.square(xf - mu), -1, keepdims=True)
    return ((xf - mu) * lax.rsqrt(var + LN_EPS) * g.astype(jnp.float32) + b.astype(jnp.float32)).astype(x.dtype)

def rms_norm(x, g):
    xf = x.astype(jnp.float32)
    return (xf * lax.rsqrt(jnp.mean(xf * xf, -1, keepdims=True) + RMS_EPS) * g.astype(jnp.float32)).astype(x.dtype)

def rope(x, rot_dim):
    s = x.shape[1]
    half = rot_dim // 2
    inv_freq = jnp.exp(-math.log(ROPE_THETA) * jnp.arange(half, dtype=jnp.float32) / half)
    ang = jnp.arange(s, dtype=jnp.float32)[:, None] * inv_freq[None, :]
    cos = jnp.cos(ang)[None, :, None, :]
    sin = jnp.sin(ang)[None, :, None, :]
    xr = x[..., :rot_dim].astype(jnp.float32)
    x1, x2 = xr[..., :half], xr[..., half:]
    rot = jnp.concatenate([x1 * cos - x2 * sin, x2 * cos + x1 * sin], -1).astype(x.dtype)
    return jnp.concatenate([rot, x[..., rot_dim:]], -1)

def blocked_attention(q, k, v, scale):
    b, s, h, dq = q.shape
    nb = s // Q_BLOCK
    qb = q.reshape(b, nb, Q_BLOCK, h, dq).transpose(1, 0, 2, 3, 4)

    def one_block(qi):
        sc = jnp.einsum('bqhd,bkhd->bhqk', qi, k, preferred_element_type=jnp.float32) * scale
        p = jax.nn.softmax(sc, axis=-1).astype(v.dtype)
        return jnp.einsum('bhqk,bkhd->bqhd', p, v)

    out = lax.map(one_block, qb)
    return out.transpose(1, 0, 2, 3, 4).reshape(b, s, h, v.shape[-1])

def neighbourhood_attention(q, k, v, rpb):
    b, s, h, d = q.shape
    rows = s // GRID_W
    kr = min(NA_WIN_ROWS, rows)
    kc = NA_WIN_COLS
    ncb = GRID_W // NA_COL_BLOCK
    qg = q.reshape(b, rows, GRID_W, h, d)
    kg = k.reshape(b, rows, GRID_W, h, d)
    vg = v.reshape(b, rows, GRID_W, h, d)
    qcol = jnp.arange(GRID_W).reshape(ncb, NA_COL_BLOCK)
    kstart = jnp.clip(jnp.arange(ncb) * NA_COL_BLOCK - kc // 2, 0, GRID_W - NA_KEY_COL_BLOCK)
    kcol = kstart[:, None] + jnp.arange(NA_KEY_COL_BLOCK)[None, :]
    wstart = jnp.clip(qcol - kc // 2, 0, GRID_W - kc)
    col_valid = (kcol[:, None, :] >= wstart[:, :, None]) & (kcol[:, None, :] < wstart[:, :, None] + kc)
    dcol_idx = jnp.clip(kcol[:, None, :] - qcol[:, :, None], -(kc - 1), kc - 1) + (kc - 1)
    row_center = NA_WIN_ROWS - 1
    scale = d ** -0.5

    def one_row(r):
        rs = jnp.clip(r - kr // 2, 0, rows - kr)
        qr = lax.dynamic_index_in_dim(qg, r, axis=1, keepdims=False)
        k_rows = lax.dynamic_slice_in_dim(kg, rs, kr, axis=1)
        v_rows = lax.dynamic_slice_in_dim(vg, rs, kr, axis=1)
        kb = jnp.take(k_rows, kcol, axis=2)
        vb = jnp.take(v_rows, kcol, axis=2)
        qb = qr.reshape(b, ncb, NA_COL_BLOCK, h, d)
        sc = jnp.einsum('bnqhd,banchd->bhnqac', qb, kb, preferred_element_type=jnp.float32) * scale
        drow = rs + jnp.arange(kr) - r + row_center
        bias = rpb[:, drow][:, :, dcol_idx].transpose(0, 2, 3, 1, 4)
        sc = sc + bias[None].astype(jnp.float32)
        sc = jnp.where(col_valid[None, None, :, :, None, :], sc, -jnp.inf)
        p = jax.nn.softmax(sc, axis=(-2, -1)).astype(v.dtype)
        o = jnp.einsum('bhnqac,banchd->bnqhd', p, vb)
        return o.reshape(b, GRID_W, h, d)

    out = lax.map(one_row, jnp.arange(rows))
    return out.transpose(1, 0, 2, 3, 4).reshape(b, s, h * d)

def diff_attention(q, k, v, lam_vecs, subln_g, lam_init):
    b, s, _ = q.shape
    q = q.reshape(b, s, DIFF_HEADS, 2, DIFF_HEAD_DIM)
    k = k.reshape(b, s, DIFF_HEADS, 2, DIFF_HEAD_DIM)
    v = v.reshape(b, s, DIFF_HEADS, 2 * DIFF_HEAD_DIM)
    q1, q2 = rope(q[:, :, :, 0], DIFF_ROT_DIM), rope(q[:, :, :, 1], DIFF_ROT_DIM)
    k1, k2 = rope(k[:, :, :, 0], DIFF_ROT_DIM), rope(k[:, :, :, 1], DIFF_ROT_DIM)
    lv = lam_vecs.astype(jnp.float32)
    lam = jnp.exp(jnp.sum(lv[0] * lv[1])) - jnp.exp(jnp.sum(lv[2] * lv[3])) + lam_init
    scale = DIFF_HEAD_DIM ** -0.5
    a1 = blocked_attention(q1, k1, v, scale)
    a2 = blocked_attention(q2, k2, v, scale)
    o = a1 - lam.astype(a1.dtype) * a2
    o = rms_norm(o, subln_g) * (1.0 - lam_init)
    return o.reshape(b, s, DIFF_V_WIDTH)

def latent_attention(c_q, c_kv, k_rope, w_qb, w_kvb, q_norm_g, kv_norm_g):
    b, s, _ = c_q.shape
    q = jnp.einsum('bsr,re->bse', rms_norm(c_q, q_norm_g), w_qb).reshape(b, s, MLA_HEADS, MLA_NOPE_DIM + MLA_ROPE_DIM)
    q = jnp.concatenate([q[..., :MLA_NOPE_DIM], rope(q[..., MLA_NOPE_DIM:], MLA_ROPE_DIM)], -1)
    kv = jnp.einsum('bsr,re->bse', rms_norm(c_kv, kv_norm_g), w_kvb).reshape(b, s, MLA_HEADS, MLA_NOPE_DIM + MLA_V_DIM)
    k_nope, v = kv[..., :MLA_NOPE_DIM], kv[..., MLA_NOPE_DIM:]
    k_r = rope(k_rope[:, :, None, :], MLA_ROPE_DIM)
    k = jnp.concatenate([k_nope, jnp.broadcast_to(k_r, (b, s, MLA_HEADS, MLA_ROPE_DIM))], -1)
    o = blocked_attention(q, k, v, (MLA_NOPE_DIM + MLA_ROPE_DIM) ** -0.5)
    return o.reshape(b, s, MLA_WIDTH)

def second_inputs(seed: int = 0) -> dict:
    key = jax.random.key(seed)
    ks = jax.random.split(key, 20)

    def nrm(k, shape, s):
        return jax.random.normal(k, shape, jnp.float32) * s

    return {
        "x": nrm(ks[0], (BATCH, SEQ, D_MODEL), 1.0),
        "ln_in_g": 1.0 + nrm(ks[1], (D_MODEL,), 0.02),
        "ln_in_b": nrm(ks[2], (D_MODEL,), 0.02),
        "w_in": nrm(ks[3], (DEPTH_2, D_MODEL, D_IN_2), D_MODEL ** -0.5),
        "b_gate": nrm(ks[4], (DEPTH_2, N_BRANCH_2 * D_MODEL), 0.02),
        "na_rpb": nrm(ks[5], (DEPTH_2, NA_HEADS, 2 * NA_WIN_ROWS - 1, 2 * NA_WIN_COLS - 1), 0.02),
        "diff_lambda": nrm(ks[6], (DEPTH_2, 4, DIFF_HEAD_DIM), 0.1),
        "diff_subln_g": 1.0 + nrm(ks[7], (DEPTH_2, 2 * DIFF_HEAD_DIM), 0.02),
        "mla_q_norm_g": 1.0 + nrm(ks[8], (DEPTH_2, MLA_Q_RANK), 0.02),
        "mla_kv_norm_g": 1.0 + nrm(ks[9], (DEPTH_2, MLA_KV_RANK), 0.02),
        "w_mla_qb": nrm(ks[10], (DEPTH_2, MLA_Q_RANK, MLA_HEADS * (MLA_NOPE_DIM + MLA_ROPE_DIM)), MLA_Q_RANK ** -0.5),
        "w_mla_kvb": nrm(ks[11], (DEPTH_2, MLA_KV_RANK, MLA_HEADS * (MLA_NOPE_DIM + MLA_V_DIM)), MLA_KV_RANK ** -0.5),
        "w_branch": nrm(ks[12], (DEPTH_2, N_BRANCH_2, BRANCH_WIDTH, D_MODEL), BRANCH_WIDTH ** -0.5 * DN_BETA),
        "w_out": nrm(ks[13], (DEPTH_2, D_MODEL, D_MODEL), D_MODEL ** -0.5 * DN_BETA),
        "ln1_g": 1.0 + nrm(ks[14], (DEPTH_2, D_MODEL), 0.02),
        "ln1_b": nrm(ks[15], (DEPTH_2, D_MODEL), 0.02),
        "w_ffn_in": nrm(ks[16], (DEPTH_2, D_MODEL, 2 * D_FF), D_MODEL ** -0.5),
        "w_ffn_out": nrm(ks[17], (DEPTH_2, D_FF, D_MODEL), D_FF ** -0.5 * DN_BETA),
        "ln2_g": 1.0 + nrm(ks[18], (DEPTH_2, D_MODEL), 0.02),
        "ln2_b": nrm(ks[19], (DEPTH_2, D_MODEL), 0.02),
    }

def second_block(x, ln_in_g, ln_in_b, w_in, b_gate, na_rpb, diff_lambda, diff_subln_g,
              mla_q_norm_g, mla_kv_norm_g, w_mla_qb, w_mla_kvb, w_branch, w_out,
              ln1_g, ln1_b, w_ffn_in, w_ffn_out, ln2_g, ln2_b):
    b, s, _ = x.shape
    sizes = (NA_WIDTH, NA_WIDTH, NA_WIDTH, DIFF_QK_WIDTH, DIFF_QK_WIDTH, DIFF_V_WIDTH,
             MLA_Q_RANK, MLA_KV_RANK, MLA_ROPE_DIM, N_BRANCH_2 * D_MODEL)
    split_points = np.cumsum(sizes)[:-1].tolist()

    x = layer_norm(x, ln_in_g, ln_in_b)
    for l in range(DEPTH_2):
        lam_init = 0.8 - 0.6 * math.exp(-0.3 * l)
        proj = jnp.einsum('bsd,de->bse', x, w_in[l])
        (na_q, na_k, na_v, df_q, df_k, df_v, m_cq, m_ckv, m_kr, gate_pre) = jnp.split(proj, split_points, axis=-1)

        na_out = neighbourhood_attention(
            na_q.reshape(b, s, NA_HEADS, NA_HEAD_DIM), na_k.reshape(b, s, NA_HEADS, NA_HEAD_DIM),
            na_v.reshape(b, s, NA_HEADS, NA_HEAD_DIM), na_rpb[l])
        df_out = diff_attention(df_q, df_k, df_v, diff_lambda[l], diff_subln_g[l], lam_init)
        mla_out = latent_attention(m_cq, m_ckv, m_kr, w_mla_qb[l], w_mla_kvb[l],
                                   mla_q_norm_g[l], mla_kv_norm_g[l])

        gates = jax.nn.sigmoid((gate_pre + b_gate[l]).astype(jnp.float32)).astype(x.dtype)
        gates = gates.reshape(b, s, N_BRANCH_2, D_MODEL)
        merged = (gates[:, :, 0] * jnp.einsum('bse,ed->bsd', na_out, w_branch[l, 0])
                  + gates[:, :, 1] * jnp.einsum('bse,ed->bsd', df_out, w_branch[l, 1])
                  + gates[:, :, 2] * jnp.einsum('bse,ed->bsd', mla_out, w_branch[l, 2]))
        mix = jnp.einsum('bsd,de->bse', merged, w_out[l])
        x = layer_norm(DN_ALPHA * x + mix, ln1_g[l], ln1_b[l])

        gu = jnp.einsum('bsd,df->bsf', x, w_ffn_in[l])
        hidden = jax.nn.silu(gu[..., :D_FF]) * gu[..., D_FF:]
        ffn = jnp.einsum('bsf,fd->bsd', hidden, w_ffn_out[l])
        x = layer_norm(DN_ALPHA * x + ffn, ln2_g[l], ln2_b[l])
    return x


def setup_inputs(seed=0):
    out = dict(first_inputs(seed))
    for name, value in second_inputs(seed + 1).items():
        if name != "x":
            out[name + "_2"] = value
    return out


def reference(
    x, c, w_mod, b_mod, norm1_g, w_in, conv_w, conv_b, w_rg_a, b_rg_a, w_rg_x, b_rg_x,
    lru_lambda, kv_norm_g, w_uk, w_uv, w_rnn_out, w_att_out, w_out, norm2_g, w_group, b_group,
    w_expert, b_expert, moe_w1, moe_w3, moe_w2, final_g, ln_in_g_2, ln_in_b_2, w_in_2, b_gate_2,
    na_rpb_2, diff_lambda_2, diff_subln_g_2, mla_q_norm_g_2, mla_kv_norm_g_2, w_mla_qb_2,
    w_mla_kvb_2, w_branch_2, w_out_2, ln1_g_2, ln1_b_2, w_ffn_in_2, w_ffn_out_2, ln2_g_2,
    ln2_b_2,
):
    x = first_block(
        x, c, w_mod, b_mod, norm1_g, w_in, conv_w, conv_b, w_rg_a, b_rg_a, w_rg_x, b_rg_x,
        lru_lambda, kv_norm_g, w_uk, w_uv, w_rnn_out, w_att_out, w_out, norm2_g, w_group,
        b_group, w_expert, b_expert, moe_w1, moe_w3, moe_w2, final_g,
    )
    return second_block(
        x, ln_in_g_2, ln_in_b_2, w_in_2, b_gate_2, na_rpb_2, diff_lambda_2, diff_subln_g_2,
        mla_q_norm_g_2, mla_kv_norm_g_2, w_mla_qb_2, w_mla_kvb_2, w_branch_2, w_out_2, ln1_g_2,
        ln1_b_2, w_ffn_in_2, w_ffn_out_2, ln2_g_2, ln2_b_2,
    )


_drawn_inputs = setup_inputs


def setup_inputs(seed=0):
    import zlib

    import numpy as np

    out = dict(_drawn_inputs(seed))
    spreads = {}
    factors = {'b_mod': 3.206,
     'norm1_g': 5.235,
     'conv_b': 6.79,
     'b_rg_a': 8.0,
     'b_rg_x': 8.0,
     'kv_norm_g': 8.0,
     'norm2_g': 7.306,
     'b_group': 7.373,
     'b_expert': 8.0,
     'final_g': 5.48,
     'b_gate_2': 8.0,
     'na_rpb_2': 8.0,
     'diff_lambda_2': 6.224,
     'diff_subln_g_2': 8.0,
     'mla_q_norm_g_2': 8.0,
     'mla_kv_norm_g_2': 8.0,
     'w_mla_qb_2': 5.013,
     'w_mla_kvb_2': 2.988}
    for name, (base, spread) in spreads.items():
        noise = np.random.default_rng([zlib.crc32(name.encode()), seed]).standard_normal(out[name].shape)
        drawn = base * np.exp(spread * noise) if base else spread * noise
        out[name] = __import__('jax').numpy.asarray(drawn.astype(out[name].dtype))
    for name, factor in factors.items():
        out[name] = (out[name] * factor).astype(out[name].dtype)
    return out
```

```python
from contextlib import ExitStack
import math

import numpy as np

import concourse.bass as bass
from concourse import mybir

P = 128
SEQ = 512
D = 1024
DC = D // P
NQB = SEQ // P
D_RNN = 1280
RC = D_RNN // P
CONV_W = 4
LRU_C = 8.0
HEADS = 8
KV_RANK = 256
KVC = KV_RANK // P
IDX_HEADS = 8
IDX_DIM = 64
IDX_SCALE = IDX_DIM ** -0.5 * IDX_HEADS ** -0.5
TOPK = min(256, SEQ // 4)
DSA_SCALE = P ** -0.5
GROUPS = 4
PER_GROUP = 8
EXPERTS = GROUPS * PER_GROUP
D_EXPERT = 512
EPS = 1e-6
LN_EPS = 1e-5
MOE_BLOCKS = 40
MOE_SURE = 32

LAYERS = 2
D_FF = 2816
FFC = D_FF // P
GRID_W = 64
GRID_ROWS = SEQ // GRID_W
NA_TILES = 4
DN_ALPHA = (2 * LAYERS) ** 0.25
ROPE_THETA = 500000.0
MQ_RANK = 384
MQC = MQ_RANK // P
MLA_QK = 96
NA_SCALE = 64 ** -0.5
DIFF_SCALE = 64 ** -0.5
MLA_SCALE = MLA_QK ** -0.5
NA_KEYS = [(0, 2), (0, 3), (1, 4), (2, 4)]

CHUNKS = 32
SLOTS = 4

OUT_OF_SIGHT = -3.3e38
TAKEN = -3.0e38
LN2_HI = 0.693145751953125
MASKED = -1.0e30

ALU = mybir.AluOpType
ACT = mybir.ActivationFunctionType
AX_X = mybir.AxisListType.X
F32 = mybir.dt.float32
I32 = mybir.dt.int32
U32 = mybir.dt.uint32


def stream_plan():
    first = [("mod_a", 16 * DC), ("xr", RC * DC), ("rg", 2 * RC), ("ckv", KVC * DC), ("qi", 4 * DC), ("ki", DC),
             ("wi", 1), ("gr", RC * DC), ("mod_b", 32 * DC), ("mg", 16 * DC), ("q", HEADS * DC),
             ("rnn_out", DC * RC), ("uk", HEADS * KVC), ("uv", 4 * 2 * KVC), ("att_out", DC * DC),
             ("out", DC * DC), ("router", 3)]
    layer = [("na_v", 4 * DC), ("na_qk", 8 * DC), ("na_gb", DC * (DC + 4)),
             ("df_v", 4 * DC), ("df_qk", 8 * DC), ("df_gb", DC * (DC + 4)),
             ("cq", MQC * DC), ("mckv", KVC * DC), ("kr", DC), ("qb", HEADS * MQC), ("kvb_k", 4 * KVC),
             ("kvb_v", 4 * KVC), ("ml_gb", DC * (DC + 4)),
             ("out2", DC * DC), ("ffn_in", 2 * FFC * DC), ("ffn_out", DC * FFC)]
    blocks = {"uv": 16, "na_v": 32, "df_v": 32, "kvb_v": 8, "router": 4}

    def place(parts, at):
        found = {}
        for name, n in parts:
            if name in blocks:
                at += -at % blocks[name]
            found[name] = at
            at += n
        return found, at + -at % CHUNKS

    one, end = place(first, 0)
    two, size = place(layer, 0)
    return one, end, two, size


def const_plan():
    widths = [("ident", P), ("tri", P), ("ones", P), ("cos_d", SEQ), ("sin_d", SEQ), ("cos_m", SEQ), ("sin_m", SEQ),
              ("perm_d", P), ("perm_m", P), ("dist", 7 * P), ("na_mask", 160), ("causal", P),
              ("block", MOE_BLOCKS), ("first", PER_GROUP), ("token", NQB)]
    at, found = 0, {}
    for name, n in widths:
        found[name] = (at, at + n)
        at += n
    return found, at


def vector_plan():
    widths = [("b_mod", 48), ("norm1_g", 8), ("conv_w", 4 * RC), ("conv_b", RC), ("b_rg_a", RC), ("b_rg_x", RC),
              ("lam", RC), ("kv_g", KVC), ("norm2_g", 8), ("final_g", 8), ("c", 8), ("ln_in_g", 8), ("ln_in_b", 8)]
    for l in range(LAYERS):
        widths += [(f"b_gate{l}", 24), (f"subln{l}", 1), (f"mq_g{l}", MQC), (f"mkv_g{l}", KVC), (f"ln1_g{l}", 8),
                   (f"ln1_b{l}", 8), (f"ln2_g{l}", 8), (f"ln2_b{l}", 8)]
    at, found = 0, {}
    for name, n in widths:
        found[name] = (at, at + n)
        at += n
    return found, at


class Bank:

    def __init__(self, ps, banks, full, free):
        self.ps, self.banks, self.full, self.free = ps, banks, full, free
        self.made, self.took = 0, 0

    def claim(self, pe):
        if self.made >= 2:
            pe.wait_ge(self.free, self.made - 1)
        b = self.banks[self.made % 2]
        self.made += 1
        return self.ps[:, b, :]

    def take(self, eng):
        b = self.banks[self.took % 2]
        self.took += 1
        eng.wait_ge(self.full, self.took)
        return self.ps[:, b, :]


def build(nc, xT, wfirst, wlayers, consts, vectors, brow, lamv, rpb, w1, w3, w2, out):
    one, end1, two, size2 = stream_plan()
    cst, NCONST = const_plan()
    vcol, NVEC = vector_plan()
    n_slots1, n_slots2 = end1 // CHUNKS, size2 // CHUNKS

    with ExitStack() as ctx:

        def at(name, kb, shape, dt=F32):
            return nc.alloc_sbuf_tensor_at(name, shape, dt, offset=(nc.sbuf_base + 31) // 32 * 32 + int(kb * 1024))

        def sem(name):
            return ctx.enter_context(nc.semaphore(name))

        hT = at("hT", 0, [P, DC, SEQ])
        uT = at("uT", 16, [P, DC, SEQ])
        wring = at("wring", 32, [P, SLOTS, CHUNKS * P])
        cs = at("cs", 189, [P, NCONST])
        vec = at("vec", 204.5, [P, NVEC])
        small = at("small", 206, [P, 384])

        def K(name, n=P):
            a, b = cst[name]
            return cs[0:n, a:b]

        def V(name):
            a, b = vcol[name]
            return vec[:, a:b]

        ident, ones = K("ident"), K("ones")
        used = [0]

        def sm(n):
            a = used[0]
            used[0] += n
            assert used[0] <= 384
            return small[:, a:a + n]

        mod = sm(48)
        a1, a2, csil, s_abs, s_z, s_zz, hsp, hbx = sm(8), sm(8), sm(8), sm(RC), sm(RC), sm(RC), sm(RC), sm(RC)
        wi_s = sm(NQB * IDX_HEADS)
        negmax, rsum, rinv = sm(8), sm(8), sm(8)
        lam_prod, lam_two, lam_neg = sm(64), sm(4), sm(2)
        subg, rinv2 = sm(2), sm(8)
        max8 = sm(24)
        s_int = sm(RC).bitcast(I32)
        gate12 = sm(2 * NQB)
        browS = sm(GROUPS + EXPERTS)[0:1, :]
        zeros = at("zeros", 116.5, [P, MOE_BLOCKS + 1], I32)
        xr = at("xr", 96, [P, RC, SEQ + CONV_W])
        rnn = at("rnn", 117, [P, RC, SEQ])
        lru_a = at("lru_a", 137, [P, RC, SEQ])
        lru_t = at("lru_t", 157, [P, 2, 3, SEQ])
        qi = at("qi", 169, [P, 4, SEQ])
        ki = at("ki", 177, [P, SEQ])
        ckv = at("ckv", 179, [P, KVC, SEQ])
        sqb = at("sqb", 183, [P, 2, SEQ])
        acc = at("acc", 187, [P, SEQ])
        qT = at("qT", 96, [P, HEADS, SEQ])
        sel = at("sel", 112, [P, 10, P])
        kT = at("kT", 117, [P, HEADS, SEQ])
        Lb = at("Lb", 133, [P, 2, SEQ])
        mixT = at("mixT", 137, [P, DC, SEQ])
        gb = at("gb", 153, [P, DC, SEQ])
        PT = at("PT", 169, [P, NQB, SEQ])
        Bb = at("Bb", 177, [P, SEQ])
        Pb = at("Pb", 183, [P, 3, SEQ])
        vS = at("vS", 16, [P, NQB, HEADS * P])
        rel = sqb

        mring = at("mring", 32, [P, 2, 3, CHUNKS * P])
        u_tok = at("u_tok", 128, [P, NQB, D])
        gt = at("gt", 144, [P, 2048])
        big = at("big", 152, [P, MOE_BLOCKS * EXPERTS])
        tixI = at("tixI", 157, [P, 2 * NQB], I32)
        destI = at("destI", 157.125, [P, 2 * NQB], I32)
        tokI = at("tokI", 157.25, [P, NQB], I32)
        bexpI = at("bexpI", 157.5, [P, MOE_BLOCKS], I32)
        ids = at("ids", 158, [P, MOE_BLOCKS + 1], I32)
        xs = at("xs", 160, [P, 2, D])
        xsT = at("xsT", 168, [P, 2, DC, P])
        sil = at("sil", 176, [P, D_EXPERT])
        hid = at("hid", 178, [P, D_EXPERT])
        hidT = at("hidT", 180, [P, 4, P])
        ysb = at("ysb", 128, [P, 2, D])
        y_tok = at("y_tok", 96, [P, 2, NQB, D])
        qk2 = at("qk2", 96, [P, 8, SEQ])
        v2 = at("v2", 112, [P, NQB, SEQ])
        near = at("near", 120, [P, 2, 10 * P])
        rp = at("rp", 130, [P, 2, 3 * P])
        P2 = at("P2", 137, [P, 4, SEQ])
        PT2 = at("PT2", 145, [P, NQB, SEQ])
        o2 = at("o2", 153, [P, 4, SEQ])
        raw = at("raw", 161, [P, 2, SEQ])
        sg = at("sg", 165, [P, 2, SEQ])
        cq = at("cq", 169, [P, MQC, SEQ])
        ckv2 = at("ckv2", 175, [P, KVC, SEQ])
        krT = at("krT", 179, [P, SEQ])
        q96 = at("q96", 96, [P, HEADS, SEQ])
        k96 = at("k96", 112, [P, HEADS, SEQ])
        vM = at("vM", 128, [P, NQB, SEQ])
        hidden = at("hidden", 96, [P, FFC, SEQ])
        lamS = at("lamS", 161, [P, LAYERS * 4 * 64])
        table = nc.dram_tensor("table", (P * (MOE_BLOCKS + 1), 1), I32, kind="Internal").ap()
        u_rows = nc.dram_tensor("u_rows", (SEQ, D), F32, kind="Internal").ap()
        y_rows = nc.dram_tensor("y_rows", (MOE_BLOCKS * P, D), F32, kind="Internal").ap()

        ps = ctx.enter_context(nc.psum_tensor("ps", [P, 8, SEQ], F32))

        const_in, vec_in, x_in = sem("const_in"), sem("vec_in"), sem("x_in")
        w_in = [sem(f"w_in{i}") for i in range(SLOTS)]
        w_used = sem("w_used")
        A = Bank(ps, (0, 1), sem("a_full"), sem("a_free"))
        B = Bank(ps, (2, 3), sem("b_full"), sem("b_free"))
        dve_step, act_step, pool_step = sem("dve_step"), sem("act_step"), sem("pool_step")
        c_silu, mod_rdy, pad_rdy = sem("c_silu"), sem("mod_rdy"), sem("pad_rdy")
        squared, sq_added, norm_var, norm_rstd, u_rdy = sem("squared"), sem("sq_added"), sem("norm_var"), sem("norm_rstd"), sem("u_rdy")
        a_coef, sp_rdy, sp_half = sem("a_coef"), sem("sp_rdy"), sem("sp_half")
        xr_rdy, conv_rdy, gate_t, gate_s, gate_a, lru_q = (sem(n) for n in ("xr_rdy", "conv_rdy", "gate_t", "gate_s", "gate_a", "lru_q"))
        lru_sqrt, h_rdy, gelu_rdy, gh_rdy = (sem(n) for n in ("lru_sqrt", "h_rdy", "gelu_rdy", "gh_rdy"))
        ckv_raw, qik_rdy, wi_rdy, ckv_rdy = (sem(n) for n in ("ckv_raw", "qik_rdy", "wi_rdy", "ckv_rdy"))
        g_rdy, q_rdy, k_rdy, v_rdy, mix_rdy, mix2_rdy = (sem(n) for n in ("g_rdy", "q_rdy", "k_rdy", "v_rdy", "mix_rdy", "mix2_rdy"))
        ix_score, ix_rel, ix_acc, sel_rdy = (sem(n) for n in ("ix_score", "ix_rel", "ix_acc", "sel_rdy"))
        sc_rdy, mx_rdy, exp_done, p_norm, turned, pt_rdy, att_rdy = (
            sem(n) for n in ("sc_rdy", "mx_rdy", "exp_done", "p_norm", "turned", "pt_rdy", "att_rdy"))
        h1_rdy = sem("h1_rdy")
        table_clear, brow_in, u_stored, logit_in, ohot, gl_diff, gl_exp, e_diff, e_exp, route_rdy = (sem(n) for n in (
            "table_clear", "brow_in", "u_stored", "logit_in", "ohot", "gl_diff", "gl_exp", "e_diff", "e_exp", "route_rdy"))
        tix_rdy, table_set, ids_in, moe_go = (sem(n) for n in ("tix_rdy", "table_set", "ids_in", "moe_go"))
        xs_in = [sem(f"xs_in{j}") for j in range(2)]
        up_in = [[sem(f"up_in{j}{k}") for k in range(2)] for j in range(2)]
        down_in = [sem(f"down_in{j}") for j in range(2)]
        xt_full, xt_rdy, gate_full, up_full, sil_done, hid_done = (sem(n) for n in (
            "xt_full", "xt_rdy", "gate_full", "up_full", "sil_done", "hid_done"))
        ht_full, ht_rdy, y0_full, y1_full, y0_rdy, y1_rdy = (sem(n) for n in (
            "ht_full", "ht_rdy", "y0_full", "y1_full", "y0_rdy", "y1_rdy"))
        y_stored = [sem(f"y_stored{j}") for j in range(2)]
        rows_back, mixed_rows, h2_rdy, b1_rdy, summed, centered, x_rdy = (sem(n) for n in (
            "rows_back", "mixed_rows", "h2_rdy", "b1_rdy", "summed", "centered", "x_rdy"))
        lam_in, lam_sum, lam_exp, sub_rdy = (sem(n) for n in ("lam_in", "lam_sum", "lam_exp", "sub_rdy"))
        rp_in, near_rdy, roped, vals_rdy, keys_rdy = (sem(n) for n in ("rp_in", "near_rdy", "roped", "vals_rdy", "keys_rdy"))
        s_free, pair_exp, pair_norm, pair_turned, pair_pt = (sem(n) for n in ("s_free", "pair_exp", "pair_norm", "pair_turned", "pair_pt"))
        pair_sc, pair_mx, o_rdy, sg_rdy, sg_used, merged_rdy = (sem(n) for n in ("pair_sc", "pair_mx", "o_rdy", "sg_rdy", "sg_used", "merged_rdy"))
        lat_rdy, kr_rdy, hid_rdy = (sem(n) for n in ("lat_rdy", "kr_rdy", "hid_rdy"))
        stored = sem("stored")

        n_norm = {"act": 0, "dve": 0, "pe": 0, "i": 0}
        cnt = {"sq_a": 0, "sq_d": 0, "sq_p": 0, "nv_a": 0, "nv_d": 0, "dv": 0, "av": 0, "pv": 0}
        plan = {"at": -1, "owed": False}

        def after(eng, ins, s, key):
            ins.then_inc(s, 1)
            cnt[key] += 1
            eng.wait_ge(s, cnt[key])

        def chunk(pe, c, n=1):
            slot = c // CHUNKS
            if slot != plan["at"]:
                assert not plan["owed"]
                plan["owed"] = plan["at"] >= 0
                plan["at"] = slot
                pe.wait_ge(w_in[slot % SLOTS], 16 * (slot // SLOTS + 1))
            o = (c % CHUNKS) * P
            return wring[:, slot % SLOTS, o:o + n * P]

        def said(ins):
            if plan["owed"]:
                ins.then_inc(w_used, 1)
                plan["owed"] = False

        def tile(pe, bank, c0, rhs, nk, m=P, wait=None):
            for k in range(nk):
                w = chunk(pe, c0 + k)
                if wait is not None:
                    wait(k)
                ins = pe.matmul(bank, w[:, 0:m], rhs[:, k, :], start=(k == 0), stop=(k == nk - 1))
                if k < nk - 1:
                    said(ins)
            return ins

        def norm_pe(pe, n):
            cnt["sq_p"] += n
            pe.wait_ge(sq_added, cnt["sq_p"])
            b = B.claim(pe)
            pe.matmul(b, ones, acc[:], start=True, stop=True).then_inc(B.full, 1)

        def squares(act, X, n, wait=None):
            for c in range(n):
                if wait is not None:
                    wait(c)
                k = cnt["sq_a"]
                if k >= 2:
                    act.wait_ge(sq_added, k - 1)
                act.activation(sqb[:, k % 2, :], X[:, c, :], ACT.Square).then_inc(squared, 1)
                cnt["sq_a"] += 1

        def root(act):
            cnt["nv_a"] += 1
            act.wait_ge(norm_var, cnt["nv_a"])
            act.activation(sqb[:, 0, :], acc[:], ACT.Sqrt).then_inc(norm_rstd, 1)

        def sum_squares(dve, n):
            for c in range(n):
                k = cnt["sq_d"]
                dve.wait_ge(squared, k + 1)
                if c == 0:
                    ins = dve.tensor_copy(acc[:], sqb[:, k % 2, :])
                else:
                    ins = dve.tensor_tensor(acc[:], acc[:], sqb[:, k % 2, :], ALU.add)
                ins.then_inc(sq_added, 1)
                cnt["sq_d"] += 1
                dve.wait_ge(sq_added, k + 1)

        def inverse_var(dve, width, eps):
            b = B.take(dve)
            r, v = sqb[:, 0, :], sqb[:, 1, :]
            dve.tensor_scalar(v, b, 1.0 / width, eps, ALU.mult, ALU.add).then_inc(B.free, 1)
            dve.wait_ge(B.free, B.took)
            dve.reciprocal(acc[:], v).then_inc(norm_var, 1)
            cnt["nv_d"] += 1
            dve.wait_ge(norm_rstd, cnt["nv_d"])
            after(dve, dve.tensor_tensor(v, v, r, ALU.mult), dve_step, "dstep")
            after(dve, dve.tensor_tensor(v, v, r, ALU.mult), dve_step, "dstep")
            after(dve, dve.tensor_scalar(v, v, -0.5, 1.5, ALU.mult, ALU.add), dve_step, "dstep")
            after(dve, dve.tensor_tensor(r, r, v, ALU.mult), dve_step, "dstep")

        rstd = sqb[:, 0, :]

        def B_also_free(dve):
            cnt["own"] = cnt.get("own", 0)
            dve.engine_nop().then_inc(B.free, 1)

        def center(dve, X):
            for c in range(1, DC):
                dve.tensor_tensor(acc[:], X[:, 0, :] if c == 1 else acc[:], X[:, c, :], ALU.add).then_inc(summed, 1)
                cnt["sum"] = cnt.get("sum", 0) + 1
                dve.wait_ge(summed, cnt["sum"])
            b = B.take(dve)
            dve.tensor_scalar(acc[:], b, 1.0 / D, None, ALU.mult).then_inc(B.free, 1)
            dve.wait_ge(B.free, B.took)
            for c in range(DC):
                dve.tensor_tensor(X[:, c, :], X[:, c, :], acc[:], ALU.subtract).then_inc(centered, 1)
            cnt["cen"] = cnt.get("cen", 0) + DC
            dve.wait_ge(centered, cnt["cen"])

        def mean_pe(pe):
            cnt["sum_p"] = cnt.get("sum_p", 0) + DC - 1
            pe.wait_ge(summed, cnt["sum_p"])
            pe.matmul(B.claim(pe), ones, acc[:], start=True, stop=True).then_inc(B.full, 1)

        def normed(dve, X, Y, g, b, turn=False):
            sum_squares(dve, DC)
            inverse_var(dve, D, LN_EPS)
            for c in range(DC):
                after(dve, dve.scalar_tensor_tensor(out=X[:, c, :], in0=X[:, c, :], scalar=g[:, c:c + 1], in1=rstd,
                                                    op0=ALU.mult, op1=ALU.mult), dve_step, "dstep")
                x, y = X[:, c, :], Y[:, c, :]
                if turn:
                    x = x.rearrange("p (r j c) -> p r j c", r=GRID_ROWS, j=NA_TILES)
                    y = y.rearrange("p (j r c) -> p r j c", r=GRID_ROWS, j=NA_TILES)
                dve.tensor_scalar(y, x, b[:, c:c + 1], None, ALU.add).then_inc(x_rdy, 1)

        names = {"lg": 144, "gmax": 4, "w": 32, "wm": 4, "goh": 16, "gd": 16, "ge": 16, "es": 32, "m1": 4, "m2": 4,
                 "oh1": 32, "oh2": 32, "d": 4, "ex": 4, "gw": 4, "p1": 4, "M1": 128, "M2": 128, "M": 128, "pos": 128,
                 "cts": 32, "nb": 32, "cum": 32, "st": 32, "bq": 128, "tix": 128, "ix": 4, "be": MOE_BLOCKS}
        starts = dict(zip(names, np.cumsum([0] + list(names.values())).tolist()))

        def T(name):
            return gt[:, starts[name]:starts[name] + names[name]]

        A_ROWS = RC + 2 * RC + KVC + 4 + 1 + 1 + RC + 2 * DC + HEADS + HEADS + 2 * NQB + HEADS

        def units_pe(pe, units, ready, Pb=Pb):
            U = len(units)
            for i in range(U + 3):
                if i < U:
                    u = units[i]
                    k = cnt["pv"] + i
                    ready(i)
                    if k >= 2:
                        pe.wait_ge(exp_done, k - 1)
                    ins = pe.matmul(ps[:, 4 + k % 2, 0:u["nk"] * P], u["q"], u["k"], start=True, stop=True)
                    ins.then_inc(sc_rdy, 1)
                if 2 <= i < U + 2:
                    u = units[i - 2]
                    k = cnt["pv"] + i - 2
                    pe.wait_ge(p_norm, k + 1)
                    if k >= 2:
                        pe.wait_ge(pt_rdy, k - 1)
                    for j in range(u["nk"]):
                        ins = pe.transpose(ps[:, 6 + k % 2, j * P:(j + 1) * P], Pb[:, k % 3, j * P:(j + 1) * P], ident)
                    ins.then_inc(turned, 1)
                if i >= 3 and "sum" in units[i - 3]:
                    pe.wait_ge(pt_rdy, cnt["pv"] + i - 2)
                    units[i - 3]["sum"](pe)
            cnt["pv"] += U

        def units_dve(dve, units, Pb=Pb):
            U = len(units)

            def norm(i):
                k = cnt["dv2"] + i
                n = units[i]["nk"] * P
                dve.wait_ge(exp_done, k + 1)
                after(dve, dve.reciprocal(rinv[:, k % 4:k % 4 + 1], rsum[:, k % 4:k % 4 + 1]), dve_step, "dstep")
                dve.tensor_scalar(Pb[:, k % 3, 0:n], Pb[:, k % 3, 0:n], rinv[:, k % 4:k % 4 + 1], None, ALU.mult).then_inc(p_norm, 1)

            for i, u in enumerate(units):
                k = cnt["dv2"] + i
                n = u["nk"] * P
                dve.wait_ge(sc_rdy, k + 1)
                s = ps[:, 4 + k % 2, 0:n]
                m = negmax[:, k % 4:k % 4 + 1]
                if "bias" in u:
                    b = u["bias"](dve)
                    if k >= 2:
                        dve.wait_ge(exp_done, k - 1)
                    after(dve, dve.scalar_tensor_tensor(out=Lb[:, k % 2, 0:n], in0=s, scalar=u["scale"], in1=b,
                                                        op0=ALU.mult, op1=ALU.add), dve_step, "dstep")
                    dve.reduce_max(m, Lb[:, k % 2, 0:n], AX_X, negate=True).then_inc(mx_rdy, 1)
                else:
                    after(dve, dve.reduce_max(m, s, AX_X, negate=True), dve_step, "dstep")
                    dve.tensor_scalar(m, m, u["scale"], None, ALU.mult).then_inc(mx_rdy, 1)
                if i >= 1:
                    norm(i - 1)
            norm(U - 1)
            cnt["dv2"] += U

        def units_act(act, units, sums, Pb=Pb, PT=PT):
            U = len(units)
            for i in range(U + 3):
                if i < U:
                    u = units[i]
                    k = cnt["av2"] + i
                    n = u["nk"] * P
                    act.wait_ge(mx_rdy, k + 1)
                    if k >= 3:
                        act.wait_ge(turned, k - 2)
                    src, sc = (Lb[:, k % 2, 0:n], 1.0) if "bias" in u else (ps[:, 4 + k % 2, 0:n], u["scale"])
                    act.activation(Pb[:, k % 3, 0:n], src, ACT.Exp, bias=negmax[:, k % 4:k % 4 + 1], scale=sc,
                                   accum_out=rsum[:, k % 4:k % 4 + 1]).then_inc(exp_done, 1)
                if i >= 3 and "sum" in units[i - 3]:
                    sums(units[i - 3])
                if 2 <= i < U + 2:
                    u = units[i - 2]
                    k = cnt["av2"] + i - 2
                    act.wait_ge(turned, k + 1)
                    t = ps[:, 6 + k % 2, 0:u["nk"] * P].rearrange("p (j q) -> p j q", q=P)
                    act.activation(PT[:, 0:u["nk"], u["qb"] * P:(u["qb"] + 1) * P], t, ACT.Copy).then_inc(pt_rdy, 1)
            cnt["av2"] += U

        cnt.update({"dv2": 0, "av2": 0, "dstep": 0, "astep": 0})

        def na_units():
            units, i0 = [], 0
            for h in range(HEADS):
                r, i0 = 64 * (h % 2), 0
                for n, (lo, hi) in enumerate(NA_KEYS):
                    units.append({"nk": hi - lo, "qb": n, "h": h, "scale": NA_SCALE,
                                  "q": qk2[r:r + 64, h // 2, n * P:(n + 1) * P], "k": qk2[r:r + 64, 4 + h // 2, lo * P:hi * P],
                                  "bias": lambda dve, h=h, a=i0, b=i0 + hi - lo, n=n: (
                                      wait_near(dve, h) if n == 0 else None, near[:, h % 2, a * P:b * P])[1]})
                    i0 += hi - lo

                def total(pe, h=h, r=r):
                    b = A.claim(pe)
                    for n, (lo, hi) in enumerate(NA_KEYS):
                        for j in range(lo, hi):
                            ins = pe.matmul(b[r:r + 64, n * P:(n + 1) * P], v2[:, j, h * 64:(h + 1) * 64],
                                            PT2[:, j - lo, n * P:(n + 1) * P], start=(j == lo), stop=(j == hi - 1))
                    ins.then_inc(A.full, 1)
                units[-1]["sum"] = total
            return units

        def wait_near(dve, h):
            cnt["near"] = cnt.get("near", 0) + 1
            dve.wait_ge(near_rdy, cnt["near"])

        def mla_units():
            units = []
            for h in range(HEADS):
                r = 64 * (h % 2)
                for qb in range(NQB):
                    units.append({"nk": NQB, "qb": qb, "h": h, "scale": MLA_SCALE,
                                  "q": q96[0:MLA_QK, h, qb * P:(qb + 1) * P], "k": k96[0:MLA_QK, h, :]})

                def total(pe, h=h, r=r):
                    b = A.claim(pe)
                    for j in range(NQB):
                        ins = pe.matmul(b[r:r + 64, :], vM[:, j, h * 64:(h + 1) * 64], PT2[:, j, :], start=(j == 0), stop=(j == NQB - 1))
                    ins.then_inc(A.full, 1)
                units[-1]["sum"] = total
            return units

        pairs = [(h, qb) for h in range(4) for qb in range(NQB)]
        pair_banks = ((4, 5), (2, 3))

        dsa = []
        for h in range(HEADS):
            for qb in range(NQB):
                dsa.append({"nk": qb + 1, "qb": qb, "h": h, "scale": DSA_SCALE,
                            "q": qT[:, h, qb * P:(qb + 1) * P], "k": kT[:, h, 0:(qb + 1) * P]})

                def bias(dve, h=h, qb=qb):
                    n = (qb + 1) * P
                    o = qb * (qb + 1) // 2
                    d = K("dist")[:, (NQB - 1 - qb) * P:(NQB - 1 - qb) * P + n]
                    after(dve, dve.scalar_tensor_tensor(
                        out=Bb[:, 0:n], in0=d, scalar=-(2.0 ** (-8.0 * (h + 1) / HEADS)),
                        in1=sel[:, o:o + qb + 1, :].rearrange("p j q -> p (j q)"), op0=ALU.mult, op1=ALU.add),
                        dve_step, "dstep")
                    return Bb[:, 0:n]
                dsa[-1]["bias"] = bias

            def total(pe, h=h):
                b = A.claim(pe)
                for j in range(NQB):
                    ins = pe.matmul(b[:, j * P:SEQ], vS[:, j, h * P:(h + 1) * P], PT[:, j, j * P:SEQ],
                                    start=(j == 0), stop=(j == NQB - 1))
                ins.then_inc(A.full, 1)
            dsa[-1]["sum"] = total

        U_DSA = HEADS * NQB
        U_LAYER = 2 * HEADS * NQB

        def layer_pe(pe, l):
            base = {name: end1 + l * size2 + c for name, c in two.items()}
            xT_ = hT

            def rows(c0, bank, k, lhs, start, stop):
                return pe.matmul(bank, lhs, chunk(pe, c0 + 4 * k, 4), start=start, stop=stop)

            def gated(c0, branch):
                for m in range(DC):
                    tile(pe, A.claim(pe), c0 + m * (DC + 4), xT_, DC).then_inc(A.full, 1)
                    tile(pe, B.claim(pe), c0 + m * (DC + 4) + DC, o2, 4).then_inc(B.full, 1)

            pe.wait_ge(x_rdy, DC + 2 * DC * l)
            for j in range(NA_TILES):
                b = A.claim(pe)
                for k in range(DC):
                    ins = rows(base["na_v"], b, k, xT_[:, k, j * P:(j + 1) * P], k == 0, k == DC - 1)
                    if k < DC - 1:
                        said(ins)
                ins.then_inc(A.full, 1)
            for m in range(8):
                tile(pe, A.claim(pe), base["na_qk"] + m * DC, xT_, DC).then_inc(A.full, 1)
            units_pe(pe, na_units(), lambda i: pe.wait_ge(A.free, A.made) if i == 0 else None, P2)
            pe.wait_ge(A.free, A.made)
            gated(base["na_gb"], 0)

            for s_ in range(NQB):
                b = A.claim(pe)
                for k in range(DC):
                    ins = rows(base["df_v"], b, k, xT_[:, k, s_ * P:(s_ + 1) * P], k == 0, k == DC - 1)
                    if k < DC - 1:
                        said(ins)
                ins.then_inc(A.full, 1)

            def turn(perm, m, n=P):
                pe.wait_ge(A.free, m)
                pe.matmul(B.claim(pe)[0:n, :], perm[0:n, 0:n], raw[0:n, (cnt["rp"]) % 2, :], start=True, stop=True).then_inc(B.full, 1)
                cnt["rp"] += 1
            for m in range(8):
                tile(pe, A.claim(pe), base["df_qk"] + m * DC, xT_, DC).then_inc(A.full, 1)
                if m >= 1:
                    turn(K("perm_d"), A.made - 1)
            turn(K("perm_d"), A.made)
            pe.wait_ge(B.free, B.made)
            pe.wait_ge(roped, l * 16 + 8)
            U = len(pairs)
            for i in range(U + 3):
                if i < U:
                    h, qb = pairs[i]
                    k = l * U + i
                    if k >= 2:
                        pe.wait_ge(pair_exp, 2 * (k - 1))
                    for a in range(2):
                        r = 64 * a
                        pe.matmul(ps[:, pair_banks[k % 2][a], :], qk2[r:r + 64, h, qb * P:(qb + 1) * P], qk2[r:r + 64, 4 + h, :],
                                  start=True, stop=True).then_inc(pair_sc, 1)
                if 2 <= i < U + 2:
                    k = l * U + i - 2
                    pe.wait_ge(pair_norm, k + 1)
                    if k >= 2:
                        pe.wait_ge(pair_pt, k - 1)
                    for j in range(NQB):
                        ins = pe.transpose(ps[:, 6 + k % 2, j * P:(j + 1) * P], P2[:, 2 * (k % 2), j * P:(j + 1) * P], ident)
                    ins.then_inc(pair_turned, 1)
                if i >= 3 and pairs[i - 3][1] == NQB - 1:
                    h = pairs[i - 3][0]
                    pe.wait_ge(pair_pt, l * U + i - 2)
                    b = A.claim(pe)
                    for j in range(NQB):
                        ins = pe.matmul(b, v2[:, j, h * P:(h + 1) * P], PT2[:, j, :], start=(j == 0), stop=(j == NQB - 1))
                    ins.then_inc(A.full, 1)
            for h in range(4):
                norm_pe(pe, 1)
            pe.wait_ge(o_rdy, 4 * (l + 1))
            gated(base["df_gb"], 1)

            for m in range(MQC):
                tile(pe, A.claim(pe), base["cq"] + m * DC, xT_, DC).then_inc(A.full, 1)
            for m in range(KVC):
                tile(pe, A.claim(pe), base["mckv"] + m * DC, xT_, DC).then_inc(A.full, 1)
            tile(pe, A.claim(pe)[0:MLA_QK, :], base["kr"], xT_, DC, MLA_QK).then_inc(A.full, 1)
            norm_pe(pe, MQC)
            norm_pe(pe, KVC)
            pe.wait_ge(A.free, A.made)
            pe.matmul(B.claim(pe)[0:MLA_QK, :], K("perm_m")[0:MLA_QK, 0:MLA_QK], krT[0:MLA_QK, :], start=True, stop=True).then_inc(B.full, 1)
            pe.wait_ge(lat_rdy, (l + 1) * (MQC + KVC))
            for h in range(HEADS):
                tile(pe, A.claim(pe)[0:MLA_QK, :], base["qb"] + h * MQC, cq, MQC, MLA_QK).then_inc(A.full, 1)
                if h >= 1:
                    turn(K("perm_m"), A.made - 1, MLA_QK)
            turn(K("perm_m"), A.made, MLA_QK)
            for h in range(HEADS):
                b = A.claim(pe)
                for k in range(KVC):
                    w = chunk(pe, base["kvb_k"] + (h // 2) * KVC + k)
                    ins = pe.matmul(b[0:64, :], w[:, 64 * (h % 2):64 * (h % 2) + 64], ckv2[:, k, :], start=(k == 0), stop=(k == KVC - 1))
                    if k < KVC - 1:
                        said(ins)
                ins.then_inc(A.full, 1)
            for s_ in range(NQB):
                b = A.claim(pe)
                for k in range(KVC):
                    ins = rows(base["kvb_v"], b, k, ckv2[:, k, s_ * P:(s_ + 1) * P], k == 0, k == KVC - 1)
                    if k < KVC - 1:
                        said(ins)
                ins.then_inc(A.full, 1)
            pe.wait_ge(roped, l * 16 + 16)
            pe.wait_ge(keys_rdy, l + 1)
            units_pe(pe, mla_units(), lambda i: pe.wait_ge(A.free, A.made) if i == 0 else None, P2)
            pe.wait_ge(A.free, A.made)
            gated(base["ml_gb"], 2)

            pe.wait_ge(merged_rdy, (l + 1) * 3 * DC)
            for m in range(DC):
                tile(pe, B.claim(pe), base["out2"] + m * DC, uT, DC).then_inc(B.full, 1)
            mean_pe(pe)
            norm_pe(pe, DC)
            pe.wait_ge(x_rdy, DC + 2 * DC * l + DC)
            for m in range(FFC):
                tile(pe, A.claim(pe), base["ffn_in"] + 2 * m * DC, xT_, DC).then_inc(A.full, 1)
                tile(pe, B.claim(pe), base["ffn_in"] + (2 * m + 1) * DC, xT_, DC).then_inc(B.full, 1)
            for m in range(DC):
                tile(pe, B.claim(pe), base["ffn_out"] + m * FFC, hidden, FFC,
                     wait=(lambda k: pe.wait_ge(hid_rdy, l * FFC + k + 1)) if m == 0 else None).then_inc(B.full, 1)
            mean_pe(pe)
            norm_pe(pe, DC)

        def layer_act(act, l):
            def copy(to, n=P):
                act.activation(to, A.take(act)[0:n, :], ACT.Copy).then_inc(A.free, 1)

            def gates(branch):
                bg = V(f"b_gate{l}")
                for m in range(DC):
                    k = (3 * l + branch) * DC + m
                    if k >= 2:
                        act.wait_ge(sg_used, k - 1)
                    act.activation(sg[:, k % 2, :], A.take(act), ACT.Sigmoid, bias=bg[:, branch * DC + m:branch * DC + m + 1]).then_inc(A.free, 1)

            for j in range(NA_TILES):
                copy(v2[:, j, :])
            for m in range(8):
                copy(qk2[:, m, :])

            def na_out(u):
                r = 64 * (u["h"] % 2)
                act.activation(o2[r:r + 64, u["h"] // 2, :], A.take(act)[r:r + 64, :], ACT.Copy).then_inc(A.free, 1)
            units_act(act, na_units(), na_out, P2, PT2)
            gates(0)

            for s_ in range(NQB):
                copy(v2[:, s_, :])
            for m in range(8):
                if m >= 2:
                    act.wait_ge(roped, l * 16 + m - 1)
                copy(raw[:, m % 2, :])
            U = len(pairs)
            for i in range(U + 3):
                if i < U:
                    k = l * U + i
                    if k >= 2:
                        act.wait_ge(pair_turned, k - 1)
                    for a in range(2):
                        act.wait_ge(pair_mx, 2 * k + a + 1)
                        act.activation(P2[:, 2 * (k % 2) + a, :], ps[:, pair_banks[k % 2][a], :], ACT.Exp,
                                       bias=negmax[:, 2 * (k % 2) + a:2 * (k % 2) + a + 1], scale=DIFF_SCALE,
                                       accum_out=rsum[:, 2 * (k % 2) + a:2 * (k % 2) + a + 1]).then_inc(pair_exp, 1)
                if i >= 3 and pairs[i - 3][1] == NQB - 1:
                    copy(o2[:, pairs[i - 3][0], :])
                if 2 <= i < U + 2:
                    k = l * U + i - 2
                    act.wait_ge(pair_turned, k + 1)
                    qb = pairs[i - 2][1]
                    act.activation(PT2[:, :, qb * P:(qb + 1) * P], ps[:, 6 + k % 2, :].rearrange("p (j q) -> p j q", q=P),
                                   ACT.Copy).then_inc(pair_pt, 1)
            act.wait_ge(A.free, A.took)
            for h in range(4):
                if h:
                    act.wait_ge(o_rdy, 4 * l + h)
                squares(act, o2[:, h:h + 1, :], 1)
                root(act)
            gates(1)

            for m in range(MQC):
                copy(cq[:, m, :])
            for m in range(KVC):
                copy(ckv2[:, m, :])
            copy(krT[0:MLA_QK, :], MLA_QK)
            act.wait_ge(A.free, A.took)
            squares(act, cq, MQC)
            root(act)
            act.wait_ge(lat_rdy, l * (MQC + KVC) + MQC)
            squares(act, ckv2, KVC)
            root(act)
            act.wait_ge(kr_rdy, l + 1)
            for h in range(HEADS):
                if h >= 2:
                    act.wait_ge(roped, l * 16 + 8 + h - 1)
                copy(raw[0:MLA_QK, h % 2, :], MLA_QK)
            for h in range(HEADS):
                copy(k96[0:64, h, :], 64)
            for s_ in range(NQB):
                copy(vM[:, s_, :])

            def mla_out(u):
                r = 64 * (u["h"] % 2)
                act.activation(o2[r:r + 64, u["h"] // 2, :], A.take(act)[r:r + 64, :], ACT.Copy).then_inc(A.free, 1)
            units_act(act, mla_units(), mla_out, P2, PT2)
            gates(2)

            squares(act, hT, DC, lambda c: act.wait_ge(centered, DC + 2 * DC * l + c + 1))
            root(act)
            for m in range(FFC):
                k = l * FFC + m
                if k >= 2:
                    act.wait_ge(hid_rdy, k - 1)
                act.activation(raw[:, k % 2, :], A.take(act), ACT.Silu).then_inc(A.free, 1)
            squares(act, hT, DC, lambda c: act.wait_ge(centered, 2 * DC + 2 * DC * l + c + 1))
            root(act)

        def layer_dve(dve, l):
            step = lambda ins: after(dve, ins, dve_step, "dstep")
            TT, TS, STT = dve.tensor_tensor, dve.tensor_scalar, dve.scalar_tensor_tensor

            def branch(n, a_free):
                for m in range(DC):
                    k = (3 * l + n) * DC + m
                    dve.wait_ge(A.free, a_free + m + 1)
                    if n == 0:
                        TT(uT[:, m, :], B.take(dve), sg[:, k % 2, :], ALU.mult).then_inc(B.free, 1)
                        dve.wait_ge(B.free, B.took)
                        dve.engine_nop().then_inc(sg_used, 1)
                        dve.engine_nop().then_inc(merged_rdy, 1)
                    else:
                        TT(sg[:, k % 2, :], B.take(dve), sg[:, k % 2, :], ALU.mult).then_inc(B.free, 1)
                        dve.wait_ge(B.free, B.took)
                        TT(uT[:, m, :], uT[:, m, :], sg[:, k % 2, :], ALU.add).then_inc(sg_used, 1)
                        dve.engine_nop().then_inc(merged_rdy, 1)

            def rope(x, to, cos, sin, n=P):
                step(TT(to, x, cos, ALU.mult))
                TT(x, B.take(dve)[0:n, :] if n != 32 else B.take(dve)[64:MLA_QK, :], sin, ALU.mult).then_inc(B.free, 1)
                dve.wait_ge(B.free, B.took)
                return TT(to, to, x, ALU.add)

            a = A2 + l * A_LAYER
            units_dve(dve, na_units(), P2)
            a += 4 + 8 + HEADS
            branch(0, a)
            a += DC + 4
            for m in range(8):
                dve.wait_ge(A.free, a + m + 1)
                rope(raw[:, m % 2, :], qk2[:, m, :], K("cos_d"), K("sin_d")).then_inc(roped, 1)
            a += 8
            U = len(pairs)

            def pair(i):
                k = l * U + i
                c = 2 * (k % 2)
                dve.wait_ge(pair_exp, 2 * (k + 1))
                step(dve.reciprocal(rinv[:, c:c + 2], rsum[:, c:c + 2]))
                step(TT(rinv[:, c + 1:c + 2], rinv[:, c + 1:c + 2], lam_neg[:, l:l + 1], ALU.mult))
                step(TS(P2[:, c + 1, :], P2[:, c + 1, :], rinv[:, c + 1:c + 2], None, ALU.mult))
                STT(out=P2[:, c, :], in0=P2[:, c, :], scalar=rinv[:, c:c + 1], in1=P2[:, c + 1, :], op0=ALU.mult, op1=ALU.add).then_inc(pair_norm, 1)

            for i in range(U):
                k = l * U + i
                for q in range(2):
                    c = 2 * (k % 2) + q
                    dve.wait_ge(pair_sc, 2 * k + q + 1)
                    step(dve.reduce_max(negmax[:, c:c + 1], ps[:, pair_banks[k % 2][q], :], AX_X, negate=True))
                    TS(negmax[:, c:c + 1], negmax[:, c:c + 1], DIFF_SCALE, None, ALU.mult).then_inc(pair_mx, 1)
                if i >= 1:
                    pair(i - 1)
            pair(U - 1)
            a += 4
            for h in range(4):
                sum_squares(dve, 1)
                inverse_var(dve, P, EPS)
                STT(out=o2[:, h, :], in0=o2[:, h, :], scalar=subg[:, l:l + 1], in1=rstd, op0=ALU.mult, op1=ALU.mult).then_inc(o_rdy, 1)
            branch(1, a)
            a += DC + MQC + KVC + 1
            for X, n, g, width in ((cq, MQC, V(f"mq_g{l}"), MQ_RANK), (ckv2, KVC, V(f"mkv_g{l}"), 256)):
                sum_squares(dve, n)
                inverse_var(dve, width, EPS)
                for c in range(n):
                    STT(out=X[:, c, :], in0=X[:, c, :], scalar=g[:, c:c + 1], in1=rstd, op0=ALU.mult, op1=ALU.mult).then_inc(lat_rdy, 1)
            x = krT[64:MLA_QK, :]
            t = raw[64:MLA_QK, 0, :]
            TT(t, B.take(dve)[64:MLA_QK, :], K("sin_m")[64:MLA_QK, :], ALU.mult).then_inc(B.free, 1)
            step(TT(x, x, K("cos_m")[64:MLA_QK, :], ALU.mult))
            TT(x, x, t, ALU.add).then_inc(kr_rdy, 1)
            for h in range(HEADS):
                dve.wait_ge(A.free, a + h + 1)
                rope(raw[0:MLA_QK, h % 2, :], q96[0:MLA_QK, h, :], K("cos_m")[0:MLA_QK, :], K("sin_m")[0:MLA_QK, :], MLA_QK).then_inc(roped, 1)
            a += HEADS + HEADS + NQB
            units_dve(dve, mla_units(), P2)
            a += HEADS
            branch(2, a)
            a += DC

            def residual():
                for m in range(DC):
                    STT(out=hT[:, m, :], in0=hT[:, m, :], scalar=DN_ALPHA, in1=B.take(dve), op0=ALU.mult, op1=ALU.add).then_inc(B.free, 1)
                dve.wait_ge(B.free, B.took)
            residual()
            center(dve, hT)
            normed(dve, hT, hT, V(f"ln1_g{l}"), V(f"ln1_b{l}"))
            for m in range(FFC):
                dve.wait_ge(A.free, a + m + 1)
                TT(hidden[:, m, :], B.take(dve), raw[:, (l * FFC + m) % 2, :], ALU.mult).then_inc(hid_rdy, 1)
                B_also_free(dve)
            a += FFC
            assert a == A2 + (l + 1) * A_LAYER, (a, A2, A_LAYER)
            residual()
            center(dve, hT)
            normed(dve, hT, hT, V(f"ln2_g{l}"), V(f"ln2_b{l}"))

        A2 = RC + 2 * RC + KVC + 4 + 1 + 1 + RC + 2 * DC + HEADS + HEADS + 2 * NQB + HEADS + 2 * NQB
        A_LAYER = 4 + 8 + HEADS + DC + 4 + 8 + 4 + DC + MQC + KVC + 1 + HEADS + HEADS + NQB + HEADS + DC + FFC
        cnt["rp"] = 0
        block = ctx.enter_context(nc.Block())

        @block.sync
        def _(sp):
            sp.dma_start(vec[:], vectors).then_inc(vec_in, 16)
            sp.dma_start(hT[:], xT).then_inc(x_in, 16)
            sp.dma_start(cs[:], consts).then_inc(const_in, 16)
            for s in range(n_slots1):
                if s >= SLOTS:
                    sp.wait_ge(w_used, s - SLOTS + 1)
                sp.dma_start(wring[:, s % SLOTS, :], wfirst[s]).then_inc(w_in[s % SLOTS], 16)

            for r in range(NQB):
                sp.wait_ge(A.free, A_ROWS + 2 * r + 2)
                sp.dma_start(u_rows[r * P:(r + 1) * P, :], u_tok[:, r, :]).then_inc(u_stored, 16)

            sp.wait_ge(moe_go, 1)
            sp.wait_ge(route_rdy, 1)

            def expert(i, j, b):
                e = sp.value_load(bexpI[0:1, bass.ds(b, 1)], min_val=0, max_val=EXPERTS - 1)
                first = isinstance(i, int) and i == 0
                if not first:
                    sp.wait_ge(up_full, 2 * i + j - 1)
                for k, w in enumerate((w1, w3)):
                    sp.dma_start(mring[:, j, k, :], w[bass.ds(e, 1)].rearrange("e p n -> (e p) n")).then_inc(up_in[j][k], 16)
                if not first:
                    sp.wait_ge(y1_full, 2 * i + j - 1)
                sp.dma_start(mring[:, j, 2, :], w2[bass.ds(e, 1)].rearrange("e p n -> (e p) n")).then_inc(down_in[j], 16)

            for j in range(2):
                expert(0, j, j)
            with sp.Fori(1, MOE_BLOCKS // 2) as i:
                for j in range(2):
                    expert(i, j, 2 * i + j)
            sp.wait_ge(y1_full, MOE_BLOCKS)
            for l in range(LAYERS):
                for s in range(n_slots2):
                    g = n_slots1 + l * n_slots2 + s
                    sp.wait_ge(w_used, g - SLOTS + 1)
                    sp.dma_start(wring[:, g % SLOTS, :], wlayers[l, s]).then_inc(w_in[g % SLOTS], 16)
            sp.wait_ge(x_rdy, DC + 2 * DC * LAYERS)
            sp.dma_start(out, hT[:]).then_inc(stored, 16)
            sp.wait_ge(stored, 16)

        @block.gpsimd
        def _(pool):
            pool.memset(xr[:, :, 0:CONV_W - 1], 0.0).then_inc(pad_rdy, 1)
            pool.memset(zeros[:], 0).then_inc(pool_step, 1)
            pool.wait_ge(pool_step, 1)
            pool.dma_start(table.rearrange("(p b) o -> p (b o)", p=P), zeros[:]).then_inc(table_clear, 16)
            pool.dma_start(browS, brow).then_inc(brow_in, 16)
            pool.wait_ge(tix_rdy, 1)
            pool.wait_ge(table_clear, 16)
            for k in range(2):
                for r in range(NQB):
                    c = k * NQB + r
                    pool.indirect_dma_start(table, bass.IndirectOffsetOnAxis(ap=tixI[:, c:c + 1], axis=0),
                                            tokI[:, r:r + 1], None).then_inc(table_set, 16)
            pool.wait_ge(table_set, 16 * 2 * NQB)
            pool.dma_start(ids[:], table.rearrange("(p b) o -> p (b o)", p=P)).then_inc(ids_in, 16)
            pool.wait_ge(ids_in, 16)
            pool.wait_ge(u_stored, 16 * NQB)
            for b in range(MOE_BLOCKS + 1):
                if b >= 2:
                    pool.wait_ge(xt_full, b - 1)
                pool.indirect_dma_start(xs[:, b % 2, :], None, u_rows, bass.IndirectOffsetOnAxis(ap=ids[:, b:b + 1], axis=0)
                                        ).then_inc(xs_in[b % 2], 16)
            for j in range(2):
                pool.wait_ge(y_stored[j], 16 * (MOE_BLOCKS // 2))
            for k in range(2):
                for r in range(NQB):
                    c = k * NQB + r
                    pool.indirect_dma_start(y_tok[:, k, r, :], None, y_rows, bass.IndirectOffsetOnAxis(ap=destI[:, c:c + 1], axis=0)
                                            ).then_inc(rows_back, 16)
            pool.wait_ge(h2_rdy, DC)
            pool.dma_start(lamS[:], lamv.partition_broadcast(P)).then_inc(lam_in, 16)
            for l in range(LAYERS):
                pool.wait_ge(x_rdy, DC + 2 * DC * l)

                def table_in(h):
                    k = l * HEADS + h
                    if h >= 2:
                        pool.wait_ge(near_rdy, k - 1)
                    pool.dma_start(rp[:, h % 2, :], rpb[l, h]).then_inc(rp_in, 16)
                table_in(0)
                for h in range(HEADS):
                    k = l * HEADS + h
                    pool.wait_ge(rp_in, 16 * (k + 1))
                    if h + 1 < HEADS:
                        table_in(h + 1)
                    if h >= 2:
                        pool.wait_ge(mx_rdy, U_DSA + l * U_LAYER + 4 * (h - 1))
                    m = K("na_mask").rearrange("p (t c) -> p t c", c=16)
                    i0 = 0
                    for n, (lo, hi) in enumerate(NA_KEYS):
                        w = hi - lo
                        ins = pool.tensor_tensor(
                            near[:, h % 2, i0 * P:(i0 + w) * P].rearrange("p (t r c) -> p t r c", r=GRID_ROWS, c=16),
                            rp[:, h % 2, (lo - n + 1) * P:(hi - n + 1) * P].rearrange("p (t r c) -> p t r c", r=GRID_ROWS, c=16),
                            m[:, i0:i0 + w, :].unsqueeze(2).broadcast_to((P, w, GRID_ROWS, 16)), ALU.add)
                        i0 += w
                    ins.then_inc(near_rdy, 1)
                pool.wait_ge(kr_rdy, l + 1)
                pool.tensor_copy(k96[64:MLA_QK, :, :], krT[64:MLA_QK, :].unsqueeze(1).broadcast_to((32, HEADS, SEQ))).then_inc(keys_rdy, 1)

        @block.scalar
        def _(act):
            act.wait_ge(vec_in, 16)
            act.activation(csil, V("c"), ACT.Silu).then_inc(c_silu, 1)
            act.activation(s_abs, V("lam"), ACT.Abs).then_inc(sp_rdy, 1)
            act.wait_ge(x_in, 16)
            squares(act, hT, DC)
            root(act)
            for n in range(RC):
                act.activation(xr[:, n, CONV_W - 1:CONV_W - 1 + SEQ], A.take(act), ACT.Copy).then_inc(A.free, 1)
            def decay(n):
                act.wait_ge(gate_s, n + 1)
                act.activation(lru_t[:, n % 2, 2, :], lru_t[:, n % 2, 0, :], ACT.Tanh, scale=0.5).then_inc(gate_a, 1)
            for n in range(RC):
                if n >= 2:
                    act.wait_ge(lru_q, n - 1)
                act.activation(lru_t[:, n % 2, 0, :], A.take(act), ACT.Sigmoid, bias=V("b_rg_a")[:, n:n + 1]).then_inc(A.free, 1)
                act.activation(lru_t[:, n % 2, 1, :], A.take(act), ACT.Tanh, scale=0.5, bias=hbx[:, n:n + 1]).then_inc(A.free, 1)
                if n >= 1:
                    decay(n - 1)
            decay(RC - 1)
            for c in range(KVC):
                act.activation(ckv[:, c, :], A.take(act), ACT.Copy).then_inc(A.free, 1)
            for m in range(4):
                act.activation(qi[:, m, :], A.take(act), ACT.Copy).then_inc(A.free, 1)
            act.activation(ki[:], A.take(act), ACT.Copy).then_inc(A.free, 1)
            act.activation(wi_s, A.take(act)[:, 0:NQB * IDX_HEADS], ACT.Copy, scale=IDX_SCALE).then_inc(A.free, 1)
            act.wait_ge(A.free, A.took)
            for n in range(RC):
                if n < 2:
                    act.wait_ge(lru_q, RC)
                else:
                    act.wait_ge(h_rdy, n - 1)
                act.activation(lru_t[:, n % 2, 0, :], xr[:, n, 0:SEQ], ACT.Sqrt).then_inc(lru_sqrt, 1)
            squares(act, ckv, KVC)
            root(act)
            for n in range(RC):
                if n >= 2:
                    act.wait_ge(gh_rdy, n - 1)
                act.activation(lru_t[:, n % 2, 0, :], A.take(act), ACT.Gelu_apprx_tanh).then_inc(A.free, 1)
            act.wait_ge(gh_rdy, RC)
            for m in range(DC):
                act.activation(mixT[:, m, :], A.take(act), ACT.Sigmoid).then_inc(A.free, 1)
            for m in range(DC):
                act.activation(gb[:, m, :], A.take(act), ACT.Sigmoid).then_inc(A.free, 1)
            k = 0
            for qb in range(NQB):
                for h in range(IDX_HEADS):
                    act.wait_ge(ix_score, k + 1)
                    if k >= 2:
                        act.wait_ge(ix_acc, k - 1)
                    n = (qb + 1) * P
                    act.activation(rel[:, k % 2, 0:n], ps[:, 4 + k % 2, 0:n], ACT.Relu).then_inc(ix_rel, 1)
                    k += 1
            for h in range(HEADS):
                act.activation(qT[:, h, :], A.take(act), ACT.Copy).then_inc(A.free, 1)
            for h in range(HEADS):
                act.activation(kT[:, h, :], A.take(act), ACT.Copy).then_inc(A.free, 1)
            for s in range(NQB):
                for n in range(2):
                    act.activation(vS[:, s, n * SEQ:(n + 1) * SEQ], A.take(act), ACT.Copy).then_inc(A.free, 1)

            def att_out(u):
                act.activation(qT[:, u["h"], :], A.take(act), ACT.Copy).then_inc(A.free, 1)
            units_act(act, dsa, att_out)
            squares(act, hT, DC, lambda c: act.wait_ge(h1_rdy, c + 1))
            root(act)
            for r in range(NQB):
                for n in range(2):
                    act.activation(u_tok[:, r, n * SEQ:(n + 1) * SEQ], A.take(act), ACT.Copy).then_inc(A.free, 1)
            act.wait_ge(gl_diff, 1)
            act.activation(T("ge"), T("gd"), ACT.Exp).then_inc(gl_exp, 1)
            act.wait_ge(e_diff, 1)
            act.activation(T("ex"), T("d"), ACT.Exp).then_inc(e_exp, 1)

            def block_x(b, j):
                act.wait_ge(xt_full, b + 1)
                act.activation(xsT[:, j, 0:4, :], ps[:, 0, :].rearrange("p (c n) -> p c n", n=P), ACT.Copy)
                act.activation(xsT[:, j, 4:8, :], ps[:, 1, :].rearrange("p (c n) -> p c n", n=P), ACT.Copy).then_inc(xt_rdy, 1)

            def block_act(i, j):
                b = 2 * i + j
                act.wait_ge(gate_full, b + 1)
                act.wait_ge(hid_done, b)
                act.activation(sil[:], ps[:, 2, :], ACT.Silu).then_inc(sil_done, 1)
                block_x(b + 1, 1 - j)
                act.wait_ge(ht_full, b + 1)
                act.activation(hidT[:], ps[:, 4, :].rearrange("p (c n) -> p c n", n=P), ACT.Copy).then_inc(ht_rdy, 1)
                act.wait_ge(y1_full, b + 1)
                act.wait_ge(y_stored[j], 16 * i)
                act.activation(ysb[:, j, SEQ:], ps[:, 6, :], ACT.Copy).then_inc(y1_rdy, 1)
                act.wait_ge(y1_rdy, b + 1)
                act.wait_ge(y0_rdy, b + 1)
                act.dma_start(y_rows[bass.ds(b * P, P), :], ysb[:, j, :]).then_inc(y_stored[j], 16)

            block_x(0, 0)
            with act.Fori(0, MOE_BLOCKS // 2) as i:
                for j in range(2):
                    block_act(i, j)
            squares(act, hT, DC, lambda c: act.wait_ge(h2_rdy, c + 1))
            root(act)
            squares(act, uT, DC, lambda c: act.wait_ge(centered, c + 1))
            root(act)
            act.wait_ge(lam_sum, 1)
            act.activation(lam_two[:, 0:4], lam_prod[:, 0:4], ACT.Exp).then_inc(lam_exp, 1)
            act.wait_ge(x_rdy, DC)
            for l in range(LAYERS):
                layer_act(act, l)

        @block.vector
        def _(dve):
            dve.wait_ge(vec_in, 16)
            dve.tensor_scalar(hbx, V("b_rg_x"), 0.5, None, ALU.mult)
            after(dve, dve.tensor_scalar(hsp, V("lam"), -1.0, 0.0, ALU.mult, ALU.max), dve_step, "dstep")
            dve.wait_ge(sp_rdy, 1)
            step = lambda ins: after(dve, ins, dve_step, "dstep")
            step(dve.tensor_scalar(s_abs, s_abs, 87.0, None, ALU.min))
            step(dve.tensor_scalar(s_int, s_abs, 1.0 / math.log(2.0), None, ALU.mult))
            step(dve.tensor_copy(s_z, s_int))
            step(dve.scalar_tensor_tensor(out=s_abs, in0=s_z, scalar=-LN2_HI, in1=s_abs, op0=ALU.mult, op1=ALU.add))
            step(dve.scalar_tensor_tensor(out=s_abs, in0=s_z, scalar=LN2_HI - math.log(2.0), in1=s_abs, op0=ALU.mult, op1=ALU.add))
            step(dve.tensor_scalar(s_int, s_z, -float(2 ** 23), 127.0 * 2 ** 23, ALU.mult, ALU.add))
            step(dve.tensor_scalar(s_zz, s_abs, -1.0 / 10.0, 1.0, ALU.mult, ALU.add))
            for k in range(9, 0, -1):
                step(dve.scalar_tensor_tensor(out=s_zz, in0=s_abs, scalar=-1.0 / k, in1=s_zz, op0=ALU.mult, op1=ALU.mult))
                step(dve.tensor_scalar(s_zz, s_zz, 1.0, None, ALU.add))
            step(dve.tensor_tensor(s_abs, s_zz, s_int.bitcast(F32), ALU.mult))
            step(dve.tensor_scalar(s_z, s_abs, 2.0, None, ALU.add))
            step(dve.reciprocal(s_z, s_z))
            step(dve.tensor_tensor(s_z, s_z, s_abs, ALU.mult))
            step(dve.tensor_tensor(s_zz, s_z, s_z, ALU.mult))
            step(dve.tensor_scalar(s_abs, s_zz, 1.0 / 19.0, None, ALU.mult))
            for k in range(17, 1, -2):
                step(dve.scalar_tensor_tensor(out=s_abs, in0=s_abs, scalar=1.0 / k, in1=s_zz, op0=ALU.add, op1=ALU.mult))
            step(dve.scalar_tensor_tensor(out=s_abs, in0=s_abs, scalar=1.0, in1=s_z, op0=ALU.add, op1=ALU.mult))
            step(dve.scalar_tensor_tensor(out=hsp, in0=s_abs, scalar=2.0, in1=hsp, op0=ALU.mult, op1=ALU.add))
            after(dve, dve.tensor_scalar(hsp, hsp, LRU_C, None, ALU.mult), dve_step, "dstep")
            b = B.take(dve)
            dve.tensor_tensor(mod[:, 0:16], b[:, 0:16], V("b_mod")[:, 0:16], ALU.add).then_inc(B.free, 1)
            dve.wait_ge(B.free, B.took)
            dve.scalar_tensor_tensor(out=a1, in0=mod[:, 8:16], scalar=1.0, in1=V("norm1_g"), op0=ALU.add, op1=ALU.mult).then_inc(a_coef, 1)
            dve.wait_ge(a_coef, 1)
            sum_squares(dve, DC)
            inverse_var(dve, D, EPS)
            for c in range(DC):
                after(dve, dve.scalar_tensor_tensor(out=uT[:, c, :], in0=hT[:, c, :], scalar=a1[:, c:c + 1], in1=rstd,
                                                    op0=ALU.mult, op1=ALU.mult), dve_step, "dstep")
                dve.tensor_scalar(uT[:, c, :], uT[:, c, :], mod[:, c:c + 1], None, ALU.add).then_inc(u_rdy, 1)
            cw, cb = V("conv_w"), V("conv_b")
            dve.wait_ge(pad_rdy, 1)
            for n in range(RC):
                dve.wait_ge(A.free, n + 1)
                after(dve, dve.tensor_scalar(rnn[:, n, :], xr[:, n, 0:SEQ], cw[:, n:n + 1], cb[:, n:n + 1], ALU.mult, ALU.add), dve_step, "dstep")
                for w in range(1, CONV_W):
                    ins = dve.scalar_tensor_tensor(out=rnn[:, n, :], in0=xr[:, n, w:w + SEQ], scalar=cw[:, w * RC + n:w * RC + n + 1],
                                                   in1=rnn[:, n, :], op0=ALU.mult, op1=ALU.add)
                    if w < CONV_W - 1:
                        after(dve, ins, dve_step, "dstep")
                ins.then_inc(conv_rdy, 1)
            def input_scale(n):
                t = lru_t[:, n % 2]
                dve.wait_ge(gate_a, n + 1)
                after(dve, dve.tensor_scalar(t[:, 0, :], t[:, 2, :], 1.0, None, ALU.add), dve_step, "dstep")
                after(dve, dve.reciprocal(t[:, 0, :], t[:, 0, :]), dve_step, "dstep")
                dve.tensor_tensor(rnn[:, n, :], rnn[:, n, :], t[:, 0, :], ALU.mult)
                dve.tensor_scalar(xr[:, n, 0:SEQ], t[:, 2, :], 1e-30, None, ALU.max)
                after(dve, dve.tensor_scalar(t[:, 2, :], t[:, 2, :], -1.0, 1.0, ALU.mult, ALU.add), dve_step, "dstep")
                dve.tensor_tensor(lru_a[:, n, :], t[:, 2, :], t[:, 0, :], ALU.mult).then_inc(lru_q, 1)
            for n in range(RC):
                t = lru_t[:, n % 2]
                dve.wait_ge(A.free, RC + 2 * n + 2)
                dve.tensor_scalar(t[:, 0, :], t[:, 0, :], hsp[:, n:n + 1], None, ALU.mult).then_inc(gate_s, 1)
                after(dve, dve.tensor_scalar(t[:, 1, :], t[:, 1, :], 0.5, 0.5, ALU.mult, ALU.add), dve_step, "dstep")
                dve.tensor_tensor(rnn[:, n, :], rnn[:, n, :], t[:, 1, :], ALU.mult)
                if n >= 1:
                    input_scale(n - 1)
            input_scale(RC - 1)
            dve.wait_ge(lru_q, RC)
            for n in range(RC):
                dve.wait_ge(lru_sqrt, n + 1)
                r, q = lru_t[:, n % 2, 0, :], lru_t[:, n % 2, 1, :]
                after(dve, dve.reciprocal(q, r), dve_step, "dstep")
                after(dve, dve.tensor_tensor(q, q, xr[:, n, 0:SEQ], ALU.mult), dve_step, "dstep")
                after(dve, dve.tensor_tensor(q, q, r, ALU.add), dve_step, "dstep")
                after(dve, dve.tensor_tensor(xr[:, n, 0:SEQ], q, rnn[:, n, :], ALU.mult), dve_step, "dstep")
                dve.tensor_tensor_scan(rnn[:, n, :], lru_a[:, n, :], xr[:, n, 0:SEQ], 0.0, ALU.mult, ALU.add).then_inc(h_rdy, 1)
            sum_squares(dve, KVC)
            inverse_var(dve, KV_RANK, EPS)
            for c in range(KVC):
                dve.scalar_tensor_tensor(out=ckv[:, c, :], in0=ckv[:, c, :], scalar=V("kv_g")[:, c:c + 1], in1=rstd,
                                         op0=ALU.mult, op1=ALU.mult).then_inc(ckv_rdy, 1)
            a_free_gr = RC + 2 * RC + KVC + 4 + 1 + 1
            dve.wait_ge(h_rdy, RC)
            for n in range(RC):
                dve.wait_ge(A.free, a_free_gr + n + 1)
                dve.tensor_tensor(rnn[:, n, :], rnn[:, n, :], lru_t[:, n % 2, 0, :], ALU.mult).then_inc(gh_rdy, 1)
            b = B.take(dve)
            dve.tensor_tensor(mod[:, 16:48], b[:, 0:32], V("b_mod")[:, 16:48], ALU.add).then_inc(B.free, 1)
            dve.wait_ge(B.free, B.took)
            dve.scalar_tensor_tensor(out=a2, in0=mod[:, 32:40], scalar=1.0, in1=V("norm2_g"), op0=ALU.add, op1=ALU.mult).then_inc(a_coef, 1)
            dve.wait_ge(table_clear, 16)
            k = 0
            for qb in range(NQB):
                o, n = qb * (qb + 1) // 2, (qb + 1) * P
                w = sel[:, o:o + qb + 1, :].rearrange("p j q -> p (j q)")
                for h in range(IDX_HEADS):
                    wt = wi_s[:, qb * IDX_HEADS + h:qb * IDX_HEADS + h + 1]
                    dve.wait_ge(ix_rel, k + 1)
                    if h == 0:
                        ins = dve.tensor_scalar(w, rel[:, k % 2, 0:n], wt, None, ALU.mult)
                    else:
                        ins = dve.scalar_tensor_tensor(out=w, in0=rel[:, k % 2, 0:n], scalar=wt, in1=w, op0=ALU.mult, op1=ALU.add)
                    ins.then_inc(ix_acc, 1)
                    k += 1
                    dve.wait_ge(ix_acc, k)
            c0 = K("causal")
            after(dve, dve.tensor_scalar(sel[:, 0, :], c0, MASKED / OUT_OF_SIGHT, None, ALU.mult), dve_step, "dstep")
            for qb in range(1, NQB):
                o = qb * (qb + 1) // 2
                ins = dve.tensor_tensor(sel[:, o + qb, :], sel[:, o + qb, :], c0, ALU.add)
            after(dve, ins, dve_step, "dstep")
            works = [sel[:, qb * (qb + 1) // 2:qb * (qb + 1) // 2 + qb + 1, :].rearrange("p j q -> p (j q)") for qb in range(NQB)]
            for r in range(TOPK // 8):
                for qb in range(1, NQB):
                    ins = dve.max(max8[:, 8 * (qb - 1):8 * qb], works[qb])
                after(dve, ins, dve_step, "dstep")
                for qb in range(1, NQB):
                    ins = dve.match_replace(works[qb], max8[:, 8 * (qb - 1):8 * qb], works[qb], TAKEN)
                after(dve, ins, dve_step, "dstep")
            for qb in range(1, NQB):
                ins = dve.tensor_scalar(works[qb], works[qb], TAKEN, -1.0, ALU.is_equal, ALU.add)
            after(dve, ins, dve_step, "dstep")
            for qb in range(1, NQB):
                ins = dve.tensor_scalar(works[qb], works[qb], -MASKED, None, ALU.mult)
            after(dve, ins, dve_step, "dstep")
            for m in range(DC):
                dve.wait_ge(A.free, a_free_gr + RC + m + 1)
                dve.tensor_tensor(mixT[:, m, :], B.take(dve), mixT[:, m, :], ALU.mult).then_inc(B.free, 1)
            units_dve(dve, dsa)
            for m in range(DC):
                dve.tensor_tensor(gb[:, m, :], B.take(dve), gb[:, m, :], ALU.mult).then_inc(B.free, 1)
                dve.wait_ge(B.free, B.took)
                dve.tensor_tensor(mixT[:, m, :], mixT[:, m, :], gb[:, m, :], ALU.add).then_inc(mix2_rdy, 1)
            for m in range(DC):
                dve.scalar_tensor_tensor(out=hT[:, m, :], in0=B.take(dve), scalar=mod[:, 16 + m:17 + m], in1=hT[:, m, :],
                                         op0=ALU.mult, op1=ALU.add).then_inc(h1_rdy, 1)
                B_also_free(dve)
            sum_squares(dve, DC)
            inverse_var(dve, D, EPS)
            for c in range(DC):
                after(dve, dve.scalar_tensor_tensor(out=uT[:, c, :], in0=hT[:, c, :], scalar=a2[:, c:c + 1], in1=rstd,
                                                    op0=ALU.mult, op1=ALU.mult), dve_step, "dstep")
                dve.tensor_scalar(uT[:, c, :], uT[:, c, :], mod[:, 24 + c:25 + c], None, ALU.add).then_inc(u_rdy, 1)
            step = lambda ins: after(dve, ins, dve_step, "dstep")
            TT, TS, STT = dve.tensor_tensor, dve.tensor_scalar, dve.scalar_tensor_tensor
            lg = T("lg").rearrange("p (s n) -> p s n", n=GROUPS + EXPERTS)
            dve.tensor_copy(T("lg"), B.take(dve)[:, 0:NQB * (GROUPS + EXPERTS)]).then_inc(B.free, 1)
            dve.wait_ge(B.free, B.took)
            gl, el = lg[:, :, 0:GROUPS], lg[:, :, GROUPS:]

            def four(t, n):
                return T(t)[:, 0:NQB * n].rearrange("p (s n) -> p s n", n=n)

            def best(values, n, m, pick):
                step(dve.reduce_max(T(m), values, AX_X))
                w = four("w", n)
                step(TT(w, values, T(m).unsqueeze(2).broadcast_to((P, NQB, n)), ALU.is_equal))
                step(TT(w, w, K("first")[:, 0:n].unsqueeze(1).broadcast_to((P, NQB, n)), ALU.mult))
                step(dve.reduce_max(T("wm"), w, AX_X))
                step(TT(four(pick, n), w, T("wm").unsqueeze(2).broadcast_to((P, NQB, n)), ALU.is_equal))

            best(gl, GROUPS, "gmax", "goh")
            TT(four("gd", GROUPS), gl, T("gmax").unsqueeze(2).broadcast_to((P, NQB, GROUPS)), ALU.subtract).then_inc(gl_diff, 1)
            prod = big[:, 0:NQB * EXPERTS].rearrange("p (s e g) -> p s e g", s=NQB, g=GROUPS)
            goh = four("goh", GROUPS)
            step(TT(prod, el.rearrange("p s (g e) -> p s e g", g=GROUPS), goh.unsqueeze(2).broadcast_to((P, NQB, PER_GROUP, GROUPS)), ALU.mult))
            es = four("es", PER_GROUP)
            step(dve.reduce_sum(es, prod, AX_X))
            best(es, PER_GROUP, "m1", "oh1")
            step(STT(out=es, in0=four("oh1", PER_GROUP), scalar=TAKEN, in1=es, op0=ALU.mult, op1=ALU.add))
            best(es, PER_GROUP, "m2", "oh2")
            TT(T("d"), T("m2"), T("m1"), ALU.subtract).then_inc(e_diff, 1)
            dve.wait_ge(gl_exp, 1)
            step(dve.reduce_sum(T("gw"), four("ge", GROUPS), AX_X))
            dve.wait_ge(e_exp, 1)
            step(TS(T("p1"), T("ex"), 1.0, None, ALU.add))
            step(TT(T("p1"), T("p1"), T("gw"), ALU.mult))
            step(dve.reciprocal(gate12[:, 0:NQB], T("p1")))
            TT(gate12[:, NQB:], gate12[:, 0:NQB], T("ex"), ALU.mult)
            for name, oh in (("M1", "oh1"), ("M2", "oh2")):
                ins = TT(T(name).rearrange("p (s g e) -> p s g e", s=NQB, e=PER_GROUP),
                         goh.unsqueeze(3).broadcast_to((P, NQB, GROUPS, PER_GROUP)),
                         four(oh, PER_GROUP).unsqueeze(2).broadcast_to((P, NQB, GROUPS, PER_GROUP)), ALU.mult)
            step(ins)
            TT(T("M"), T("M1"), T("M2"), ALU.add).then_inc(ohot, 1)
            b = B.take(dve)
            pos, cts = T("pos"), T("cts")
            dve.tensor_copy(pos, b[:, 0:NQB * EXPERTS])
            dve.tensor_copy(cts, b[:, NQB * EXPERTS:(NQB + 1) * EXPERTS]).then_inc(B.free, 1)
            dve.wait_ge(B.free, B.took)
            step(TS(T("nb"), cts, 0.0, None, ALU.is_gt))
            for lim in (P, 2 * P, 3 * P):
                step(STT(out=T("nb"), in0=cts, scalar=float(lim), in1=T("nb"), op0=ALU.is_gt, op1=ALU.add))
            step(dve.tensor_tensor_scan(T("cum"), ones[:, 0:EXPERTS], T("nb"), 0.0, ALU.mult, ALU.add))
            dve.tensor_tensor(T("st"), T("cum"), T("nb"), ALU.subtract)
            step(TS(T("bq"), pos, float(P), None, ALU.is_ge))
            for lim in (2 * P, 3 * P):
                step(STT(out=T("bq"), in0=pos, scalar=float(lim), in1=T("bq"), op0=ALU.is_ge, op1=ALU.add))
            step(STT(out=pos, in0=T("bq"), scalar=float(-P), in1=pos, op0=ALU.mult, op1=ALU.add))
            v3 = lambda t: T(t).rearrange("p (s e) -> p s e", e=EXPERTS)
            step(TT(v3("bq"), v3("bq"), T("st").unsqueeze(1).broadcast_to((P, NQB, EXPERTS)), ALU.add))
            TS(T("tix"), pos, float(MOE_BLOCKS + 1), None, ALU.mult)
            step(STT(out=pos, in0=T("bq"), scalar=float(P), in1=pos, op0=ALU.mult, op1=ALU.add))
            step(TT(T("tix"), T("tix"), T("bq"), ALU.add))
            for k, M in enumerate(("M1", "M2")):
                for t, to in (("tix", tixI), ("pos", destI)):
                    step(TT(T("bq"), T(M), T(t), ALU.mult))
                    step(dve.reduce_sum(T("ix"), v3("bq"), AX_X))
                    step(dve.tensor_copy(to[:, k * NQB:(k + 1) * NQB], T("ix")))
            dve.tensor_copy(tokI[:], K("token")).then_inc(tix_rdy, 1)
            bb = big[:].rearrange("p (b e) -> p b e", e=EXPERTS)
            step(TT(bb, T("cum").unsqueeze(1).broadcast_to((P, MOE_BLOCKS, EXPERTS)),
                    K("block").unsqueeze(2).broadcast_to((P, MOE_BLOCKS, EXPERTS)), ALU.is_le))
            step(dve.reduce_sum(T("be"), bb, AX_X))
            step(TS(T("be"), T("be"), float(EXPERTS - 1), None, ALU.min))
            dve.tensor_copy(bexpI[:], T("be")).then_inc(route_rdy, 1)

            def block_dve(i, j):
                b = 2 * i + j
                dve.wait_ge(up_full, b + 1)
                dve.wait_ge(sil_done, b + 1)
                dve.tensor_tensor(hid[:], ps[:, 3, :], sil[:], ALU.mult).then_inc(hid_done, 1)
                dve.wait_ge(y0_full, b + 1)
                dve.wait_ge(y_stored[j], 16 * i)
                dve.tensor_copy(ysb[:, j, 0:SEQ], ps[:, 5, :]).then_inc(y0_rdy, 1)

            with dve.Fori(0, MOE_BLOCKS // 2) as i:
                for j in range(2):
                    block_dve(i, j)
            for r in range(NQB):
                dve.wait_ge(rows_back, 16 * 2 * NQB)
                step(TS(y_tok[:, 0, r, :], y_tok[:, 0, r, :], gate12[:, r:r + 1], None, ALU.mult))
                STT(out=y_tok[:, 0, r, :], in0=y_tok[:, 1, r, :], scalar=gate12[:, NQB + r:NQB + r + 1], in1=y_tok[:, 0, r, :],
                    op0=ALU.mult, op1=ALU.add).then_inc(mixed_rows, 1)
            for c in range(DC):
                STT(out=hT[:, c, :], in0=B.take(dve), scalar=mod[:, 40 + c:41 + c], in1=hT[:, c, :],
                    op0=ALU.mult, op1=ALU.add).then_inc(h2_rdy, 1)
                B_also_free(dve)
            sum_squares(dve, DC)
            inverse_var(dve, D, EPS)
            for c in range(DC):
                STT(out=uT[:, c, :], in0=hT[:, c, :], scalar=V("final_g")[:, c:c + 1], in1=rstd, op0=ALU.mult, op1=ALU.mult).then_inc(b1_rdy, 1)
            dve.wait_ge(b1_rdy, DC)
            center(dve, uT)
            normed(dve, uT, hT, V("ln_in_g"), V("ln_in_b"), turn=True)
            dve.wait_ge(lam_in, 16)
            lv = lamS[:].rearrange("p (l a d) -> p l a d", l=LAYERS, a=4)
            step(TT(lv[:, :, 0:4:2, :], lv[:, :, 0:4:2, :], lv[:, :, 1:4:2, :], ALU.mult))
            dve.reduce_sum(lam_prod[:, 0:4].rearrange("p (l a) -> p l a", a=2), lv[:, :, 0:4:2, :], AX_X).then_inc(lam_sum, 1)
            dve.wait_ge(lam_exp, 1)
            for l in range(LAYERS):
                init = 0.8 - 0.6 * math.exp(-0.3 * l)
                step(TT(lam_neg[:, l:l + 1], lam_two[:, 2 * l + 1:2 * l + 2], lam_two[:, 2 * l:2 * l + 1], ALU.subtract))
                step(TS(lam_neg[:, l:l + 1], lam_neg[:, l:l + 1], -init, None, ALU.add))
                step(TS(subg[:, l:l + 1], V(f"subln{l}"), 1.0 - init, None, ALU.mult))
            for l in range(LAYERS):
                layer_dve(dve, l)

        @block.tensor
        def _(pe):
            def columns(c0, n):
                b = B.claim(pe)
                for m in range(n):
                    for k in range(DC):
                        ins = pe.matmul(b[:, m:m + 1], chunk(pe, c0 + m * DC + k), csil[:, k:k + 1], start=(k == 0), stop=(k == DC - 1))
                        if not (m == n - 1 and k == DC - 1):
                            said(ins)
                ins.then_inc(B.full, 1)
            pe.wait_ge(c_silu, 1)
            columns(one["mod_a"], 16)
            pe.wait_ge(const_in, 16)
            norm_pe(pe, DC)
            for n in range(RC):
                tile(pe, A.claim(pe), one["xr"] + n * DC, uT, DC, wait=(lambda k: pe.wait_ge(u_rdy, k + 1)) if n == 0 else None).then_inc(A.full, 1)
            for n in range(RC):
                pe.wait_ge(conv_rdy, n + 1)
                for g in range(2):
                    b = A.claim(pe)
                    pe.matmul(b, chunk(pe, one["rg"] + 2 * n + g), rnn[:, n, :], start=True, stop=True).then_inc(A.full, 1)
            for m in range(KVC):
                tile(pe, A.claim(pe), one["ckv"] + m * DC, uT, DC).then_inc(A.full, 1)
            for m in range(4):
                tile(pe, A.claim(pe), one["qi"] + m * DC, uT, DC).then_inc(A.full, 1)
            tile(pe, A.claim(pe), one["ki"], uT, DC).then_inc(A.full, 1)
            b = A.claim(pe)
            w = chunk(pe, one["wi"])
            for s in range(NQB):
                for k in range(DC):
                    ins = pe.matmul(b[:, s * IDX_HEADS:(s + 1) * IDX_HEADS], uT[:, k, s * P:(s + 1) * P],
                                    w[:, k * IDX_HEADS:(k + 1) * IDX_HEADS], start=(k == 0), stop=(k == DC - 1))
                    if s < NQB - 1:
                        said(ins)
            ins.then_inc(A.full, 1)
            norm_pe(pe, KVC)
            for m in range(RC):
                tile(pe, A.claim(pe), one["gr"] + m * DC, uT, DC).then_inc(A.full, 1)
            columns(one["mod_b"], 32)
            for m in range(2 * DC):
                tile(pe, A.claim(pe), one["mg"] + m * DC, uT, DC).then_inc(A.full, 1)
            k = 0
            for qb in range(NQB):
                for h in range(IDX_HEADS):
                    r = 64 * (h % 2)
                    if k >= 2:
                        pe.wait_ge(ix_rel, k - 1)
                    pe.matmul(ps[:, 4 + k % 2, 0:(qb + 1) * P], qi[r:r + 64, h // 2, qb * P:(qb + 1) * P],
                              ki[r:r + 64, 0:(qb + 1) * P], start=True, stop=True).then_inc(ix_score, 1)
                    k += 1
            for m in range(HEADS):
                tile(pe, A.claim(pe), one["q"] + m * DC, uT, DC).then_inc(A.full, 1)
            pe.wait_ge(gh_rdy, RC)
            for m in range(DC):
                tile(pe, B.claim(pe), one["rnn_out"] + m * RC, rnn, RC).then_inc(B.full, 1)
            pe.wait_ge(ckv_rdy, KVC)
            for m in range(HEADS):
                tile(pe, A.claim(pe), one["uk"] + m * KVC, ckv, KVC).then_inc(A.full, 1)
            for s in range(NQB):
                for n in range(2):
                    b = A.claim(pe)
                    for k in range(KVC):
                        w = chunk(pe, one["uv"] + (2 * k + n) * 4, 4)
                        ins = pe.matmul(b, ckv[:, k, s * P:(s + 1) * P], w, start=(k == 0), stop=(k == KVC - 1))
                    ins.then_inc(A.full, 1)
            units_pe(pe, dsa, lambda i: (pe.wait_ge(ix_rel, NQB * IDX_HEADS), pe.wait_ge(A.free, A.made)) if i == 0 else None)
            pe.wait_ge(A.free, A.made)
            for m in range(DC):
                tile(pe, B.claim(pe), one["att_out"] + m * DC, qT, DC).then_inc(B.full, 1)
            pe.wait_ge(mix2_rdy, DC)
            for m in range(DC):
                tile(pe, B.claim(pe), one["out"] + m * DC, mixT, DC).then_inc(B.full, 1)
            norm_pe(pe, DC)
            pe.wait_ge(u_rdy, 2 * DC)
            assert A.made == A_ROWS
            for r in range(NQB):
                for n in range(2):
                    b = A.claim(pe)
                    for c in range(4):
                        ins = pe.transpose(b[:, c * P:(c + 1) * P], uT[:, 4 * n + c, r * P:(r + 1) * P], ident)
                    ins.then_inc(A.full, 1)
            b = B.claim(pe)
            w = chunk(pe, one["router"], 3)
            N = GROUPS + EXPERTS
            pe.wait_ge(brow_in, 16)
            for r in range(NQB):
                for k in range(DC):
                    said(pe.matmul(b[:, r * N:(r + 1) * N], uT[:, k, r * P:(r + 1) * P], w[:, k * N:(k + 1) * N], start=(k == 0), stop=False))
                ins = pe.matmul(b[:, r * N:(r + 1) * N], ones[0:1, :], browS, start=False, stop=True)
            ins.then_inc(B.full, 1)
            pe.wait_ge(ohot, 1)
            b = B.claim(pe)
            M = T("M").rearrange("p (s e) -> p s e", e=EXPERTS)
            for r in range(NQB):
                pe.matmul(b[:, r * EXPERTS:(r + 1) * EXPERTS], K("tri"), M[:, r, :], start=True, stop=(r == 0))
                for q in range(r):
                    pe.matmul(b[:, r * EXPERTS:(r + 1) * EXPERTS], ones, M[:, q, :], start=False, stop=(q == r - 1))
            for q in range(NQB):
                ins = pe.matmul(b[:, NQB * EXPERTS:(NQB + 1) * EXPERTS], ones, M[:, q, :], start=(q == 0), stop=(q == NQB - 1))
            ins.then_inc(B.full, 1)
            pe.wait_ge(A.free, A.made)
            pe.wait_ge(B.free, B.made)
            pe.transpose(ps[:, 7, 0:P], ident, ident).then_inc(moe_go, 1)

            def block_x(i, b, j):
                pe.wait_ge(xs_in[j], 16 * i + 16)
                pe.wait_ge(xt_rdy, b)
                for c in range(DC):
                    ins = pe.transpose(ps[:, c // 4, (c % 4) * P:(c % 4 + 1) * P], xs[:, j, c * P:(c + 1) * P], ident)
                ins.then_inc(xt_full, 1)

            def block_pe(i, j):
                b = 2 * i + j
                pe.wait_ge(xt_rdy, b + 1)
                pe.wait_ge(up_in[j][0], 16 * i + 16)
                for k in range(DC):
                    ins = pe.matmul(ps[:, 2, :], xsT[:, j, k, :], mring[:, j, 0, k * SEQ:(k + 1) * SEQ], start=(k == 0), stop=(k == DC - 1))
                ins.then_inc(gate_full, 1)
                pe.wait_ge(up_in[j][1], 16 * i + 16)
                for k in range(DC):
                    ins = pe.matmul(ps[:, 3, :], xsT[:, j, k, :], mring[:, j, 1, k * SEQ:(k + 1) * SEQ], start=(k == 0), stop=(k == DC - 1))
                ins.then_inc(up_full, 1)
                block_x(i + j, b + 1, 1 - j)
                pe.wait_ge(hid_done, b + 1)
                for c in range(4):
                    ins = pe.transpose(ps[:, 4, c * P:(c + 1) * P], hid[:, c * P:(c + 1) * P], ident)
                ins.then_inc(ht_full, 1)
                pe.wait_ge(ht_rdy, b + 1)
                pe.wait_ge(down_in[j], 16 * i + 16)
                for n, full in enumerate((y0_full, y1_full)):
                    pe.wait_ge((y0_rdy, y1_rdy)[n], b)
                    for k in range(4):
                        ins = pe.matmul(ps[:, 5 + n, :], hidT[:, k, :], mring[:, j, 2, k * D + n * SEQ:k * D + (n + 1) * SEQ],
                                        start=(k == 0), stop=(k == 3))
                    ins.then_inc(full, 1)

            block_x(0, 0, 0)
            with pe.Fori(0, MOE_BLOCKS // 2) as i:
                for j in range(2):
                    block_pe(i, j)
            pe.wait_ge(mixed_rows, NQB)
            for c in range(DC):
                b = B.claim(pe)
                for r in range(NQB):
                    ins = pe.transpose(b[:, r * P:(r + 1) * P], y_tok[:, 0, r, c * P:(c + 1) * P], ident)
                ins.then_inc(B.full, 1)
            norm_pe(pe, DC)
            mean_pe(pe)
            norm_pe(pe, DC)
            for l in range(LAYERS):
                layer_pe(pe, l)


def _columns(v):
    return v.reshape(-1, P).T


def _chunks(w, nk=None):
    k, m = w.shape
    return w.reshape(k // P, P, m // P, P).transpose(2, 0, 1, 3).reshape(-1, P, P)


def _blocks(w):
    k, m = w.shape
    return w.reshape(k // P, P, m // 512, 4, P).transpose(0, 2, 3, 1, 4).reshape(-1, P, P)


def _wide(w, width=P):
    out = np.zeros((w.shape[0], width), w.dtype)
    out[:, :w.shape[1]] = w
    return out


def _pack(w, n):
    k, m = w.shape
    a = _wide(w.reshape(k // P, P, m).transpose(1, 0, 2).reshape(P, -1), n * P)
    return a.reshape(P, n, P).transpose(1, 0, 2)


def _stream(found, size, parts):
    s = np.zeros((size, P, P), np.float32)
    for name, chunks in parts.items():
        s[found[name]:found[name] + len(chunks)] = chunks
    return np.ascontiguousarray(s.reshape(-1, CHUNKS, P, P).transpose(0, 2, 1, 3)).reshape(-1, P, CHUNKS * P)


def _constants():
    cst, n = const_plan()
    t = np.zeros((P, n), np.float32)

    def put(name, v):
        a, b = cst[name]
        t[:v.shape[0], a:b] = v.reshape(v.shape[0], -1)

    p = np.arange(P)
    put("ident", np.eye(P))
    put("ones", np.ones((P, P)))
    put("tri", p[:, None] < p[None, :])
    pos = np.arange(SEQ).reshape(GRID_ROWS, NA_TILES, 16).transpose(1, 0, 2).reshape(-1).astype(np.float32)

    def rotary(base, half, group, rows):
        cos, sin, perm = np.ones((rows, SEQ)), np.zeros((rows, SEQ)), np.zeros((rows, P))
        inv = np.exp(np.float32(-math.log(ROPE_THETA)) * np.arange(half, dtype=np.float32) / np.float32(half)).astype(np.float32)
        ang = (pos[:, None] * inv[None, :]).astype(np.float32)
        for g in range(base, rows, group):
            for j in range(half):
                cos[g + j] = cos[g + half + j] = np.cos(ang[:, j])
                sin[g + j] = sin[g + half + j] = np.sin(ang[:, j])
                perm[g + half + j, g + j] = -1.0
                perm[g + j, g + half + j] = 1.0
        return cos, sin, perm

    c, s, m = rotary(0, 8, 64, P)
    put("cos_d", c), put("sin_d", s), put("perm_d", m)
    c, s, m = rotary(64, 16, 64, MLA_QK)
    put("cos_m", c), put("sin_m", s), put("perm_m", m)
    put("dist", p[:, None] - np.arange(7 * P)[None, :] + 3 * P)
    put("causal", np.where(p[None, :] <= p[:, None], 0.0, OUT_OF_SIGHT))
    mask = np.zeros((P, 10, 16))
    i = 0
    for n_, (lo, hi) in enumerate(NA_KEYS):
        for j in range(lo, hi):
            qc = n_ * 16 + p % 16
            kc = j * 16 + np.arange(16)
            w = np.clip(qc - 8, 0, GRID_W - 16)
            mask[:, i] = np.where((kc[None] >= w[:, None]) & (kc[None] < w[:, None] + 16), 0.0, MASKED)
            i += 1
    put("na_mask", mask)
    put("block", np.broadcast_to(np.arange(MOE_BLOCKS), (P, MOE_BLOCKS)))
    put("first", np.broadcast_to(PER_GROUP - np.arange(PER_GROUP), (P, PER_GROUP)))
    put("token", np.arange(SEQ).reshape(NQB, P).T)
    return t


def _arrays(i):
    one, end1, two, size2 = stream_plan()
    w_in = i["w_in"][0]
    cut = np.cumsum([0, D_RNN, D_RNN, D, KV_RANK, 512, IDX_DIM, IDX_HEADS, 2 * D])
    part = dict(zip(["xr", "gr", "q", "ckv", "qi", "ki", "wi", "mg"], [w_in[:, a:b] for a, b in zip(cut[:-1], cut[1:])]))
    parts = {n: _chunks(part[n]) for n in ("xr", "gr", "q", "ckv", "qi", "mg")}
    parts["mod_a"] = _chunks(i["w_mod"][0][:, :2 * D])
    parts["mod_b"] = _chunks(i["w_mod"][0][:, 2 * D:])
    parts["rg"] = np.stack([i["w_rg_a"][0], i["w_rg_x"][0]], 1).reshape(-1, P, P)
    parts["ki"] = _chunks(np.concatenate([part["ki"], part["ki"]], 1))
    parts["wi"] = _pack(part["wi"], 1)
    parts["rnn_out"] = _chunks(i["w_rnn_out"][0])
    parts["uk"] = _chunks(i["w_uk"][0].reshape(KV_RANK, -1))
    parts["uv"] = _blocks(i["w_uv"][0].reshape(KV_RANK, -1))
    parts["att_out"] = _chunks(i["w_att_out"][0])
    parts["out"] = _chunks(i["w_out"][0])
    parts["router"] = _pack(np.concatenate([i["w_group"][0], i["w_expert"][0]], 1), 3)
    first = _stream(one, end1, parts)

    layers = []
    for l in range(LAYERS):
        w = i["w_in_2"][l]
        cut = np.cumsum([0, 1024, 512, 1024, 512, MQ_RANK, 256, 32, 3 * D])
        part = dict(zip(["na_qk", "na_v", "df_qk", "df_v", "cq", "mckv", "kr", "gate"], [w[:, a:b] for a, b in zip(cut[:-1], cut[1:])]))
        parts = {n: _chunks(part[n]) for n in ("na_qk", "df_qk", "cq", "mckv")}
        parts["na_v"], parts["df_v"] = _blocks(part["na_v"]), _blocks(part["df_v"])
        parts["kr"] = _chunks(_wide(np.concatenate([part["mckv"][:, 192:], part["kr"]], 1)))
        for b, name in enumerate(("na_gb", "df_gb", "ml_gb")):
            g = _chunks(part["gate"][:, b * D:(b + 1) * D]).reshape(DC, DC, P, P)
            o = _chunks(i["w_branch_2"][l, b]).reshape(DC, 4, P, P)
            parts[name] = np.concatenate([g, o], 1).reshape(-1, P, P)
        qb = i["w_mla_qb_2"][l].reshape(MQ_RANK, HEADS, MLA_QK)
        parts["qb"] = np.concatenate([_chunks(_wide(qb[:, h])) for h in range(HEADS)])
        kvb = i["w_mla_kvb_2"][l].reshape(256, HEADS, 2, 64)
        parts["kvb_k"] = _chunks(kvb[:, :, 0].reshape(256, 512))
        parts["kvb_v"] = _blocks(kvb[:, :, 1].reshape(256, 512))
        parts["out2"] = _chunks(i["w_out_2"][l])
        gu = i["w_ffn_in_2"][l].reshape(D, 2, FFC, P).transpose(0, 2, 1, 3).reshape(D, 2 * D_FF)
        parts["ffn_in"] = _chunks(gu)
        parts["ffn_out"] = _chunks(i["w_ffn_out_2"][l])
        layers.append(_stream(two, size2, parts))

    vcol, n = vector_plan()
    names = {"b_mod": "b_mod", "norm1_g": "norm1_g", "conv_w": "conv_w", "conv_b": "conv_b", "b_rg_a": "b_rg_a",
             "b_rg_x": "b_rg_x", "lam": "lru_lambda", "kv_g": "kv_norm_g", "norm2_g": "norm2_g", "final_g": "final_g",
             "c": "c", "ln_in_g": "ln_in_g_2", "ln_in_b": "ln_in_b_2"}
    per = {"b_gate": "b_gate_2", "subln": "diff_subln_g_2", "mq_g": "mla_q_norm_g_2", "mkv_g": "mla_kv_norm_g_2",
           "ln1_g": "ln1_g_2", "ln1_b": "ln1_b_2", "ln2_g": "ln2_g_2", "ln2_b": "ln2_b_2"}
    vectors = np.zeros((P, n), np.float32)
    for name, (a, b) in vcol.items():
        v = i[names[name]] if name in names else i[per[name[:-1]]][int(name[-1])]
        vectors[:, a:b] = _columns(np.asarray(v).reshape(-1))

    rpb = np.zeros((LAYERS, HEADS, P, 3, GRID_ROWS, 16), np.float32)
    table = np.zeros((LAYERS, HEADS, 15, 31 + 64), np.float32)
    table[:, :, :, 32:63] = i["na_rpb_2"]
    for qr in range(GRID_ROWS):
        for qc in range(16):
            for dj in range(3):
                b = 32 + 16 * (dj - 1) - qc + 15
                rpb[:, :, qr * 16 + qc, dj] = table[:, :, 7 - qr:15 - qr, b:b + 16]

    def moe(w, cols):
        e, k, m = w.shape
        return np.ascontiguousarray(w.reshape(e, k // P, P, m).transpose(0, 2, 1, 3)).reshape(e, P, -1)

    return {
        "xT": np.ascontiguousarray(i["x"][0].T.reshape(DC, P, SEQ).transpose(1, 0, 2)),
        "wfirst": first, "wlayers": np.stack(layers), "consts": _constants(), "vectors": vectors,
        "brow": np.concatenate([i["b_group"][0], i["b_expert"][0]])[None, :],
        "lamv": i["diff_lambda_2"].reshape(1, -1),
        "rpb": rpb.reshape(LAYERS, HEADS, P, -1),
        "w1": moe(i["moe_w1"][0], 512), "w3": moe(i["moe_w3"][0], 512), "w2": moe(i["moe_w2"][0], 1024),
    }


def kernel(**inputs):
    import concourse.bacc as bacc
    from concourse.bass_utils import run_bass_kernel_spmd as run

    nc = bacc.Bacc("TRN2", target_bir_lowering=False, num_devices=1)
    arrays = _arrays(inputs)
    args = {name: nc.dram_tensor(name, a.shape, mybir.dt.from_np(a.dtype), kind="ExternalInput").ap() for name, a in arrays.items()}
    args["out"] = nc.dram_tensor("out", (P, DC, SEQ), F32, kind="ExternalOutput").ap()
    build(nc, **args)
    got = run(nc, [arrays], core_ids=[0]).results[0]["out"]
    got = got.transpose(2, 1, 0).reshape(NA_TILES, GRID_ROWS, 16, D).transpose(1, 0, 2, 3)
    return np.ascontiguousarray(got).reshape(1, SEQ, D)
```

```python
from contextlib import ExitStack
import math

import numpy as np

import concourse.bass as bass
from concourse import mybir

P = 128
SEQ = 512
D = 1024
DC = D // P
NQB = SEQ // P
D_RNN = 1280
RC = D_RNN // P
CONV_W = 4
LRU_C = 8.0
HEADS = 8
KV_RANK = 256
KVC = KV_RANK // P
IDX_HEADS = 8
IDX_DIM = 64
IDX_SCALE = IDX_DIM ** -0.5 * IDX_HEADS ** -0.5
TOPK = min(256, SEQ // 4)
DSA_SCALE = P ** -0.5
GROUPS = 4
PER_GROUP = 8
EXPERTS = GROUPS * PER_GROUP
D_EXPERT = 512
EPS = 1e-6
LN_EPS = 1e-5
MOE_BLOCKS = 40
MOE_SURE = 32

LAYERS = 2
D_FF = 2816
FFC = D_FF // P
GRID_W = 64
GRID_ROWS = SEQ // GRID_W
NA_TILES = 4
DN_ALPHA = (2 * LAYERS) ** 0.25
ROPE_THETA = 500000.0
MQ_RANK = 384
MQC = MQ_RANK // P
MLA_QK = 96
NA_SCALE = 64 ** -0.5
DIFF_SCALE = 64 ** -0.5
MLA_SCALE = MLA_QK ** -0.5
NA_KEYS = [(0, 2), (0, 3), (1, 4), (2, 4)]

CHUNKS = 16
SLOTS = 5
HI_SLOTS = 3

OUT_OF_SIGHT = -3.3e38
TAKEN = -3.0e38
LN2_HI = 0.693145751953125
MASKED = -1.0e30

ALU = mybir.AluOpType
ACT = mybir.ActivationFunctionType
AX_X = mybir.AxisListType.X
F32 = mybir.dt.float32
I32 = mybir.dt.int32
F32R = mybir.dt.float32r


def stream_plan():
    first = [("mod_a", 16 * DC), ("xr", RC * DC), ("rg", 2 * RC), ("ckv", KVC * DC), ("qi", 4 * DC), ("ki", DC),
             ("wi", 1), ("gr", RC * DC), ("mod_b", 32 * DC), ("mg", 16 * DC), ("q", HEADS * DC),
             ("rnn_out", DC * RC), ("uk", HEADS * KVC), ("uv", 4 * 2 * KVC), ("att_out", DC * DC),
             ("out", DC * DC), ("router", 3)]
    layer = [("na_v", 4 * DC), ("na_qk", 8 * DC), ("na_gb", DC * (DC + 4)),
             ("df_v", 4 * DC), ("df_qk", 8 * DC), ("cq", MQC * DC), ("mckv", KVC * DC), ("kr", DC),
             ("df_gb", DC * (DC + 4)), ("qb", HEADS * MQC), ("kvb_k", 4 * KVC),
             ("kvb_v", 4 * KVC), ("ml_gb", DC * (DC + 4)),
             ("out2", DC * DC), ("ffn_in", 2 * FFC * DC), ("ffn_out", DC * FFC)]
    blocks = {"uv": 16, "na_v": 16, "df_v": 16, "qb": 16, "kvb_v": 8, "ml_gb": 16, "router": 4}

    def place(parts, at):
        found = {}
        for name, n in parts:
            if name in blocks:
                at += -at % blocks[name]
            found[name] = at
            at += n
        return found, at + -at % CHUNKS

    one, end = place(first, 0)
    two, size = place(layer, 0)
    return one, end, two, size


def const_plan():
    widths = [("ident", P), ("tri", P), ("ones", P), ("cos_d", SEQ), ("sin_d", SEQ), ("cos_m", SEQ), ("sin_m", SEQ),
              ("perm_d", P), ("perm_m", P), ("dist", 7 * P), ("na_mask", 160), ("causal", P),
              ("block", MOE_BLOCKS), ("first", PER_GROUP), ("token", NQB)]
    at, found = 0, {}
    for name, n in widths:
        found[name] = (at, at + n)
        at += n
    return found, at


def vector_plan():
    widths = [("b_mod", 48), ("norm1_g", 8), ("conv_w", 4 * RC), ("conv_b", RC), ("b_rg_a", RC), ("b_rg_x", RC),
              ("lam", RC), ("kv_g", KVC), ("norm2_g", 8), ("final_g", 8), ("c", 8), ("ln_in_g", 8), ("ln_in_b", 8)]
    for l in range(LAYERS):
        widths += [(f"b_gate{l}", 24), (f"subln{l}", 1), (f"mq_g{l}", MQC), (f"mkv_g{l}", KVC), (f"ln1_g{l}", 8),
                   (f"ln1_b{l}", 8), (f"ln2_g{l}", 8), (f"ln2_b{l}", 8)]
    at, found = 0, {}
    for name, n in widths:
        found[name] = (at, at + n)
        at += n
    return found, at


class Bank:

    def __init__(self, ps, banks, full, free):
        self.ps, self.banks, self.full, self.free = ps, banks, full, free
        self.made, self.took = 0, 0

    def claim(self, pe):
        if self.made >= 2:
            pe.wait_ge(self.free, self.made - 1)
        b = self.banks[self.made % 2]
        self.made += 1
        return self.ps[:, b, :]

    def take(self, eng):
        b = self.banks[self.took % 2]
        self.took += 1
        eng.wait_ge(self.full, self.took)
        return self.ps[:, b, :]


def build(nc, xT, wfirst, wlayers, consts, vectors, brow, lamv, rpb, w1, w3, w2, out):
    one, end1, two, size2 = stream_plan()
    cst, NCONST = const_plan()
    vcol, NVEC = vector_plan()
    n_slots1, n_slots2 = end1 // CHUNKS, size2 // CHUNKS
    plain2 = range(two["qb"] // CHUNKS, two["ml_gb"] // CHUNKS)
    n_split = n_slots2 - len(plain2)

    def split_no(slot):
        if slot < n_slots1:
            return None
        l, s = divmod(slot - n_slots1, n_slots2)
        if s in plain2:
            return None
        return l * n_split + s - (len(plain2) if s >= plain2.stop else 0)

    with ExitStack() as ctx:

        def at(name, kb, shape, dt=F32):
            return nc.alloc_sbuf_tensor_at(name, shape, dt, offset=(nc.sbuf_base + 31) // 32 * 32 + int(kb * 1024))

        def sem(name):
            return ctx.enter_context(nc.semaphore(name))

        hT = at("hT", 0, [P, DC, SEQ])
        uT = at("uT", 16, [P, DC, SEQ])
        wring = at("wring", 32, [P, SLOTS, CHUNKS * P])
        w_hi = at("w_hi", 72, [P, HI_SLOTS, CHUNKS * P], F32R)
        w_lo = at("w_lo", 32, [P, SLOTS, CHUNKS * P], F32R)
        cs = at("cs", 189, [P, NCONST])
        vec = at("vec", 204.5, [P, NVEC])
        small = at("small", 206, [P, 384])

        def K(name, n=P):
            a, b = cst[name]
            return cs[0:n, a:b]

        def V(name):
            a, b = vcol[name]
            return vec[:, a:b]

        ident, ones = K("ident"), K("ones")
        used = [0]

        def sm(n):
            a = used[0]
            used[0] += n
            assert used[0] <= 384
            return small[:, a:a + n]

        mod = sm(48)
        a1, a2, csil, s_abs, s_z, s_zz, hsp, hbx = sm(8), sm(8), sm(8), sm(RC), sm(RC), sm(RC), sm(RC), sm(RC)
        wi_s = sm(NQB * IDX_HEADS)
        negmax, rsum, rinv = sm(8), sm(8), sm(8)
        lam_prod, lam_two, lam_neg = sm(64), sm(4), sm(2)
        subg, rinv2 = sm(2), sm(8)
        max8 = sm(24)
        s_int = sm(RC).bitcast(I32)
        gate12 = sm(2 * NQB)
        browS = sm(GROUPS + EXPERTS)[0:1, :]
        zeros = at("zeros", 116.5, [P, MOE_BLOCKS + 1], I32)
        xr = at("xr", 96, [P, RC, SEQ + CONV_W])
        rnn = at("rnn", 117, [P, RC, SEQ])
        lru_a = at("lru_a", 137, [P, RC, SEQ])
        lru_t = at("lru_t", 157, [P, 2, 3, SEQ])
        qi = at("qi", 169, [P, 4, SEQ])
        ki = at("ki", 177, [P, SEQ])
        ckv = at("ckv", 179, [P, KVC, SEQ])
        sqb = at("sqb", 183, [P, 2, SEQ])
        acc = at("acc", 187, [P, SEQ])
        qT = at("qT", 96, [P, HEADS, SEQ])
        sel = at("sel", 112, [P, 10, P])
        kT = at("kT", 117, [P, HEADS, SEQ])
        Lb = at("Lb", 133, [P, 2, SEQ])
        mixT = at("mixT", 137, [P, DC, SEQ])
        gb = at("gb", 153, [P, DC, SEQ])
        PT = at("PT", 169, [P, NQB, SEQ])
        Bb = at("Bb", 177, [P, SEQ])
        Pb = at("Pb", 183, [P, 3, SEQ])
        vS = at("vS", 16, [P, NQB, HEADS * P])
        rel = sqb

        mring = at("mring", 32, [P, 2, 3, 4 * D])
        u_tok = at("u_tok", 128, [P, NQB, D])
        gt = at("gt", 144, [P, 2048])
        big = at("big", 152, [P, MOE_BLOCKS * EXPERTS])
        tixI = at("tixI", 157, [P, 2 * NQB], I32)
        destI = at("destI", 157.125, [P, 2 * NQB], I32)
        tokI = at("tokI", 157.25, [P, NQB], I32)
        bexpI = at("bexpI", 157.5, [P, MOE_BLOCKS], I32)
        overI = at("overI", 157.75, [P, 1], I32)
        ids = at("ids", 158, [P, MOE_BLOCKS + 1], I32)
        xs = at("xs", 160, [P, 2, D])
        xsT = at("xsT", 168, [P, 2, DC, P])
        sil = at("sil", 176, [P, D_EXPERT])
        hid = at("hid", 178, [P, D_EXPERT])
        hidT = at("hidT", 180, [P, 4, P])
        ysb = at("ysb", 128, [P, 2, D])
        y_tok = at("y_tok", 96, [P, 2, NQB, D])
        qk2 = at("qk2", 96, [P, 8, SEQ])
        v2 = at("v2", 112, [P, NQB, SEQ])
        near = at("near", 120, [P, 2, 10 * P])
        rp = at("rp", 130, [P, 2, 3 * P])
        P2 = at("P2", 137, [P, 4, SEQ])
        PT2 = at("PT2", 145, [P, NQB, SEQ])
        o2 = at("o2", 153, [P, 4, SEQ])
        sg = at("sg", 161, [P, 2, SEQ])
        cq = at("cq", 137, [P, MQC, SEQ])
        ckv2 = at("ckv2", 143, [P, KVC, SEQ])
        krT = at("krT", 147, [P, SEQ])
        raw = at("raw", 149, [P, 2, SEQ])
        q96 = at("q96", 96, [P, HEADS, SEQ])
        k96 = at("k96", 112, [P, HEADS, SEQ])
        vM = at("vM", 128, [P, NQB, SEQ])
        x_hi = at("x_hi", 0, [P, DC, SEQ], F32R)
        x_lo = [at("xa_lo", 165, [P, DC, SEQ], F32R), at("xf_lo", 16, [P, DC, SEQ], F32R)]
        x_lo_f = [at("xa_lo_f", 165, [P, DC, SEQ]), uT]
        o_hi = at("o_hi", 96, [P, 4, SEQ], F32R)
        o_lo = at("o_lo", 153, [P, 4, SEQ], F32R)
        m_hi = at("m_hi", 104, [P, DC, SEQ], F32R)
        m_lo = at("m_lo", 16, [P, DC, SEQ], F32R)
        g_hi = at("g_hi", 96, [P, FFC, SEQ], F32R)
        g_lo = at("g_lo", 140, [P, FFC, SEQ], F32R)
        g_f = at("g_f", 140, [P, FFC, SEQ])
        lamS = at("lamS", 161, [P, LAYERS * 4 * 64])
        table = nc.dram_tensor("table", (P * (MOE_BLOCKS + 1), 1), I32, kind="Internal").ap()
        u_rows = nc.dram_tensor("u_rows", (SEQ, D), F32, kind="Internal").ap()
        y_rows = nc.dram_tensor("y_rows", (MOE_BLOCKS * P, D), F32, kind="Internal").ap()

        ps = ctx.enter_context(nc.psum_tensor("ps", [P, 8, SEQ], F32))

        const_in, vec_in, x_in = sem("const_in"), sem("vec_in"), sem("x_in")
        w_in = [sem(f"w_in{i}") for i in range(SLOTS)]
        w_used, hi_rdy, lo_rdy, t_rdy, y_hi_rdy, o2_rdy = (sem(n) for n in ("w_used", "hi_rdy", "lo_rdy", "t_rdy", "y_hi_rdy", "o2_rdy"))
        A = Bank(ps, (0, 1), sem("a_full"), sem("a_free"))
        B = Bank(ps, (2, 3), sem("b_full"), sem("b_free"))
        dve_step, act_step, pool_step = sem("dve_step"), sem("act_step"), sem("pool_step")
        c_silu, mod_rdy, pad_rdy = sem("c_silu"), sem("mod_rdy"), sem("pad_rdy")
        squared, sq_added, norm_var, norm_rstd, u_rdy = sem("squared"), sem("sq_added"), sem("norm_var"), sem("norm_rstd"), sem("u_rdy")
        a_coef, sp_rdy, sp_half = sem("a_coef"), sem("sp_rdy"), sem("sp_half")
        xr_rdy, conv_rdy, gate_t, gate_s, gate_a, lru_q = (sem(n) for n in ("xr_rdy", "conv_rdy", "gate_t", "gate_s", "gate_a", "lru_q"))
        lru_sqrt, h_rdy, gelu_rdy, gh_rdy = (sem(n) for n in ("lru_sqrt", "h_rdy", "gelu_rdy", "gh_rdy"))
        ckv_raw, qik_rdy, wi_rdy, ckv_rdy = (sem(n) for n in ("ckv_raw", "qik_rdy", "wi_rdy", "ckv_rdy"))
        g_rdy, q_rdy, k_rdy, v_rdy, mix_rdy, mix2_rdy = (sem(n) for n in ("g_rdy", "q_rdy", "k_rdy", "v_rdy", "mix_rdy", "mix2_rdy"))
        ix_score, ix_rel, ix_acc, sel_rdy = (sem(n) for n in ("ix_score", "ix_rel", "ix_acc", "sel_rdy"))
        sc_rdy, mx_rdy, exp_done, p_norm, turned, pt_rdy, att_rdy = (
            sem(n) for n in ("sc_rdy", "mx_rdy", "exp_done", "p_norm", "turned", "pt_rdy", "att_rdy"))
        h1_rdy = sem("h1_rdy")
        table_clear, brow_in, u_stored, logit_in, ohot, gl_diff, gl_exp, e_diff, e_exp, route_rdy = (sem(n) for n in (
            "table_clear", "brow_in", "u_stored", "logit_in", "ohot", "gl_diff", "gl_exp", "e_diff", "e_exp", "route_rdy"))
        tix_rdy, table_set, ids_in, moe_go = (sem(n) for n in ("tix_rdy", "table_set", "ids_in", "moe_go"))
        xs_in = [sem(f"xs_in{j}") for j in range(2)]
        up_in = [[sem(f"up_in{j}{k}") for k in range(2)] for j in range(2)]
        down_in = [sem(f"down_in{j}") for j in range(2)]
        xt_full, xt_rdy, gate_full, up_full, sil_done, hid_done = (sem(n) for n in (
            "xt_full", "xt_rdy", "gate_full", "up_full", "sil_done", "hid_done"))
        ht_full, ht_rdy, y0_full, y1_full, y0_rdy, y1_rdy = (sem(n) for n in (
            "ht_full", "ht_rdy", "y0_full", "y1_full", "y0_rdy", "y1_rdy"))
        y_stored = [sem(f"y_stored{j}") for j in range(2)]
        rows_back, mixed_rows, h2_rdy, b1_rdy, summed, centered, x_rdy = (sem(n) for n in (
            "rows_back", "mixed_rows", "h2_rdy", "b1_rdy", "summed", "centered", "x_rdy"))
        lam_in, lam_sum, lam_exp, sub_rdy = (sem(n) for n in ("lam_in", "lam_sum", "lam_exp", "sub_rdy"))
        rp_in, near_rdy, roped, vals_rdy, keys_rdy = (sem(n) for n in ("rp_in", "near_rdy", "roped", "vals_rdy", "keys_rdy"))
        s_free, pair_exp, pair_norm, pair_turned, pair_pt = (sem(n) for n in ("s_free", "pair_exp", "pair_norm", "pair_turned", "pair_pt"))
        pair_sc, pair_mx, o_rdy, sg_rdy, sg_used, merged_rdy = (sem(n) for n in ("pair_sc", "pair_mx", "o_rdy", "sg_rdy", "sg_used", "merged_rdy"))
        lat_rdy, kr_rdy, hid_rdy = (sem(n) for n in ("lat_rdy", "kr_rdy", "hid_rdy"))
        stored = sem("stored")

        n_norm = {"act": 0, "dve": 0, "pe": 0, "i": 0}
        cnt = {"hi": n_slots1, "t_a": 0, "t_d": 0, "sq_a": 0, "sq_d": 0, "sq_p": 0, "nv_a": 0, "nv_d": 0, "dv": 0, "av": 0, "pv": 0}
        plan = {"at": -1, "owed": False}

        def after(eng, ins, s, key):
            ins.then_inc(s, 1)
            cnt[key] += 1
            eng.wait_ge(s, cnt[key])

        def chunk(pe, c, n=1):
            slot = c // CHUNKS
            if slot != plan["at"]:
                assert not plan["owed"]
                plan["owed"] = plan["at"] >= 0
                plan["at"] = slot
                q = split_no(slot)
                if q is None:
                    pe.wait_ge(w_in[slot % SLOTS], 16 * (slot // SLOTS + 1))
                else:
                    pe.wait_ge(lo_rdy, q + 1)
            return views(c, n)

        def views(c, n=1):
            slot, o = c // CHUNKS, (c % CHUNKS) * P
            q = split_no(slot)
            if q is None:
                return wring[:, slot % SLOTS, o:o + n * P]
            return w_hi[:, q % HI_SLOTS, o:o + n * P], w_lo[:, slot % SLOTS, o:o + n * P]

        def said(ins):
            if plan["owed"]:
                ins.then_inc(w_used, 1)
                plan["owed"] = False

        def tile(pe, bank, c0, rhs, nk, m=P, wait=None):
            for k in range(nk):
                w = chunk(pe, c0 + k)
                if wait is not None:
                    wait(k)
                ins = pe.matmul(bank, w[:, 0:m], rhs[:, k, :], start=(k == 0), stop=(k == nk - 1))
                if k < nk - 1:
                    said(ins)
            return ins

        def tile3(pe, bank, c0, hi, lo, nk, m=P, wait=None):
            for k in range(nk):
                wh, wl = chunk(pe, c0 + k)
                if wait is not None:
                    wait(k)
                said(pe.matmul(bank, wh[:, 0:m], hi[:, k, :], start=(k == 0), stop=False))
                pe.matmul(bank, wh[:, 0:m], lo[:, k, :], start=False, stop=False)
                ins = pe.matmul(bank, wl[:, 0:m], hi[:, k, :], start=False, stop=(k == nk - 1))
            return ins

        def norm_pe(pe, n):
            cnt["sq_p"] += n
            pe.wait_ge(sq_added, cnt["sq_p"])
            b = B.claim(pe)
            pe.matmul(b, ones, acc[:], start=True, stop=True).then_inc(B.full, 1)

        def squares(act, X, n, wait=None):
            for c in range(n):
                if wait is not None:
                    wait(c)
                k = cnt["sq_a"]
                if k >= 2:
                    act.wait_ge(sq_added, k - 1)
                act.activation(sqb[:, k % 2, :], X[:, c, :], ACT.Square).then_inc(squared, 1)
                cnt["sq_a"] += 1

        def weights_hi(act, l, c):
            last = min(n_slots1 + l * n_slots2 + c // CHUNKS + 2, n_slots1 + LAYERS * n_slots2 - 1)
            while cnt["hi"] <= last:
                slot = cnt["hi"]
                q = split_no(slot)
                if q is not None:
                    act.wait_ge(w_in[slot % SLOTS], 16 * (slot // SLOTS + 1))
                    if q >= HI_SLOTS:
                        before = next(g for g in range(slot - HI_SLOTS - len(plain2), slot) if split_no(g) == q - HI_SLOTS)
                        act.wait_ge(w_used, before + 1)
                    act.activation(w_hi[:, q % HI_SLOTS, :], wring[:, slot % SLOTS, :], ACT.Copy).then_inc(hi_rdy, 1)
                cnt["hi"] += 1

        def weights_lo(pool, l, s):
            slot = n_slots1 + l * n_slots2 + s
            q = split_no(slot)
            if q is not None:
                pool.wait_ge(hi_rdy, q + 1)
                pool.tensor_tensor(w_lo[:, slot % SLOTS, :], wring[:, slot % SLOTS, :], w_hi[:, q % HI_SLOTS, :].bitcast(F32),
                                   ALU.subtract).then_inc(lo_rdy, 1)

        def norm_hi(act, b):
            for c in range(DC):
                cnt["t_a"] += 1
                act.wait_ge(t_rdy, cnt["t_a"])
                act.activation(x_hi[:, c, :], x_lo_f[b[1]][:, c, :], ACT.Identity, bias=b[0][:, c:c + 1]).then_inc(y_hi_rdy, 1)

        def root(act):
            cnt["nv_a"] += 1
            act.wait_ge(norm_var, cnt["nv_a"])
            act.activation(sqb[:, 0, :], acc[:], ACT.Sqrt).then_inc(norm_rstd, 1)

        def sum_squares(dve, n):
            for c in range(n):
                k = cnt["sq_d"]
                dve.wait_ge(squared, k + 1)
                if c == 0:
                    ins = dve.tensor_copy(acc[:], sqb[:, k % 2, :])
                else:
                    ins = dve.tensor_tensor(acc[:], acc[:], sqb[:, k % 2, :], ALU.add)
                ins.then_inc(sq_added, 1)
                cnt["sq_d"] += 1
                dve.wait_ge(sq_added, k + 1)

        def inverse_var(dve, width, eps):
            b = B.take(dve)
            r, v = sqb[:, 0, :], sqb[:, 1, :]
            dve.tensor_scalar(v, b, 1.0 / width, eps, ALU.mult, ALU.add).then_inc(B.free, 1)
            dve.wait_ge(B.free, B.took)
            dve.reciprocal(acc[:], v).then_inc(norm_var, 1)
            cnt["nv_d"] += 1
            dve.wait_ge(norm_rstd, cnt["nv_d"])
            after(dve, dve.tensor_tensor(v, v, r, ALU.mult), dve_step, "dstep")
            after(dve, dve.tensor_tensor(v, v, r, ALU.mult), dve_step, "dstep")
            after(dve, dve.tensor_scalar(v, v, -0.5, 1.5, ALU.mult, ALU.add), dve_step, "dstep")
            after(dve, dve.tensor_tensor(r, r, v, ALU.mult), dve_step, "dstep")

        rstd = sqb[:, 0, :]

        def B_also_free(dve):
            cnt["own"] = cnt.get("own", 0)
            dve.engine_nop().then_inc(B.free, 1)

        def add_up(dve, X, c):
            dve.tensor_tensor(acc[:], X[:, 0, :] if c == 1 else acc[:], X[:, c, :], ALU.add).then_inc(summed, 1)
            cnt["sum"] = cnt.get("sum", 0) + 1
            dve.wait_ge(summed, cnt["sum"])

        def center(dve, X):
            b = B.take(dve)
            dve.tensor_scalar(acc[:], b, 1.0 / D, None, ALU.mult).then_inc(B.free, 1)
            dve.wait_ge(B.free, B.took)
            for c in range(DC):
                dve.tensor_tensor(X[:, c, :], X[:, c, :], acc[:], ALU.subtract).then_inc(centered, 1)
            cnt["cen"] = cnt.get("cen", 0) + DC
            dve.wait_ge(centered, cnt["cen"])

        def mean_pe(pe):
            cnt["sum_p"] = cnt.get("sum_p", 0) + DC - 1
            pe.wait_ge(summed, cnt["sum_p"])
            pe.matmul(B.claim(pe), ones, acc[:], start=True, stop=True).then_inc(B.full, 1)

        def normed(dve, X, Y, g, b, turn=False):
            sum_squares(dve, DC)
            inverse_var(dve, D, LN_EPS)
            for c in range(DC):
                after(dve, dve.scalar_tensor_tensor(out=X[:, c, :], in0=X[:, c, :], scalar=g[:, c:c + 1], in1=rstd,
                                                    op0=ALU.mult, op1=ALU.mult), dve_step, "dstep")
                x, y = X[:, c, :], Y[:, c, :]
                if turn:
                    x = x.rearrange("p (r j c) -> p r j c", r=GRID_ROWS, j=NA_TILES)
                    y = y.rearrange("p (j r c) -> p r j c", r=GRID_ROWS, j=NA_TILES)
                dve.tensor_scalar(y, x, b[:, c:c + 1], None, ALU.add).then_inc(x_rdy, 1)

        def normed_split(dve, X, to, g, b, turn=False):
            sum_squares(dve, DC)
            inverse_var(dve, D, LN_EPS)

            def low(c):
                t = x_lo_f[to][:, c, :]
                dve.wait_ge(y_hi_rdy, cnt["t_d"] + c + 1)
                dve.scalar_tensor_tensor(out=x_lo[to][:, c, :], in0=t, scalar=b[:, c:c + 1], in1=x_hi[:, c, :].bitcast(F32),
                                         op0=ALU.add, op1=ALU.subtract).then_inc(x_rdy, 1)
            for c in range(DC):
                y = x_lo_f[to][:, c, :]
                ins = dve.scalar_tensor_tensor(out=X[:, c, :] if turn else y, in0=X[:, c, :], scalar=g[:, c:c + 1], in1=rstd, op0=ALU.mult, op1=ALU.mult)
                if turn:
                    after(dve, ins, dve_step, "dstep")
                    ins = dve.tensor_copy(y.rearrange("p (j r c) -> p r j c", r=GRID_ROWS, j=NA_TILES),
                                          X[:, c, :].rearrange("p (r j c) -> p r j c", r=GRID_ROWS, j=NA_TILES))
                ins.then_inc(t_rdy, 1)
                if c >= 1:
                    low(c - 1)
            low(DC - 1)
            cnt["t_d"] += DC

        names = {"lg": 144, "gmax": 4, "w": 32, "wm": 4, "goh": 16, "gd": 16, "ge": 16, "es": 32, "m1": 4, "m2": 4,
                 "oh1": 32, "oh2": 32, "d": 4, "ex": 4, "gw": 4, "p1": 4, "M1": 128, "M2": 128, "M": 128, "pos": 128,
                 "cts": 32, "nb": 32, "cum": 32, "st": 32, "bq": 128, "tix": 128, "ix": 4, "be": MOE_BLOCKS}
        starts = dict(zip(names, np.cumsum([0] + list(names.values())).tolist()))

        def T(name):
            return gt[:, starts[name]:starts[name] + names[name]]

        A_ROWS = RC + 2 * RC + KVC + 4 + 1 + 1 + RC + 2 * DC + HEADS + HEADS + 2 * NQB + HEADS

        def units_pe(pe, units, ready, Pb=Pb):
            U = len(units)
            for i in range(U + 3):
                if i < U:
                    u = units[i]
                    k = cnt["pv"] + i
                    ready(i)
                    if k >= 2:
                        pe.wait_ge(exp_done, k - 1)
                    ins = pe.matmul(ps[:, 4 + k % 2, 0:u["nk"] * P], u["q"], u["k"], start=True, stop=True)
                    ins.then_inc(sc_rdy, 1)
                if 2 <= i < U + 2:
                    u = units[i - 2]
                    k = cnt["pv"] + i - 2
                    pe.wait_ge(p_norm, k + 1)
                    if k >= 2:
                        pe.wait_ge(pt_rdy, k - 1)
                    for j in range(u["nk"]):
                        ins = pe.transpose(ps[:, 6 + k % 2, j * P:(j + 1) * P], Pb[:, k % 3, j * P:(j + 1) * P], ident)
                    ins.then_inc(turned, 1)
                if i >= 3 and "sum" in units[i - 3]:
                    pe.wait_ge(pt_rdy, cnt["pv"] + i - 2)
                    units[i - 3]["sum"](pe)
            cnt["pv"] += U

        def units_dve(dve, units, Pb=Pb):
            U = len(units)

            def norm(i):
                k = cnt["dv2"] + i
                n = units[i]["nk"] * P
                dve.wait_ge(exp_done, k + 1)
                after(dve, dve.reciprocal(rinv[:, k % 4:k % 4 + 1], rsum[:, k % 4:k % 4 + 1]), dve_step, "dstep")
                dve.tensor_scalar(Pb[:, k % 3, 0:n], Pb[:, k % 3, 0:n], rinv[:, k % 4:k % 4 + 1], None, ALU.mult).then_inc(p_norm, 1)

            for i, u in enumerate(units):
                k = cnt["dv2"] + i
                n = u["nk"] * P
                dve.wait_ge(sc_rdy, k + 1)
                s = ps[:, 4 + k % 2, 0:n]
                m = negmax[:, k % 4:k % 4 + 1]
                if "bias" in u:
                    b = u["bias"](dve)
                    if k >= 2:
                        dve.wait_ge(exp_done, k - 1)
                    after(dve, dve.scalar_tensor_tensor(out=Lb[:, k % 2, 0:n], in0=s, scalar=u["scale"], in1=b,
                                                        op0=ALU.mult, op1=ALU.add), dve_step, "dstep")
                    dve.reduce_max(m, Lb[:, k % 2, 0:n], AX_X, negate=True).then_inc(mx_rdy, 1)
                else:
                    after(dve, dve.reduce_max(m, s, AX_X, negate=True), dve_step, "dstep")
                    dve.tensor_scalar(m, m, u["scale"], None, ALU.mult).then_inc(mx_rdy, 1)
                if i >= 1:
                    norm(i - 1)
            norm(U - 1)
            cnt["dv2"] += U

        def units_act(act, units, sums, Pb=Pb, PT=PT):
            U = len(units)
            for i in range(U + 3):
                if i < U:
                    u = units[i]
                    k = cnt["av2"] + i
                    n = u["nk"] * P
                    act.wait_ge(mx_rdy, k + 1)
                    if k >= 3:
                        act.wait_ge(turned, k - 2)
                    src, sc = (Lb[:, k % 2, 0:n], 1.0) if "bias" in u else (ps[:, 4 + k % 2, 0:n], u["scale"])
                    act.activation(Pb[:, k % 3, 0:n], src, ACT.Exp, bias=negmax[:, k % 4:k % 4 + 1], scale=sc,
                                   accum_out=rsum[:, k % 4:k % 4 + 1]).then_inc(exp_done, 1)
                if i >= 3 and "sum" in units[i - 3]:
                    sums(units[i - 3])
                if 2 <= i < U + 2:
                    u = units[i - 2]
                    k = cnt["av2"] + i - 2
                    act.wait_ge(turned, k + 1)
                    t = ps[:, 6 + k % 2, 0:u["nk"] * P].rearrange("p (j q) -> p j q", q=P)
                    act.activation(PT[:, 0:u["nk"], u["qb"] * P:(u["qb"] + 1) * P], t, ACT.Copy).then_inc(pt_rdy, 1)
            cnt["av2"] += U

        cnt.update({"dv2": 0, "av2": 0, "dstep": 0, "astep": 0})

        def na_units():
            units, i0 = [], 0
            for h in range(HEADS):
                r, i0 = 64 * (h % 2), 0
                for n, (lo, hi) in enumerate(NA_KEYS):
                    units.append({"nk": hi - lo, "qb": n, "h": h, "scale": NA_SCALE,
                                  "q": qk2[r:r + 64, h // 2, n * P:(n + 1) * P], "k": qk2[r:r + 64, 4 + h // 2, lo * P:hi * P],
                                  "bias": lambda dve, h=h, a=i0, b=i0 + hi - lo, n=n: (
                                      wait_near(dve, h) if n == 0 else None, near[:, h % 2, a * P:b * P])[1]})
                    i0 += hi - lo

                def total(pe, h=h, r=r):
                    b = A.claim(pe)
                    for n, (lo, hi) in enumerate(NA_KEYS):
                        for j in range(lo, hi):
                            ins = pe.matmul(b[r:r + 64, n * P:(n + 1) * P], v2[:, j, h * 64:(h + 1) * 64],
                                            PT2[:, j - lo, n * P:(n + 1) * P], start=(j == lo), stop=(j == hi - 1))
                    ins.then_inc(A.full, 1)
                units[-1]["sum"] = total
            return units

        def wait_near(dve, h):
            cnt["near"] = cnt.get("near", 0) + 1
            dve.wait_ge(near_rdy, cnt["near"])

        def mla_units():
            units = []
            for h in range(HEADS):
                r = 64 * (h % 2)
                for qb in range(NQB):
                    units.append({"nk": NQB, "qb": qb, "h": h, "scale": MLA_SCALE,
                                  "q": q96[0:MLA_QK, h, qb * P:(qb + 1) * P], "k": k96[0:MLA_QK, h, :]})

                def total(pe, h=h, r=r):
                    b = A.claim(pe)
                    for j in range(NQB):
                        ins = pe.matmul(b[r:r + 64, :], vM[:, j, h * 64:(h + 1) * 64], PT2[:, j, :], start=(j == 0), stop=(j == NQB - 1))
                    ins.then_inc(A.full, 1)
                units[-1]["sum"] = total
            return units

        pairs = [(h, qb) for h in range(4) for qb in range(NQB)]
        pair_banks = ((4, 5), (2, 3))

        dsa = []
        for h in range(HEADS):
            for qb in range(NQB):
                dsa.append({"nk": qb + 1, "qb": qb, "h": h, "scale": DSA_SCALE,
                            "q": qT[:, h, qb * P:(qb + 1) * P], "k": kT[:, h, 0:(qb + 1) * P]})

                def bias(dve, h=h, qb=qb):
                    n = (qb + 1) * P
                    o = qb * (qb + 1) // 2
                    d = K("dist")[:, (NQB - 1 - qb) * P:(NQB - 1 - qb) * P + n]
                    after(dve, dve.scalar_tensor_tensor(
                        out=Bb[:, 0:n], in0=d, scalar=-(2.0 ** (-8.0 * (h + 1) / HEADS)),
                        in1=sel[:, o:o + qb + 1, :].rearrange("p j q -> p (j q)"), op0=ALU.mult, op1=ALU.add),
                        dve_step, "dstep")
                    return Bb[:, 0:n]
                dsa[-1]["bias"] = bias

            def total(pe, h=h):
                b = A.claim(pe)
                for j in range(NQB):
                    ins = pe.matmul(b[:, j * P:SEQ], vS[:, j, h * P:(h + 1) * P], PT[:, j, j * P:SEQ],
                                    start=(j == 0), stop=(j == NQB - 1))
                ins.then_inc(A.full, 1)
            dsa[-1]["sum"] = total

        U_DSA = HEADS * NQB
        U_LAYER = 2 * HEADS * NQB

        def layer_pe(pe, l):
            base = {name: end1 + l * size2 + c for name, c in two.items()}
            xa, xf = (x_hi, x_lo[0]), (x_hi, x_lo[1])

            def gated(c0, branch, between=None):
                for m in range(DC):
                    tile3(pe, A.claim(pe), c0 + m * (DC + 4), *xa, DC).then_inc(A.full, 1)
                    tile3(pe, B.claim(pe), c0 + m * (DC + 4) + DC, o_hi, o_lo, 4,
                          wait=(lambda k: pe.wait_ge(o2_rdy, 4 * (3 * l + branch) + k + 1)) if m == 0 else None).then_inc(B.full, 1)
                    if between is not None:
                        between(m)

            def values(c0, wait=None):
                for j in range(NQB):
                    b = A.claim(pe)
                    for k in range(DC):
                        c = c0 + 4 * k
                        if k < DC // 2 or j == NQB - 1:
                            wh, wl = chunk(pe, c, 4)
                        else:
                            if j == 0 and k == DC // 2:
                                pe.wait_ge(lo_rdy, split_no(c // CHUNKS) + 1)
                            wh, wl = views(c, 4)
                        if j == 0 and wait is not None:
                            wait(k)
                        xh, xl = (x[:, k, j * P:(j + 1) * P] for x in xa)
                        said(pe.matmul(b, xh, wh, start=(k == 0), stop=False))
                        pe.matmul(b, xh, wl, start=False, stop=False)
                        ins = pe.matmul(b, xl, wh, start=False, stop=(k == DC - 1))
                    ins.then_inc(A.full, 1)

            values(base["na_v"], lambda k: pe.wait_ge(x_rdy, 2 * DC * l + k + 1))
            for m in range(8):
                tile3(pe, A.claim(pe), base["na_qk"] + m * DC, *xa, DC).then_inc(A.full, 1)
            units_pe(pe, na_units(), lambda i: pe.wait_ge(A.free, A.made) if i == 0 else None, P2)
            gated(base["na_gb"], 0)

            values(base["df_v"])

            def turn(perm, m, n=P):
                pe.wait_ge(A.free, m)
                pe.matmul(B.claim(pe)[0:n, :], perm[0:n, 0:n], raw[0:n, (cnt["rp"]) % 2, :], start=True, stop=True).then_inc(B.full, 1)
                cnt["rp"] += 1
            for m in range(8):
                tile3(pe, A.claim(pe), base["df_qk"] + m * DC, *xa, DC).then_inc(A.full, 1)
                if m >= 1:
                    turn(K("perm_d"), A.made - 1)
            turn(K("perm_d"), A.made)
            pe.wait_ge(B.free, B.made)
            pe.wait_ge(roped, l * 16 + 8)
            U = len(pairs)
            for i in range(U + 3):
                if i < U:
                    h, qb = pairs[i]
                    k = l * U + i
                    if k >= 2:
                        pe.wait_ge(pair_exp, 2 * (k - 1))
                    for a in range(2):
                        r = 64 * a
                        pe.matmul(ps[:, pair_banks[k % 2][a], :], qk2[r:r + 64, h, qb * P:(qb + 1) * P], qk2[r:r + 64, 4 + h, :],
                                  start=True, stop=True).then_inc(pair_sc, 1)
                if 2 <= i < U + 2:
                    k = l * U + i - 2
                    pe.wait_ge(pair_norm, k + 1)
                    if k >= 2:
                        pe.wait_ge(pair_pt, k - 1)
                    for j in range(NQB):
                        ins = pe.transpose(ps[:, 6 + k % 2, j * P:(j + 1) * P], P2[:, 2 * (k % 2), j * P:(j + 1) * P], ident)
                    ins.then_inc(pair_turned, 1)
                if i >= 3 and pairs[i - 3][1] == NQB - 1:
                    h = pairs[i - 3][0]
                    pe.wait_ge(pair_pt, l * U + i - 2)
                    b = A.claim(pe)
                    for j in range(NQB):
                        ins = pe.matmul(b, v2[:, j, h * P:(h + 1) * P], PT2[:, j, :], start=(j == 0), stop=(j == NQB - 1))
                    ins.then_inc(A.full, 1)
            for m in range(MQC + KVC):
                tile3(pe, A.claim(pe), base["cq"] + m * DC, *xa, DC).then_inc(A.full, 1)
                if m < 4:
                    norm_pe(pe, 1)
            tile3(pe, A.claim(pe)[0:MLA_QK, :], base["kr"], *xa, DC, MLA_QK).then_inc(A.full, 1)
            kr_copied = A.made

            def latent_norms(m):
                if m == 1:
                    norm_pe(pe, MQC)
                elif m == 3:
                    norm_pe(pe, KVC)
                elif m == 5:
                    pe.wait_ge(A.free, kr_copied)
                    pe.matmul(B.claim(pe)[0:MLA_QK, :], K("perm_m")[0:MLA_QK, 0:MLA_QK], krT[0:MLA_QK, :], start=True, stop=True).then_inc(B.full, 1)
            gated(base["df_gb"], 1, latent_norms)

            pe.wait_ge(lat_rdy, (l + 1) * (MQC + KVC))
            for h in range(HEADS):
                tile(pe, A.claim(pe)[0:MLA_QK, :], base["qb"] + h * MQC, cq, MQC, MLA_QK).then_inc(A.full, 1)
                if h >= 1:
                    turn(K("perm_m"), A.made - 1, MLA_QK)
            turn(K("perm_m"), A.made, MLA_QK)
            for h in range(HEADS):
                b = A.claim(pe)
                for k in range(KVC):
                    w = chunk(pe, base["kvb_k"] + (h // 2) * KVC + k)
                    ins = pe.matmul(b[0:64, :], w[:, 64 * (h % 2):64 * (h % 2) + 64], ckv2[:, k, :], start=(k == 0), stop=(k == KVC - 1))
                    if k < KVC - 1:
                        said(ins)
                ins.then_inc(A.full, 1)
            for s_ in range(NQB):
                b = A.claim(pe)
                for k in range(KVC):
                    ins = pe.matmul(b, ckv2[:, k, s_ * P:(s_ + 1) * P], chunk(pe, base["kvb_v"] + 4 * k, 4), start=(k == 0), stop=(k == KVC - 1))
                    if k < KVC - 1:
                        said(ins)
                ins.then_inc(A.full, 1)
            pe.wait_ge(roped, l * 16 + 16)
            pe.wait_ge(keys_rdy, l + 1)
            units_pe(pe, mla_units(), lambda i: pe.wait_ge(A.free, A.made) if i == 0 else None, P2)
            gated(base["ml_gb"], 2)

            pe.wait_ge(merged_rdy, (l + 1) * 3 * DC)
            for m in range(DC):
                tile3(pe, B.claim(pe), base["out2"] + m * DC, m_hi, m_lo, DC).then_inc(B.full, 1)
            mean_pe(pe)
            norm_pe(pe, DC)
            for m in range(FFC):
                tile3(pe, A.claim(pe), base["ffn_in"] + 2 * m * DC, *xf, DC,
                     wait=(lambda k: pe.wait_ge(x_rdy, 2 * DC * l + DC + k + 1)) if m == 0 else None).then_inc(A.full, 1)
                tile3(pe, B.claim(pe), base["ffn_in"] + (2 * m + 1) * DC, *xf, DC).then_inc(B.full, 1)
            for m in range(DC):
                tile3(pe, B.claim(pe), base["ffn_out"] + m * FFC, g_hi, g_lo, FFC,
                     wait=(lambda k: pe.wait_ge(hid_rdy, l * FFC + k + 1)) if m == 0 else None).then_inc(B.full, 1)
            mean_pe(pe)
            norm_pe(pe, DC)

        def layer_act(act, l):
            def copy(to, n=P):
                act.activation(to, A.take(act)[0:n, :], ACT.Copy).then_inc(A.free, 1)

            def gates(branch, between=None):
                bg = V(f"b_gate{l}")
                for m in range(DC):
                    weights_hi(act, l, two[("na_gb", "df_gb", "ml_gb")[branch]] + m * (DC + 4))
                    k = (3 * l + branch) * DC + m
                    if k >= 2:
                        act.wait_ge(sg_used, k - 1)
                    act.activation(sg[:, k % 2, :], A.take(act), ACT.Sigmoid, bias=bg[:, branch * DC + m:branch * DC + m + 1]).then_inc(A.free, 1)
                    if between is not None:
                        between(m)

            for j in range(NA_TILES):
                weights_hi(act, l, two["na_v"] + (CHUNKS if j == NA_TILES - 1 else 0))
                copy(v2[:, j, :])
            for m in range(8):
                weights_hi(act, l, two["na_qk"] + m * DC)
                copy(qk2[:, m, :])

            def na_out(u):
                r = 64 * (u["h"] % 2)
                act.activation(o2[r:r + 64, u["h"] // 2, :], A.take(act)[r:r + 64, :], ACT.Copy).then_inc(A.free, 1)
            units_act(act, na_units(), na_out, P2, PT2)
            gates(0)

            for s_ in range(NQB):
                weights_hi(act, l, two["df_v"] + (CHUNKS if s_ == NQB - 1 else 0))
                copy(v2[:, s_, :])
            for m in range(8):
                weights_hi(act, l, two["df_qk"] + m * DC)
                if m >= 2:
                    act.wait_ge(roped, l * 16 + m - 1)
                copy(raw[:, m % 2, :])
            U = len(pairs)
            for i in range(U + 3):
                if i < U:
                    k = l * U + i
                    if k >= 2:
                        act.wait_ge(pair_turned, k - 1)
                    for a in range(2):
                        act.wait_ge(pair_mx, 2 * k + a + 1)
                        act.activation(P2[:, 2 * (k % 2) + a, :], ps[:, pair_banks[k % 2][a], :], ACT.Exp,
                                       bias=negmax[:, 2 * (k % 2) + a:2 * (k % 2) + a + 1], scale=DIFF_SCALE,
                                       accum_out=rsum[:, 2 * (k % 2) + a:2 * (k % 2) + a + 1]).then_inc(pair_exp, 1)
                if i >= 3 and pairs[i - 3][1] == NQB - 1:
                    copy(o2[:, pairs[i - 3][0], :])
                if 2 <= i < U + 2:
                    k = l * U + i - 2
                    act.wait_ge(pair_turned, k + 1)
                    qb = pairs[i - 2][1]
                    act.activation(PT2[:, :, qb * P:(qb + 1) * P], ps[:, 6 + k % 2, :].rearrange("p (j q) -> p j q", q=P),
                                   ACT.Copy).then_inc(pair_pt, 1)
            act.wait_ge(A.free, A.took)
            for h in range(4):
                if h:
                    act.wait_ge(o_rdy, 4 * l + h)
                squares(act, o2[:, h:h + 1, :], 1)
                weights_hi(act, l, two["cq"] + h * DC)
                copy(cq[:, h, :] if h < MQC else ckv2[:, h - MQC, :])
                root(act)
            for m in range(4 - MQC, KVC):
                weights_hi(act, l, two["mckv"] + m * DC)
                copy(ckv2[:, m, :])
            copy(krT[0:MLA_QK, :], MLA_QK)
            latents_copied = A.took

            def latent_norms(m):
                if m == 1:
                    act.wait_ge(A.free, latents_copied)
                    act.wait_ge(o_rdy, 4 * (l + 1))
                    squares(act, cq, MQC)
                elif m == 2:
                    root(act)
                    act.wait_ge(lat_rdy, l * (MQC + KVC) + MQC)
                    squares(act, ckv2, KVC)
                elif m == 4:
                    root(act)
            gates(1, latent_norms)
            act.wait_ge(kr_rdy, l + 1)
            for h in range(HEADS):
                if h >= 2:
                    act.wait_ge(roped, l * 16 + 8 + h - 1)
                copy(raw[0:MLA_QK, h % 2, :], MLA_QK)
            for h in range(HEADS):
                copy(k96[0:64, h, :], 64)
            for s_ in range(NQB):
                copy(vM[:, s_, :])

            def mla_out(u):
                r = 64 * (u["h"] % 2)
                act.activation(o2[r:r + 64, u["h"] // 2, :], A.take(act)[r:r + 64, :], ACT.Copy).then_inc(A.free, 1)
            units_act(act, mla_units(), mla_out, P2, PT2)
            gates(2)

            for m in range(DC):
                weights_hi(act, l, two["out2"] + m * DC)
            squares(act, hT, DC, lambda c: act.wait_ge(centered, DC + 2 * DC * l + c + 1))
            root(act)
            norm_hi(act, (V(f"ln1_b{l}"), 1))
            for m in range(FFC):
                weights_hi(act, l, two["ffn_in"] + 2 * m * DC)
                act.activation(g_f[:, m, :], A.take(act), ACT.Silu).then_inc(A.free, 1)
            for c in range(0, DC * FFC, CHUNKS):
                weights_hi(act, l, two["ffn_out"] + c)
            squares(act, hT, DC, lambda c: act.wait_ge(centered, 2 * DC + 2 * DC * l + c + 1))
            root(act)
            if l < LAYERS - 1:
                norm_hi(act, (V(f"ln2_b{l}"), 0))

        def layer_dve(dve, l):
            step = lambda ins: after(dve, ins, dve_step, "dstep")
            TT, TS, STT = dve.tensor_tensor, dve.tensor_scalar, dve.scalar_tensor_tensor

            def branch(n, a_free, between=None):
                for m in range(DC):
                    k = (3 * l + n) * DC + m
                    dve.wait_ge(A.free, a_free + m + 1)
                    if n == 0:
                        TT(uT[:, m, :], B.take(dve), sg[:, k % 2, :], ALU.mult).then_inc(B.free, 1)
                        dve.wait_ge(B.free, B.took)
                        dve.engine_nop().then_inc(sg_used, 1)
                        dve.engine_nop().then_inc(merged_rdy, 1)
                    else:
                        TT(sg[:, k % 2, :], B.take(dve), sg[:, k % 2, :], ALU.mult).then_inc(B.free, 1)
                        dve.wait_ge(B.free, B.took)
                        TT(uT[:, m, :], uT[:, m, :], sg[:, k % 2, :], ALU.add).then_inc(sg_used, 1)
                        if n == 2:
                            dve.wait_ge(sg_used, k + 1)
                            step(dve.tensor_copy(m_hi[:, m, :], uT[:, m, :]))
                            TT(m_lo[:, m, :], uT[:, m, :], m_hi[:, m, :].bitcast(F32), ALU.subtract).then_inc(merged_rdy, 1)
                        else:
                            dve.engine_nop().then_inc(merged_rdy, 1)
                    if between is not None:
                        between(m)

            def heads_split():
                for c in range(4):
                    step(dve.tensor_copy(o_hi[:, c, :], o2[:, c, :]))
                    TT(o_lo[:, c, :], o2[:, c, :], o_hi[:, c, :].bitcast(F32), ALU.subtract).then_inc(o2_rdy, 1)

            def rope(x, to, cos, sin, n=P):
                step(TT(to, x, cos, ALU.mult))
                TT(x, B.take(dve)[0:n, :] if n != 32 else B.take(dve)[64:MLA_QK, :], sin, ALU.mult).then_inc(B.free, 1)
                dve.wait_ge(B.free, B.took)
                return TT(to, to, x, ALU.add)

            a = A2 + l * A_LAYER
            units_dve(dve, na_units(), P2)
            a += 4 + 8 + HEADS
            dve.wait_ge(A.free, a)
            heads_split()
            branch(0, a)
            a += DC + 4
            for m in range(8):
                dve.wait_ge(A.free, a + m + 1)
                rope(raw[:, m % 2, :], qk2[:, m, :], K("cos_d"), K("sin_d")).then_inc(roped, 1)
            a += 8
            U = len(pairs)

            def pair(i):
                k = l * U + i
                c = 2 * (k % 2)
                dve.wait_ge(pair_exp, 2 * (k + 1))
                step(dve.reciprocal(rinv[:, c:c + 2], rsum[:, c:c + 2]))
                step(TT(rinv[:, c + 1:c + 2], rinv[:, c + 1:c + 2], lam_neg[:, l:l + 1], ALU.mult))
                step(TS(P2[:, c + 1, :], P2[:, c + 1, :], rinv[:, c + 1:c + 2], None, ALU.mult))
                STT(out=P2[:, c, :], in0=P2[:, c, :], scalar=rinv[:, c:c + 1], in1=P2[:, c + 1, :], op0=ALU.mult, op1=ALU.add).then_inc(pair_norm, 1)

            for i in range(U):
                k = l * U + i
                for q in range(2):
                    c = 2 * (k % 2) + q
                    dve.wait_ge(pair_sc, 2 * k + q + 1)
                    step(dve.reduce_max(negmax[:, c:c + 1], ps[:, pair_banks[k % 2][q], :], AX_X, negate=True))
                    TS(negmax[:, c:c + 1], negmax[:, c:c + 1], DIFF_SCALE, None, ALU.mult).then_inc(pair_mx, 1)
                if i >= 1:
                    pair(i - 1)
            pair(U - 1)
            a += 4
            for h in range(4):
                sum_squares(dve, 1)
                inverse_var(dve, P, EPS)
                STT(out=o2[:, h, :], in0=o2[:, h, :], scalar=subg[:, l:l + 1], in1=rstd, op0=ALU.mult, op1=ALU.mult).then_inc(o_rdy, 1)
            a += MQC + KVC + 1
            dve.wait_ge(o_rdy, 4 * (l + 1))
            heads_split()

            def latent_norms(m):
                if m in (1, 3):
                    X, n, g, width = ((cq, MQC, V(f"mq_g{l}"), MQ_RANK), (ckv2, KVC, V(f"mkv_g{l}"), KV_RANK))[m // 2]
                    sum_squares(dve, n)
                    inverse_var(dve, width, EPS)
                    for c in range(n):
                        STT(out=X[:, c, :], in0=X[:, c, :], scalar=g[:, c:c + 1], in1=rstd, op0=ALU.mult, op1=ALU.mult).then_inc(lat_rdy, 1)
                elif m == 5:
                    x = krT[64:MLA_QK, :]
                    t = raw[64:MLA_QK, 0, :]
                    TT(t, B.take(dve)[64:MLA_QK, :], K("sin_m")[64:MLA_QK, :], ALU.mult).then_inc(B.free, 1)
                    step(TT(x, x, K("cos_m")[64:MLA_QK, :], ALU.mult))
                    dve.wait_ge(B.free, B.took)
                    TT(x, x, t, ALU.add).then_inc(kr_rdy, 1)
                    dve.wait_ge(kr_rdy, l + 1)
                    dve.tensor_copy(k96[64:MLA_QK, :, :], krT[64:MLA_QK, :].unsqueeze(1).broadcast_to((32, HEADS, SEQ))).then_inc(keys_rdy, 1)
            branch(1, a, latent_norms)
            a += DC
            for h in range(HEADS):
                dve.wait_ge(A.free, a + h + 1)
                rope(raw[0:MLA_QK, h % 2, :], q96[0:MLA_QK, h, :], K("cos_m")[0:MLA_QK, :], K("sin_m")[0:MLA_QK, :], MLA_QK).then_inc(roped, 1)
            a += HEADS + HEADS + NQB
            units_dve(dve, mla_units(), P2)
            a += HEADS
            dve.wait_ge(A.free, a)
            heads_split()
            branch(2, a)
            a += DC

            def residual(where):
                for m in range(DC):
                    STT(out=hT[:, m, :], in0=x_hi[:, m, :].bitcast(F32), scalar=DN_ALPHA, in1=B.take(dve), op0=ALU.mult, op1=ALU.add).then_inc(B.free, 1)
                    dve.wait_ge(B.free, B.took)
                    step(STT(out=hT[:, m, :], in0=x_lo[where][:, m, :].bitcast(F32), scalar=DN_ALPHA, in1=hT[:, m, :], op0=ALU.mult, op1=ALU.add))
                    if m >= 1:
                        add_up(dve, hT, m)
            residual(0)
            center(dve, hT)
            normed_split(dve, hT, 1, V(f"ln1_g{l}"), V(f"ln1_b{l}"))
            for m in range(FFC):
                dve.wait_ge(A.free, a + m + 1)
                TT(g_f[:, m, :], B.take(dve), g_f[:, m, :], ALU.mult).then_inc(B.free, 1)
                dve.wait_ge(B.free, B.took)
                step(dve.tensor_copy(g_hi[:, m, :], g_f[:, m, :]))
                TT(g_lo[:, m, :], g_f[:, m, :], g_hi[:, m, :].bitcast(F32), ALU.subtract).then_inc(hid_rdy, 1)
            a += FFC
            assert a == A2 + (l + 1) * A_LAYER, (a, A2, A_LAYER)
            residual(1)
            center(dve, hT)
            if l < LAYERS - 1:
                normed_split(dve, hT, 0, V(f"ln2_g{l}"), V(f"ln2_b{l}"))
            else:
                normed(dve, hT, hT, V(f"ln2_g{l}"), V(f"ln2_b{l}"))

        A2 = RC + 2 * RC + KVC + 4 + 1 + 1 + RC + 2 * DC + HEADS + HEADS + 2 * NQB + HEADS + 2 * NQB
        A_LAYER = 4 + 8 + HEADS + DC + 4 + 8 + 4 + DC + MQC + KVC + 1 + HEADS + HEADS + NQB + HEADS + DC + FFC
        cnt["rp"] = 0
        block = ctx.enter_context(nc.Block())

        @block.sync
        def _(sp):
            sp.dma_start(vec[:], vectors).then_inc(vec_in, 16)
            sp.dma_start(hT[:], xT).then_inc(x_in, 16)
            sp.dma_start(cs[:], consts).then_inc(const_in, 16)
            for s in range(n_slots1):
                if s >= SLOTS:
                    sp.wait_ge(w_used, s - SLOTS + 1)
                sp.dma_start(wring[:, s % SLOTS, :], wfirst[s]).then_inc(w_in[s % SLOTS], 16)

            for r in range(NQB):
                sp.wait_ge(A.free, A_ROWS + 2 * r + 2)
                sp.dma_start(u_rows[r * P:(r + 1) * P, :], u_tok[:, r, :]).then_inc(u_stored, 16)

            sp.wait_ge(moe_go, 1)
            sp.wait_ge(route_rdy, 1)

            def expert(i, j, b):
                e = sp.value_load(bexpI[0:1, bass.ds(b, 1)], min_val=0, max_val=EXPERTS - 1)
                first = isinstance(i, int) and i == 0
                if not first:
                    sp.wait_ge(up_full, 2 * i + j - 1)
                for k, w in enumerate((w1, w3)):
                    sp.dma_start(mring[:, j, k, :], w[bass.ds(e, 1)].rearrange("e p n -> (e p) n")).then_inc(up_in[j][k], 16)
                if not first:
                    sp.wait_ge(y1_full, 2 * i + j - 1)
                sp.dma_start(mring[:, j, 2, :], w2[bass.ds(e, 1)].rearrange("e p n -> (e p) n")).then_inc(down_in[j], 16)

            for j in range(2):
                expert(0, j, j)
            with sp.Fori(1, MOE_SURE // 2) as i:
                for j in range(2):
                    expert(i, j, 2 * i + j)
            sp.wait_ge(y1_full, MOE_SURE)
            over = sp.value_load(overI[0:1, 0:1], min_val=0, max_val=1)
            with sp.If(over):
                with sp.Fori(MOE_SURE // 2, MOE_BLOCKS // 2) as i:
                    for j in range(2):
                        expert(i, j, 2 * i + j)
                sp.wait_ge(y1_full, MOE_BLOCKS)
            for l in range(LAYERS):
                for s in range(n_slots2):
                    g = n_slots1 + l * n_slots2 + s
                    sp.wait_ge(w_used, g - SLOTS + 1)
                    sp.dma_start(wring[:, g % SLOTS, :], wlayers[l, s]).then_inc(w_in[g % SLOTS], 16)
            sp.wait_ge(x_rdy, DC + 2 * DC * LAYERS)
            sp.dma_start(out, hT[:]).then_inc(stored, 16)
            sp.wait_ge(stored, 16)

        @block.gpsimd
        def _(pool):
            pool.memset(xr[:, :, 0:CONV_W - 1], 0.0).then_inc(pad_rdy, 1)
            pool.memset(zeros[:], 0).then_inc(pool_step, 1)
            pool.wait_ge(pool_step, 1)
            pool.dma_start(table.rearrange("(p b) o -> p (b o)", p=P), zeros[:]).then_inc(table_clear, 16)
            pool.dma_start(browS, brow).then_inc(brow_in, 16)
            pool.wait_ge(tix_rdy, 1)
            pool.wait_ge(table_clear, 16)
            for k in range(2):
                for r in range(NQB):
                    c = k * NQB + r
                    pool.indirect_dma_start(table, bass.IndirectOffsetOnAxis(ap=tixI[:, c:c + 1], axis=0),
                                            tokI[:, r:r + 1], None).then_inc(table_set, 16)
            pool.wait_ge(table_set, 16 * 2 * NQB)
            pool.dma_start(ids[:], table.rearrange("(p b) o -> p (b o)", p=P)).then_inc(ids_in, 16)
            pool.wait_ge(ids_in, 16)
            pool.wait_ge(u_stored, 16 * NQB)
            def rows_in(blocks):
                for j in range(2):
                    pool.wait_ge(y_stored[j], 16 * (blocks // 2))
                for c in range(2 * NQB):
                    pool.indirect_dma_start(y_tok[:, c // NQB, c % NQB, :], None, y_rows[0:blocks * P, :],
                                            bass.IndirectOffsetOnAxis(ap=destI[:, c:c + 1], axis=0)).then_inc(rows_back, 16)

            def gather(b):
                if b >= 2:
                    pool.wait_ge(xt_full, b - 1)
                pool.indirect_dma_start(xs[:, b % 2, :], None, u_rows, bass.IndirectOffsetOnAxis(ap=ids[:, b:b + 1], axis=0)
                                        ).then_inc(xs_in[b % 2], 16)

            for b in range(MOE_SURE + 1):
                gather(b)
            pool.wait_ge(route_rdy, 1)
            over = pool.value_load(overI[0:1, 0:1], min_val=0, max_val=1)
            with pool.If(over):
                for b in range(MOE_SURE + 1, MOE_BLOCKS + 1):
                    gather(b)
                rows_in(MOE_BLOCKS)
            with pool.Else():
                rows_in(MOE_SURE)
            pool.wait_ge(h2_rdy, DC)
            pool.dma_start(lamS[:], lamv.partition_broadcast(P)).then_inc(lam_in, 16)
            for l in range(LAYERS):
                def table_in(h):
                    k = l * HEADS + h
                    if h >= 2:
                        pool.wait_ge(near_rdy, k - 1)
                    pool.dma_start(rp[:, h % 2, :], rpb[l, h]).then_inc(rp_in, 16)

                def near_bias(h):
                    k = l * HEADS + h
                    pool.wait_ge(rp_in, 16 * (k + 1))
                    if h + 1 < HEADS:
                        table_in(h + 1)
                    if h >= 2:
                        pool.wait_ge(mx_rdy, U_DSA + l * U_LAYER + 4 * (h - 1))
                    m = K("na_mask").rearrange("p (t c) -> p t c", c=16)
                    i0 = 0
                    for n, (lo, hi) in enumerate(NA_KEYS):
                        w = hi - lo
                        ins = pool.tensor_tensor(
                            near[:, h % 2, i0 * P:(i0 + w) * P].rearrange("p (t r c) -> p t r c", r=GRID_ROWS, c=16),
                            rp[:, h % 2, (lo - n + 1) * P:(hi - n + 1) * P].rearrange("p (t r c) -> p t r c", r=GRID_ROWS, c=16),
                            m[:, i0:i0 + w, :].unsqueeze(2).broadcast_to((P, w, GRID_ROWS, 16)), ALU.add)
                        i0 += w
                    ins.then_inc(near_rdy, 1)

                attention = two["na_gb"] // CHUNKS
                for slot in range(n_slots2):
                    if slot == 3:
                        pool.wait_ge(x_rdy, DC + 2 * DC * l)
                        table_in(0)
                    if slot in (4, 5):
                        near_bias(slot - 4)
                    if slot == attention + 2:
                        for h in range(2, HEADS):
                            near_bias(h)
                    weights_lo(pool, l, slot)

        @block.scalar
        def _(act):
            act.wait_ge(vec_in, 16)
            act.activation(csil, V("c"), ACT.Silu).then_inc(c_silu, 1)
            act.activation(s_abs, V("lam"), ACT.Abs).then_inc(sp_rdy, 1)
            act.wait_ge(x_in, 16)
            squares(act, hT, DC)
            root(act)
            for n in range(RC):
                act.activation(xr[:, n, CONV_W - 1:CONV_W - 1 + SEQ], A.take(act), ACT.Copy).then_inc(A.free, 1)
            def decay(n):
                act.wait_ge(gate_s, n + 1)
                act.activation(lru_t[:, n % 2, 2, :], lru_t[:, n % 2, 0, :], ACT.Tanh, scale=0.5).then_inc(gate_a, 1)
            for n in range(RC):
                if n >= 2:
                    act.wait_ge(lru_q, n - 1)
                act.activation(lru_t[:, n % 2, 0, :], A.take(act), ACT.Sigmoid, bias=V("b_rg_a")[:, n:n + 1]).then_inc(A.free, 1)
                act.activation(lru_t[:, n % 2, 1, :], A.take(act), ACT.Tanh, scale=0.5, bias=hbx[:, n:n + 1]).then_inc(A.free, 1)
                if n >= 1:
                    decay(n - 1)
            decay(RC - 1)
            for c in range(KVC):
                act.activation(ckv[:, c, :], A.take(act), ACT.Copy).then_inc(A.free, 1)
            for m in range(4):
                act.activation(qi[:, m, :], A.take(act), ACT.Copy).then_inc(A.free, 1)
            act.activation(ki[:], A.take(act), ACT.Copy).then_inc(A.free, 1)
            act.activation(wi_s, A.take(act)[:, 0:NQB * IDX_HEADS], ACT.Copy, scale=IDX_SCALE).then_inc(A.free, 1)
            act.wait_ge(A.free, A.took)
            def gelu(n):
                if n >= 2:
                    act.wait_ge(gh_rdy, n - 1)
                act.activation(lru_t[:, n % 2, 2, :], A.take(act), ACT.Gelu_apprx_tanh).then_inc(A.free, 1)
            for n in range(RC):
                if n < 2:
                    act.wait_ge(lru_q, RC)
                else:
                    act.wait_ge(h_rdy, n - 1)
                act.activation(lru_t[:, n % 2, 0, :], xr[:, n, 0:SEQ], ACT.Sqrt).then_inc(lru_sqrt, 1)
                if n >= 1:
                    gelu(n - 1)
            gelu(RC - 1)
            squares(act, ckv, KVC)
            root(act)
            act.wait_ge(gh_rdy, RC)
            for m in range(DC):
                act.activation(mixT[:, m, :], A.take(act), ACT.Sigmoid).then_inc(A.free, 1)
            for m in range(DC):
                act.activation(gb[:, m, :], A.take(act), ACT.Sigmoid).then_inc(A.free, 1)
            act.wait_ge(ckv_rdy, KVC)
            k = 0
            for qb in range(NQB):
                for h in range(IDX_HEADS):
                    act.wait_ge(ix_score, k + 1)
                    if k >= 2:
                        act.wait_ge(ix_acc, k - 1)
                    n = (qb + 1) * P
                    act.activation(rel[:, k % 2, 0:n], ps[:, 4 + k % 2, 0:n], ACT.Relu).then_inc(ix_rel, 1)
                    k += 1
            for h in range(HEADS):
                act.activation(qT[:, h, :], A.take(act), ACT.Copy).then_inc(A.free, 1)
            for h in range(HEADS):
                act.activation(kT[:, h, :], A.take(act), ACT.Copy).then_inc(A.free, 1)
            for s in range(NQB):
                for n in range(2):
                    act.activation(vS[:, s, n * SEQ:(n + 1) * SEQ], A.take(act), ACT.Copy).then_inc(A.free, 1)

            def att_out(u):
                act.activation(qT[:, u["h"], :], A.take(act), ACT.Copy).then_inc(A.free, 1)
            units_act(act, dsa, att_out)
            squares(act, hT, DC, lambda c: act.wait_ge(h1_rdy, c + 1))
            root(act)
            for r in range(NQB):
                for n in range(2):
                    act.activation(u_tok[:, r, n * SEQ:(n + 1) * SEQ], A.take(act), ACT.Copy).then_inc(A.free, 1)
            act.wait_ge(gl_diff, 1)
            act.activation(T("ge"), T("gd"), ACT.Exp).then_inc(gl_exp, 1)
            act.wait_ge(e_diff, 1)
            act.activation(T("ex"), T("d"), ACT.Exp).then_inc(e_exp, 1)

            def block_x(b, j):
                act.wait_ge(xt_full, b + 1)
                act.activation(xsT[:, j, 0:4, :], ps[:, 0, :].rearrange("p (c n) -> p c n", n=P), ACT.Copy)
                act.activation(xsT[:, j, 4:8, :], ps[:, 1, :].rearrange("p (c n) -> p c n", n=P), ACT.Copy).then_inc(xt_rdy, 1)

            def block_act(i, j):
                b = 2 * i + j
                act.wait_ge(gate_full, b + 1)
                if not (isinstance(b, int) and b == 0):
                    act.wait_ge(hid_done, b)
                act.activation(sil[:], ps[:, 2, :], ACT.Silu).then_inc(sil_done, 1)
                block_x(b + 1, 1 - j)
                act.wait_ge(ht_full, b + 1)
                act.activation(hidT[:], ps[:, 4, :].rearrange("p (c n) -> p c n", n=P), ACT.Copy).then_inc(ht_rdy, 1)
                act.wait_ge(y1_full, b + 1)
                if not (isinstance(i, int) and i == 0):
                    act.wait_ge(y_stored[j], 16 * i)
                act.activation(ysb[:, j, SEQ:], ps[:, 6, :], ACT.Copy).then_inc(y1_rdy, 1)
                act.wait_ge(y1_rdy, b + 1)
                act.wait_ge(y0_rdy, b + 1)
                act.dma_start(y_rows[bass.ds(b * P, P), :], ysb[:, j, :]).then_inc(y_stored[j], 16)

            block_x(0, 0)
            for j in range(2):
                block_act(0, j)
            with act.Fori(1, MOE_SURE // 2) as i:
                for j in range(2):
                    block_act(i, j)
            act.wait_ge(route_rdy, 1)
            over = act.value_load(overI[0:1, 0:1], min_val=0, max_val=1)
            with act.If(over):
                with act.Fori(MOE_SURE // 2, MOE_BLOCKS // 2) as i:
                    for j in range(2):
                        block_act(i, j)
            weights_hi(act, 0, 0)
            squares(act, hT, DC, lambda c: act.wait_ge(h2_rdy, c + 1))
            root(act)
            squares(act, uT, DC, lambda c: act.wait_ge(centered, c + 1))
            root(act)
            norm_hi(act, (V("ln_in_b"), 0))
            act.wait_ge(lam_sum, 1)
            act.activation(lam_two[:, 0:4], lam_prod[:, 0:4], ACT.Exp).then_inc(lam_exp, 1)
            act.wait_ge(x_rdy, DC)
            for l in range(LAYERS):
                layer_act(act, l)

        @block.vector
        def _(dve):
            dve.wait_ge(vec_in, 16)
            dve.tensor_scalar(hbx, V("b_rg_x"), 0.5, None, ALU.mult)
            after(dve, dve.tensor_scalar(hsp, V("lam"), -1.0, 0.0, ALU.mult, ALU.max), dve_step, "dstep")
            dve.wait_ge(sp_rdy, 1)
            step = lambda ins: after(dve, ins, dve_step, "dstep")
            step(dve.tensor_scalar(s_abs, s_abs, 87.0, None, ALU.min))
            step(dve.tensor_scalar(s_int, s_abs, 1.0 / math.log(2.0), None, ALU.mult))
            step(dve.tensor_copy(s_z, s_int))
            step(dve.scalar_tensor_tensor(out=s_abs, in0=s_z, scalar=-LN2_HI, in1=s_abs, op0=ALU.mult, op1=ALU.add))
            step(dve.scalar_tensor_tensor(out=s_abs, in0=s_z, scalar=LN2_HI - math.log(2.0), in1=s_abs, op0=ALU.mult, op1=ALU.add))
            step(dve.tensor_scalar(s_int, s_z, -float(2 ** 23), 127.0 * 2 ** 23, ALU.mult, ALU.add))
            step(dve.tensor_scalar(s_zz, s_abs, -1.0 / 10.0, 1.0, ALU.mult, ALU.add))
            for k in range(9, 0, -1):
                step(dve.scalar_tensor_tensor(out=s_zz, in0=s_abs, scalar=-1.0 / k, in1=s_zz, op0=ALU.mult, op1=ALU.mult))
                step(dve.tensor_scalar(s_zz, s_zz, 1.0, None, ALU.add))
            step(dve.tensor_tensor(s_abs, s_zz, s_int.bitcast(F32), ALU.mult))
            step(dve.tensor_scalar(s_z, s_abs, 2.0, None, ALU.add))
            step(dve.reciprocal(s_z, s_z))
            step(dve.tensor_tensor(s_z, s_z, s_abs, ALU.mult))
            step(dve.tensor_tensor(s_zz, s_z, s_z, ALU.mult))
            step(dve.tensor_scalar(s_abs, s_zz, 1.0 / 19.0, None, ALU.mult))
            for k in range(17, 1, -2):
                step(dve.scalar_tensor_tensor(out=s_abs, in0=s_abs, scalar=1.0 / k, in1=s_zz, op0=ALU.add, op1=ALU.mult))
            step(dve.scalar_tensor_tensor(out=s_abs, in0=s_abs, scalar=1.0, in1=s_z, op0=ALU.add, op1=ALU.mult))
            step(dve.scalar_tensor_tensor(out=hsp, in0=s_abs, scalar=2.0, in1=hsp, op0=ALU.mult, op1=ALU.add))
            after(dve, dve.tensor_scalar(hsp, hsp, LRU_C, None, ALU.mult), dve_step, "dstep")
            b = B.take(dve)
            dve.tensor_tensor(mod[:, 0:16], b[:, 0:16], V("b_mod")[:, 0:16], ALU.add).then_inc(B.free, 1)
            dve.wait_ge(B.free, B.took)
            dve.scalar_tensor_tensor(out=a1, in0=mod[:, 8:16], scalar=1.0, in1=V("norm1_g"), op0=ALU.add, op1=ALU.mult).then_inc(a_coef, 1)
            dve.wait_ge(a_coef, 1)
            sum_squares(dve, DC)
            inverse_var(dve, D, EPS)
            for c in range(DC):
                after(dve, dve.scalar_tensor_tensor(out=uT[:, c, :], in0=hT[:, c, :], scalar=a1[:, c:c + 1], in1=rstd,
                                                    op0=ALU.mult, op1=ALU.mult), dve_step, "dstep")
                dve.tensor_scalar(uT[:, c, :], uT[:, c, :], mod[:, c:c + 1], None, ALU.add).then_inc(u_rdy, 1)
            cw, cb = V("conv_w"), V("conv_b")
            dve.wait_ge(pad_rdy, 1)
            for n in range(RC):
                dve.wait_ge(A.free, n + 1)
                after(dve, dve.tensor_scalar(rnn[:, n, :], xr[:, n, 0:SEQ], cw[:, n:n + 1], cb[:, n:n + 1], ALU.mult, ALU.add), dve_step, "dstep")
                for w in range(1, CONV_W):
                    ins = dve.scalar_tensor_tensor(out=rnn[:, n, :], in0=xr[:, n, w:w + SEQ], scalar=cw[:, w * RC + n:w * RC + n + 1],
                                                   in1=rnn[:, n, :], op0=ALU.mult, op1=ALU.add)
                    if w < CONV_W - 1:
                        after(dve, ins, dve_step, "dstep")
                ins.then_inc(conv_rdy, 1)
            def input_scale(n):
                t = lru_t[:, n % 2]
                dve.wait_ge(gate_a, n + 1)
                after(dve, dve.tensor_scalar(t[:, 0, :], t[:, 2, :], 1.0, None, ALU.add), dve_step, "dstep")
                after(dve, dve.reciprocal(t[:, 0, :], t[:, 0, :]), dve_step, "dstep")
                dve.tensor_tensor(rnn[:, n, :], rnn[:, n, :], t[:, 0, :], ALU.mult)
                dve.tensor_scalar(xr[:, n, 0:SEQ], t[:, 2, :], 1e-30, None, ALU.max)
                after(dve, dve.tensor_scalar(t[:, 2, :], t[:, 2, :], -1.0, 1.0, ALU.mult, ALU.add), dve_step, "dstep")
                dve.tensor_tensor(lru_a[:, n, :], t[:, 2, :], t[:, 0, :], ALU.mult).then_inc(lru_q, 1)
            for n in range(RC):
                t = lru_t[:, n % 2]
                dve.wait_ge(A.free, RC + 2 * n + 2)
                dve.tensor_scalar(t[:, 0, :], t[:, 0, :], hsp[:, n:n + 1], None, ALU.mult).then_inc(gate_s, 1)
                after(dve, dve.tensor_scalar(t[:, 1, :], t[:, 1, :], 0.5, 0.5, ALU.mult, ALU.add), dve_step, "dstep")
                dve.tensor_tensor(rnn[:, n, :], rnn[:, n, :], t[:, 1, :], ALU.mult)
                if n >= 1:
                    input_scale(n - 1)
            input_scale(RC - 1)
            dve.wait_ge(lru_q, RC)
            a_free_gr = RC + 2 * RC + KVC + 4 + 1 + 1

            def gated_h(n):
                dve.wait_ge(A.free, a_free_gr + n + 1)
                dve.wait_ge(h_rdy, n + 1)
                dve.tensor_tensor(rnn[:, n, :], rnn[:, n, :], lru_t[:, n % 2, 2, :], ALU.mult).then_inc(gh_rdy, 1)
            for n in range(RC):
                dve.wait_ge(lru_sqrt, n + 1)
                r, q = lru_t[:, n % 2, 0, :], lru_t[:, n % 2, 1, :]
                after(dve, dve.reciprocal(q, r), dve_step, "dstep")
                after(dve, dve.tensor_tensor(q, q, xr[:, n, 0:SEQ], ALU.mult), dve_step, "dstep")
                after(dve, dve.tensor_tensor(q, q, r, ALU.add), dve_step, "dstep")
                after(dve, dve.tensor_tensor(xr[:, n, 0:SEQ], q, rnn[:, n, :], ALU.mult), dve_step, "dstep")
                dve.tensor_tensor_scan(rnn[:, n, :], lru_a[:, n, :], xr[:, n, 0:SEQ], 0.0, ALU.mult, ALU.add).then_inc(h_rdy, 1)
                if n >= 1:
                    gated_h(n - 1)
            gated_h(RC - 1)
            b = B.take(dve)
            dve.tensor_tensor(mod[:, 16:48], b[:, 0:32], V("b_mod")[:, 16:48], ALU.add).then_inc(B.free, 1)
            dve.wait_ge(B.free, B.took)
            dve.scalar_tensor_tensor(out=a2, in0=mod[:, 32:40], scalar=1.0, in1=V("norm2_g"), op0=ALU.add, op1=ALU.mult).then_inc(a_coef, 1)
            sum_squares(dve, KVC)
            inverse_var(dve, KV_RANK, EPS)
            for c in range(KVC):
                dve.scalar_tensor_tensor(out=ckv[:, c, :], in0=ckv[:, c, :], scalar=V("kv_g")[:, c:c + 1], in1=rstd,
                                         op0=ALU.mult, op1=ALU.mult).then_inc(ckv_rdy, 1)
            dve.wait_ge(table_clear, 16)
            k = 0
            for qb in range(NQB):
                o, n = qb * (qb + 1) // 2, (qb + 1) * P
                w = sel[:, o:o + qb + 1, :].rearrange("p j q -> p (j q)")
                for h in range(IDX_HEADS):
                    wt = wi_s[:, qb * IDX_HEADS + h:qb * IDX_HEADS + h + 1]
                    dve.wait_ge(ix_rel, k + 1)
                    if h == 0:
                        ins = dve.tensor_scalar(w, rel[:, k % 2, 0:n], wt, None, ALU.mult)
                    else:
                        ins = dve.scalar_tensor_tensor(out=w, in0=rel[:, k % 2, 0:n], scalar=wt, in1=w, op0=ALU.mult, op1=ALU.add)
                    ins.then_inc(ix_acc, 1)
                    k += 1
                    dve.wait_ge(ix_acc, k)
            c0 = K("causal")
            after(dve, dve.tensor_scalar(sel[:, 0, :], c0, MASKED / OUT_OF_SIGHT, None, ALU.mult), dve_step, "dstep")
            for qb in range(1, NQB):
                o = qb * (qb + 1) // 2
                ins = dve.tensor_tensor(sel[:, o + qb, :], sel[:, o + qb, :], c0, ALU.add)
            after(dve, ins, dve_step, "dstep")
            works = [sel[:, qb * (qb + 1) // 2:qb * (qb + 1) // 2 + qb + 1, :].rearrange("p j q -> p (j q)") for qb in range(NQB)]
            for r in range(TOPK // 8):
                for qb in range(1, NQB):
                    ins = dve.max(max8[:, 8 * (qb - 1):8 * qb], works[qb])
                after(dve, ins, dve_step, "dstep")
                for qb in range(1, NQB):
                    ins = dve.match_replace(works[qb], max8[:, 8 * (qb - 1):8 * qb], works[qb], TAKEN)
                after(dve, ins, dve_step, "dstep")
            for qb in range(1, NQB):
                ins = dve.tensor_scalar(works[qb], works[qb], TAKEN, -1.0, ALU.is_equal, ALU.add)
            after(dve, ins, dve_step, "dstep")
            for qb in range(1, NQB):
                ins = dve.tensor_scalar(works[qb], works[qb], -MASKED, None, ALU.mult)
            after(dve, ins, dve_step, "dstep")
            for m in range(DC):
                dve.wait_ge(A.free, a_free_gr + RC + m + 1)
                dve.tensor_tensor(mixT[:, m, :], B.take(dve), mixT[:, m, :], ALU.mult).then_inc(B.free, 1)
            units_dve(dve, dsa)
            for m in range(DC):
                dve.tensor_tensor(gb[:, m, :], B.take(dve), gb[:, m, :], ALU.mult).then_inc(B.free, 1)
                dve.wait_ge(B.free, B.took)
                dve.tensor_tensor(mixT[:, m, :], mixT[:, m, :], gb[:, m, :], ALU.add).then_inc(mix2_rdy, 1)
            for m in range(DC):
                dve.scalar_tensor_tensor(out=hT[:, m, :], in0=B.take(dve), scalar=mod[:, 16 + m:17 + m], in1=hT[:, m, :],
                                         op0=ALU.mult, op1=ALU.add).then_inc(h1_rdy, 1)
                B_also_free(dve)
            sum_squares(dve, DC)
            inverse_var(dve, D, EPS)
            for c in range(DC):
                after(dve, dve.scalar_tensor_tensor(out=uT[:, c, :], in0=hT[:, c, :], scalar=a2[:, c:c + 1], in1=rstd,
                                                    op0=ALU.mult, op1=ALU.mult), dve_step, "dstep")
                dve.tensor_scalar(uT[:, c, :], uT[:, c, :], mod[:, 24 + c:25 + c], None, ALU.add).then_inc(u_rdy, 1)
            step = lambda ins: after(dve, ins, dve_step, "dstep")
            TT, TS, STT = dve.tensor_tensor, dve.tensor_scalar, dve.scalar_tensor_tensor
            lg = T("lg").rearrange("p (s n) -> p s n", n=GROUPS + EXPERTS)
            dve.tensor_copy(T("lg"), B.take(dve)[:, 0:NQB * (GROUPS + EXPERTS)]).then_inc(B.free, 1)
            dve.wait_ge(B.free, B.took)
            gl, el = lg[:, :, 0:GROUPS], lg[:, :, GROUPS:]

            def four(t, n):
                return T(t)[:, 0:NQB * n].rearrange("p (s n) -> p s n", n=n)

            def best(values, n, m, pick):
                step(dve.reduce_max(T(m), values, AX_X))
                w = four("w", n)
                step(TT(w, values, T(m).unsqueeze(2).broadcast_to((P, NQB, n)), ALU.is_equal))
                step(TT(w, w, K("first")[:, 0:n].unsqueeze(1).broadcast_to((P, NQB, n)), ALU.mult))
                step(dve.reduce_max(T("wm"), w, AX_X))
                step(TT(four(pick, n), w, T("wm").unsqueeze(2).broadcast_to((P, NQB, n)), ALU.is_equal))

            best(gl, GROUPS, "gmax", "goh")
            TT(four("gd", GROUPS), gl, T("gmax").unsqueeze(2).broadcast_to((P, NQB, GROUPS)), ALU.subtract).then_inc(gl_diff, 1)
            prod = big[:, 0:NQB * EXPERTS].rearrange("p (s e g) -> p s e g", s=NQB, g=GROUPS)
            goh = four("goh", GROUPS)
            step(TT(prod, el.rearrange("p s (g e) -> p s e g", g=GROUPS), goh.unsqueeze(2).broadcast_to((P, NQB, PER_GROUP, GROUPS)), ALU.mult))
            es = four("es", PER_GROUP)
            step(dve.reduce_sum(es, prod, AX_X))
            best(es, PER_GROUP, "m1", "oh1")
            step(STT(out=es, in0=four("oh1", PER_GROUP), scalar=TAKEN, in1=es, op0=ALU.mult, op1=ALU.add))
            best(es, PER_GROUP, "m2", "oh2")
            TT(T("d"), T("m2"), T("m1"), ALU.subtract).then_inc(e_diff, 1)
            dve.wait_ge(gl_exp, 1)
            step(dve.reduce_sum(T("gw"), four("ge", GROUPS), AX_X))
            dve.wait_ge(e_exp, 1)
            step(TS(T("p1"), T("ex"), 1.0, None, ALU.add))
            step(TT(T("p1"), T("p1"), T("gw"), ALU.mult))
            step(dve.reciprocal(gate12[:, 0:NQB], T("p1")))
            TT(gate12[:, NQB:], gate12[:, 0:NQB], T("ex"), ALU.mult)
            for name, oh in (("M1", "oh1"), ("M2", "oh2")):
                ins = TT(T(name).rearrange("p (s g e) -> p s g e", s=NQB, e=PER_GROUP),
                         goh.unsqueeze(3).broadcast_to((P, NQB, GROUPS, PER_GROUP)),
                         four(oh, PER_GROUP).unsqueeze(2).broadcast_to((P, NQB, GROUPS, PER_GROUP)), ALU.mult)
            step(ins)
            TT(T("M"), T("M1"), T("M2"), ALU.add).then_inc(ohot, 1)
            b = B.take(dve)
            pos, cts = T("pos"), T("cts")
            dve.tensor_copy(pos, b[:, 0:NQB * EXPERTS])
            dve.tensor_copy(cts, b[:, NQB * EXPERTS:(NQB + 1) * EXPERTS]).then_inc(B.free, 1)
            dve.wait_ge(B.free, B.took)
            step(TS(T("nb"), cts, 0.0, None, ALU.is_gt))
            for lim in (P, 2 * P, 3 * P):
                step(STT(out=T("nb"), in0=cts, scalar=float(lim), in1=T("nb"), op0=ALU.is_gt, op1=ALU.add))
            step(dve.tensor_tensor_scan(T("cum"), ones[:, 0:EXPERTS], T("nb"), 0.0, ALU.mult, ALU.add))
            dve.tensor_tensor(T("st"), T("cum"), T("nb"), ALU.subtract)
            step(TS(T("bq"), pos, float(P), None, ALU.is_ge))
            for lim in (2 * P, 3 * P):
                step(STT(out=T("bq"), in0=pos, scalar=float(lim), in1=T("bq"), op0=ALU.is_ge, op1=ALU.add))
            step(STT(out=pos, in0=T("bq"), scalar=float(-P), in1=pos, op0=ALU.mult, op1=ALU.add))
            v3 = lambda t: T(t).rearrange("p (s e) -> p s e", e=EXPERTS)
            step(TT(v3("bq"), v3("bq"), T("st").unsqueeze(1).broadcast_to((P, NQB, EXPERTS)), ALU.add))
            TS(T("tix"), pos, float(MOE_BLOCKS + 1), None, ALU.mult)
            step(STT(out=pos, in0=T("bq"), scalar=float(P), in1=pos, op0=ALU.mult, op1=ALU.add))
            step(TT(T("tix"), T("tix"), T("bq"), ALU.add))
            for k, M in enumerate(("M1", "M2")):
                for t, to in (("tix", tixI), ("pos", destI)):
                    step(TT(T("bq"), T(M), T(t), ALU.mult))
                    step(dve.reduce_sum(T("ix"), v3("bq"), AX_X))
                    step(dve.tensor_copy(to[:, k * NQB:(k + 1) * NQB], T("ix")))
            dve.tensor_copy(tokI[:], K("token")).then_inc(tix_rdy, 1)
            bb = big[:].rearrange("p (b e) -> p b e", e=EXPERTS)
            step(TT(bb, T("cum").unsqueeze(1).broadcast_to((P, MOE_BLOCKS, EXPERTS)),
                    K("block").unsqueeze(2).broadcast_to((P, MOE_BLOCKS, EXPERTS)), ALU.is_le))
            step(dve.reduce_sum(T("be"), bb, AX_X))
            step(TS(T("be"), T("be"), float(EXPERTS - 1), None, ALU.min))
            step(TS(T("d")[:, 0:1], T("cum")[:, EXPERTS - 1:EXPERTS], float(MOE_SURE), None, ALU.is_gt))
            step(dve.tensor_copy(overI[:], T("d")[:, 0:1]))
            dve.tensor_copy(bexpI[:], T("be")).then_inc(route_rdy, 1)
            dve.wait_ge(route_rdy, 1)
            over = dve.value_load(overI[0:1, 0:1], min_val=0, max_val=1)

            def block_dve(i, j):
                b = 2 * i + j
                dve.wait_ge(up_full, b + 1)
                dve.wait_ge(sil_done, b + 1)
                dve.tensor_tensor(hid[:], ps[:, 3, :], sil[:], ALU.mult).then_inc(hid_done, 1)
                dve.wait_ge(y0_full, b + 1)
                if not (isinstance(i, int) and i == 0):
                    dve.wait_ge(y_stored[j], 16 * i)
                dve.tensor_copy(ysb[:, j, 0:SEQ], ps[:, 5, :]).then_inc(y0_rdy, 1)

            for j in range(2):
                block_dve(0, j)
            with dve.Fori(1, MOE_SURE // 2) as i:
                for j in range(2):
                    block_dve(i, j)
            with dve.If(over):
                with dve.Fori(MOE_SURE // 2, MOE_BLOCKS // 2) as i:
                    for j in range(2):
                        block_dve(i, j)
            for r in range(NQB):
                dve.wait_ge(rows_back, 16 * 2 * NQB)
                step(TS(y_tok[:, 0, r, :], y_tok[:, 0, r, :], gate12[:, r:r + 1], None, ALU.mult))
                STT(out=y_tok[:, 0, r, :], in0=y_tok[:, 1, r, :], scalar=gate12[:, NQB + r:NQB + r + 1], in1=y_tok[:, 0, r, :],
                    op0=ALU.mult, op1=ALU.add).then_inc(mixed_rows, 1)
            for c in range(DC):
                STT(out=hT[:, c, :], in0=B.take(dve), scalar=mod[:, 40 + c:41 + c], in1=hT[:, c, :],
                    op0=ALU.mult, op1=ALU.add).then_inc(h2_rdy, 1)
                B_also_free(dve)
            sum_squares(dve, DC)
            inverse_var(dve, D, EPS)
            for c in range(DC):
                STT(out=uT[:, c, :], in0=hT[:, c, :], scalar=V("final_g")[:, c:c + 1], in1=rstd, op0=ALU.mult, op1=ALU.mult).then_inc(b1_rdy, 1)
            dve.wait_ge(b1_rdy, DC)
            for c in range(1, DC):
                add_up(dve, uT, c)
            center(dve, uT)
            normed_split(dve, uT, 0, V("ln_in_g"), V("ln_in_b"), turn=True)
            dve.wait_ge(lam_in, 16)
            lv = lamS[:].rearrange("p (l a d) -> p l a d", l=LAYERS, a=4)
            step(TT(lv[:, :, 0:4:2, :], lv[:, :, 0:4:2, :], lv[:, :, 1:4:2, :], ALU.mult))
            dve.reduce_sum(lam_prod[:, 0:4].rearrange("p (l a) -> p l a", a=2), lv[:, :, 0:4:2, :], AX_X).then_inc(lam_sum, 1)
            dve.wait_ge(lam_exp, 1)
            for l in range(LAYERS):
                init = 0.8 - 0.6 * math.exp(-0.3 * l)
                step(TT(lam_neg[:, l:l + 1], lam_two[:, 2 * l + 1:2 * l + 2], lam_two[:, 2 * l:2 * l + 1], ALU.subtract))
                step(TS(lam_neg[:, l:l + 1], lam_neg[:, l:l + 1], -init, None, ALU.add))
                step(TS(subg[:, l:l + 1], V(f"subln{l}"), 1.0 - init, None, ALU.mult))
            for l in range(LAYERS):
                layer_dve(dve, l)

        @block.tensor
        def _(pe):
            def columns(c0, n):
                b = B.claim(pe)
                for m in range(n):
                    for k in range(DC):
                        ins = pe.matmul(b[:, m:m + 1], chunk(pe, c0 + m * DC + k), csil[:, k:k + 1], start=(k == 0), stop=(k == DC - 1))
                        if not (m == n - 1 and k == DC - 1):
                            said(ins)
                ins.then_inc(B.full, 1)
            pe.wait_ge(c_silu, 1)
            columns(one["mod_a"], 16)
            pe.wait_ge(const_in, 16)
            norm_pe(pe, DC)
            for n in range(RC):
                tile(pe, A.claim(pe), one["xr"] + n * DC, uT, DC, wait=(lambda k: pe.wait_ge(u_rdy, k + 1)) if n == 0 else None).then_inc(A.full, 1)
            for n in range(RC):
                pe.wait_ge(conv_rdy, n + 1)
                for g in range(2):
                    b = A.claim(pe)
                    w = chunk(pe, one["rg"] + 2 * n + g)
                    said(pe.matmul(b[:, 0:SEQ // 2], w, rnn[:, n, 0:SEQ // 2], start=True, stop=True))
                    pe.matmul(b[:, SEQ // 2:], w, rnn[:, n, SEQ // 2:], start=True, stop=True).then_inc(A.full, 1)
            for m in range(KVC):
                tile(pe, A.claim(pe), one["ckv"] + m * DC, uT, DC).then_inc(A.full, 1)
            for m in range(4):
                tile(pe, A.claim(pe), one["qi"] + m * DC, uT, DC).then_inc(A.full, 1)
            tile(pe, A.claim(pe), one["ki"], uT, DC).then_inc(A.full, 1)
            b = A.claim(pe)
            w = chunk(pe, one["wi"])
            for s in range(NQB):
                for k in range(DC):
                    ins = pe.matmul(b[:, s * IDX_HEADS:(s + 1) * IDX_HEADS], uT[:, k, s * P:(s + 1) * P],
                                    w[:, k * IDX_HEADS:(k + 1) * IDX_HEADS], start=(k == 0), stop=(k == DC - 1))
                    if s < NQB - 1:
                        said(ins)
            ins.then_inc(A.full, 1)
            for m in range(RC):
                tile(pe, A.claim(pe), one["gr"] + m * DC, uT, DC).then_inc(A.full, 1)
            columns(one["mod_b"], 32)
            norm_pe(pe, KVC)
            for m in range(2 * DC):
                tile(pe, A.claim(pe), one["mg"] + m * DC, uT, DC).then_inc(A.full, 1)
            k = 0
            for qb in range(NQB):
                for h in range(IDX_HEADS):
                    r = 64 * (h % 2)
                    if k >= 2:
                        pe.wait_ge(ix_rel, k - 1)
                    pe.matmul(ps[:, 4 + k % 2, 0:(qb + 1) * P], qi[r:r + 64, h // 2, qb * P:(qb + 1) * P],
                              ki[r:r + 64, 0:(qb + 1) * P], start=True, stop=True).then_inc(ix_score, 1)
                    k += 1
            for m in range(HEADS):
                tile(pe, A.claim(pe), one["q"] + m * DC, uT, DC).then_inc(A.full, 1)
            pe.wait_ge(gh_rdy, RC)
            for m in range(DC):
                tile(pe, B.claim(pe), one["rnn_out"] + m * RC, rnn, RC).then_inc(B.full, 1)
            pe.wait_ge(ckv_rdy, KVC)
            for m in range(HEADS):
                tile(pe, A.claim(pe), one["uk"] + m * KVC, ckv, KVC).then_inc(A.full, 1)
            for s in range(NQB):
                for n in range(2):
                    b = A.claim(pe)
                    for k in range(KVC):
                        w = chunk(pe, one["uv"] + (2 * k + n) * 4, 4)
                        ins = pe.matmul(b, ckv[:, k, s * P:(s + 1) * P], w, start=(k == 0), stop=(k == KVC - 1))
                        if k < KVC - 1:
                            said(ins)
                    ins.then_inc(A.full, 1)
            units_pe(pe, dsa, lambda i: (pe.wait_ge(ix_rel, NQB * IDX_HEADS), pe.wait_ge(A.free, A.made)) if i == 0 else None)
            pe.wait_ge(A.free, A.made)
            for m in range(DC):
                tile(pe, B.claim(pe), one["att_out"] + m * DC, qT, DC).then_inc(B.full, 1)
            pe.wait_ge(mix2_rdy, DC)
            for m in range(DC):
                tile(pe, B.claim(pe), one["out"] + m * DC, mixT, DC).then_inc(B.full, 1)
            norm_pe(pe, DC)
            pe.wait_ge(u_rdy, 2 * DC)
            assert A.made == A_ROWS
            for r in range(NQB):
                for n in range(2):
                    b = A.claim(pe)
                    for c in range(4):
                        ins = pe.transpose(b[:, c * P:(c + 1) * P], uT[:, 4 * n + c, r * P:(r + 1) * P], ident)
                    ins.then_inc(A.full, 1)
            b = B.claim(pe)
            w = chunk(pe, one["router"], 3)
            N = GROUPS + EXPERTS
            pe.wait_ge(brow_in, 16)
            for r in range(NQB):
                for k in range(DC):
                    said(pe.matmul(b[:, r * N:(r + 1) * N], uT[:, k, r * P:(r + 1) * P], w[:, k * N:(k + 1) * N], start=(k == 0), stop=False))
                ins = pe.matmul(b[:, r * N:(r + 1) * N], ones[0:1, :], browS, start=False, stop=True)
            ins.then_inc(B.full, 1)
            pe.wait_ge(ohot, 1)
            b = B.claim(pe)
            M = T("M").rearrange("p (s e) -> p s e", e=EXPERTS)
            for r in range(NQB):
                pe.matmul(b[:, r * EXPERTS:(r + 1) * EXPERTS], K("tri"), M[:, r, :], start=True, stop=(r == 0))
                for q in range(r):
                    pe.matmul(b[:, r * EXPERTS:(r + 1) * EXPERTS], ones, M[:, q, :], start=False, stop=(q == r - 1))
            for q in range(NQB):
                ins = pe.matmul(b[:, NQB * EXPERTS:(NQB + 1) * EXPERTS], ones, M[:, q, :], start=(q == 0), stop=(q == NQB - 1))
            ins.then_inc(B.full, 1)
            pe.wait_ge(A.free, A.made)
            pe.wait_ge(B.free, B.made)
            pe.transpose(ps[:, 7, 0:P], ident, ident).then_inc(moe_go, 1)

            def block_x(i, b, j):
                pe.wait_ge(xs_in[j], 16 * i + 16)
                if not (isinstance(b, int) and b == 0):
                    pe.wait_ge(xt_rdy, b)
                for c in range(DC):
                    ins = pe.transpose(ps[:, c // 4, (c % 4) * P:(c % 4 + 1) * P], xs[:, j, c * P:(c + 1) * P], ident)
                ins.then_inc(xt_full, 1)

            def block_pe(i, j):
                b = 2 * i + j
                pe.wait_ge(xt_rdy, b + 1)
                pe.wait_ge(up_in[j][0], 16 * i + 16)
                for k in range(DC):
                    ins = pe.matmul(ps[:, 2, :], xsT[:, j, k, :], mring[:, j, 0, k * SEQ:(k + 1) * SEQ], start=(k == 0), stop=(k == DC - 1))
                ins.then_inc(gate_full, 1)
                pe.wait_ge(up_in[j][1], 16 * i + 16)
                for k in range(DC):
                    ins = pe.matmul(ps[:, 3, :], xsT[:, j, k, :], mring[:, j, 1, k * SEQ:(k + 1) * SEQ], start=(k == 0), stop=(k == DC - 1))
                ins.then_inc(up_full, 1)
                block_x(i + j, b + 1, 1 - j)
                pe.wait_ge(hid_done, b + 1)
                for c in range(4):
                    ins = pe.transpose(ps[:, 4, c * P:(c + 1) * P], hid[:, c * P:(c + 1) * P], ident)
                ins.then_inc(ht_full, 1)
                pe.wait_ge(ht_rdy, b + 1)
                pe.wait_ge(down_in[j], 16 * i + 16)
                for n, full in enumerate((y0_full, y1_full)):
                    if not (isinstance(b, int) and b == 0):
                        pe.wait_ge((y0_rdy, y1_rdy)[n], b)
                    for k in range(4):
                        ins = pe.matmul(ps[:, 5 + n, :], hidT[:, k, :], mring[:, j, 2, k * D + n * SEQ:k * D + (n + 1) * SEQ],
                                        start=(k == 0), stop=(k == 3))
                    ins.then_inc(full, 1)

            block_x(0, 0, 0)
            for j in range(2):
                block_pe(0, j)
            with pe.Fori(1, MOE_SURE // 2) as i:
                for j in range(2):
                    block_pe(i, j)
            pe.wait_ge(route_rdy, 1)
            over = pe.value_load(overI[0:1, 0:1], min_val=0, max_val=1)
            with pe.If(over):
                with pe.Fori(MOE_SURE // 2, MOE_BLOCKS // 2) as i:
                    for j in range(2):
                        block_pe(i, j)
            pe.wait_ge(mixed_rows, NQB)
            for c in range(DC):
                b = B.claim(pe)
                for r in range(NQB):
                    ins = pe.transpose(b[:, r * P:(r + 1) * P], y_tok[:, 0, r, c * P:(c + 1) * P], ident)
                ins.then_inc(B.full, 1)
            norm_pe(pe, DC)
            mean_pe(pe)
            norm_pe(pe, DC)
            for l in range(LAYERS):
                layer_pe(pe, l)


def _columns(v):
    return v.reshape(-1, P).T


def _chunks(w, nk=None):
    k, m = w.shape
    return w.reshape(k // P, P, m // P, P).transpose(2, 0, 1, 3).reshape(-1, P, P)


def _blocks(w):
    k, m = w.shape
    return w.reshape(k // P, P, m // 512, 4, P).transpose(0, 2, 3, 1, 4).reshape(-1, P, P)


def _wide(w, width=P):
    out = np.zeros((w.shape[0], width), w.dtype)
    out[:, :w.shape[1]] = w
    return out


def _pack(w, n):
    k, m = w.shape
    a = _wide(w.reshape(k // P, P, m).transpose(1, 0, 2).reshape(P, -1), n * P)
    return a.reshape(P, n, P).transpose(1, 0, 2)


def _stream(found, size, parts):
    s = np.zeros((size, P, P), np.float32)
    for name, chunks in parts.items():
        s[found[name]:found[name] + len(chunks)] = chunks
    return np.ascontiguousarray(s.reshape(-1, CHUNKS, P, P).transpose(0, 2, 1, 3)).reshape(-1, P, CHUNKS * P)


def _constants():
    cst, n = const_plan()
    t = np.zeros((P, n), np.float32)

    def put(name, v):
        a, b = cst[name]
        t[:v.shape[0], a:b] = v.reshape(v.shape[0], -1)

    p = np.arange(P)
    put("ident", np.eye(P))
    put("ones", np.ones((P, P)))
    put("tri", p[:, None] < p[None, :])
    pos = np.arange(SEQ).reshape(GRID_ROWS, NA_TILES, 16).transpose(1, 0, 2).reshape(-1).astype(np.float32)

    def rotary(base, half, group, rows):
        cos, sin, perm = np.ones((rows, SEQ)), np.zeros((rows, SEQ)), np.zeros((rows, P))
        inv = np.exp(np.float32(-math.log(ROPE_THETA)) * np.arange(half, dtype=np.float32) / np.float32(half)).astype(np.float32)
        ang = (pos[:, None] * inv[None, :]).astype(np.float32)
        for g in range(base, rows, group):
            for j in range(half):
                cos[g + j] = cos[g + half + j] = np.cos(ang[:, j])
                sin[g + j] = sin[g + half + j] = np.sin(ang[:, j])
                perm[g + half + j, g + j] = -1.0
                perm[g + j, g + half + j] = 1.0
        return cos, sin, perm

    c, s, m = rotary(0, 8, 64, P)
    put("cos_d", c), put("sin_d", s), put("perm_d", m)
    c, s, m = rotary(64, 16, 64, MLA_QK)
    put("cos_m", c), put("sin_m", s), put("perm_m", m)
    put("dist", p[:, None] - np.arange(7 * P)[None, :] + 3 * P)
    put("causal", np.where(p[None, :] <= p[:, None], 0.0, OUT_OF_SIGHT))
    mask = np.zeros((P, 10, 16))
    i = 0
    for n_, (lo, hi) in enumerate(NA_KEYS):
        for j in range(lo, hi):
            qc = n_ * 16 + p % 16
            kc = j * 16 + np.arange(16)
            w = np.clip(qc - 8, 0, GRID_W - 16)
            mask[:, i] = np.where((kc[None] >= w[:, None]) & (kc[None] < w[:, None] + 16), 0.0, MASKED)
            i += 1
    put("na_mask", mask)
    put("block", np.broadcast_to(np.arange(MOE_BLOCKS), (P, MOE_BLOCKS)))
    put("first", np.broadcast_to(PER_GROUP - np.arange(PER_GROUP), (P, PER_GROUP)))
    put("token", np.arange(SEQ).reshape(NQB, P).T)
    return t


def _arrays(i):
    one, end1, two, size2 = stream_plan()
    w_in = i["w_in"][0]
    cut = np.cumsum([0, D_RNN, D_RNN, D, KV_RANK, 512, IDX_DIM, IDX_HEADS, 2 * D])
    part = dict(zip(["xr", "gr", "q", "ckv", "qi", "ki", "wi", "mg"], [w_in[:, a:b] for a, b in zip(cut[:-1], cut[1:])]))
    parts = {n: _chunks(part[n]) for n in ("xr", "gr", "q", "ckv", "qi", "mg")}
    parts["mod_a"] = _chunks(i["w_mod"][0][:, :2 * D])
    parts["mod_b"] = _chunks(i["w_mod"][0][:, 2 * D:])
    parts["rg"] = np.stack([i["w_rg_a"][0], i["w_rg_x"][0]], 1).reshape(-1, P, P)
    parts["ki"] = _chunks(np.concatenate([part["ki"], part["ki"]], 1))
    parts["wi"] = _pack(part["wi"], 1)
    parts["rnn_out"] = _chunks(i["w_rnn_out"][0])
    parts["uk"] = _chunks(i["w_uk"][0].reshape(KV_RANK, -1))
    parts["uv"] = _blocks(i["w_uv"][0].reshape(KV_RANK, -1))
    parts["att_out"] = _chunks(i["w_att_out"][0])
    parts["out"] = _chunks(i["w_out"][0])
    parts["router"] = _pack(np.concatenate([i["w_group"][0], i["w_expert"][0]], 1), 3)
    first = _stream(one, end1, parts)

    layers = []
    for l in range(LAYERS):
        w = i["w_in_2"][l]
        cut = np.cumsum([0, 1024, 512, 1024, 512, MQ_RANK, 256, 32, 3 * D])
        part = dict(zip(["na_qk", "na_v", "df_qk", "df_v", "cq", "mckv", "kr", "gate"], [w[:, a:b] for a, b in zip(cut[:-1], cut[1:])]))
        parts = {n: _chunks(part[n]) for n in ("na_qk", "df_qk", "cq", "mckv")}
        parts["na_v"], parts["df_v"] = _blocks(part["na_v"]), _blocks(part["df_v"])
        parts["kr"] = _chunks(_wide(np.concatenate([part["mckv"][:, 192:], part["kr"]], 1)))
        for b, name in enumerate(("na_gb", "df_gb", "ml_gb")):
            g = _chunks(part["gate"][:, b * D:(b + 1) * D]).reshape(DC, DC, P, P)
            o = _chunks(i["w_branch_2"][l, b]).reshape(DC, 4, P, P)
            parts[name] = np.concatenate([g, o], 1).reshape(-1, P, P)
        qb = i["w_mla_qb_2"][l].reshape(MQ_RANK, HEADS, MLA_QK)
        parts["qb"] = np.concatenate([_chunks(_wide(qb[:, h])) for h in range(HEADS)])
        kvb = i["w_mla_kvb_2"][l].reshape(256, HEADS, 2, 64)
        parts["kvb_k"] = _chunks(kvb[:, :, 0].reshape(256, 512))
        parts["kvb_v"] = _blocks(kvb[:, :, 1].reshape(256, 512))
        parts["out2"] = _chunks(i["w_out_2"][l])
        gu = i["w_ffn_in_2"][l].reshape(D, 2, FFC, P).transpose(0, 2, 1, 3).reshape(D, 2 * D_FF)
        parts["ffn_in"] = _chunks(gu)
        parts["ffn_out"] = _chunks(i["w_ffn_out_2"][l])
        layers.append(_stream(two, size2, parts))

    vcol, n = vector_plan()
    names = {"b_mod": "b_mod", "norm1_g": "norm1_g", "conv_w": "conv_w", "conv_b": "conv_b", "b_rg_a": "b_rg_a",
             "b_rg_x": "b_rg_x", "lam": "lru_lambda", "kv_g": "kv_norm_g", "norm2_g": "norm2_g", "final_g": "final_g",
             "c": "c", "ln_in_g": "ln_in_g_2", "ln_in_b": "ln_in_b_2"}
    per = {"b_gate": "b_gate_2", "subln": "diff_subln_g_2", "mq_g": "mla_q_norm_g_2", "mkv_g": "mla_kv_norm_g_2",
           "ln1_g": "ln1_g_2", "ln1_b": "ln1_b_2", "ln2_g": "ln2_g_2", "ln2_b": "ln2_b_2"}
    vectors = np.zeros((P, n), np.float32)
    for name, (a, b) in vcol.items():
        v = i[names[name]] if name in names else i[per[name[:-1]]][int(name[-1])]
        vectors[:, a:b] = _columns(np.asarray(v).reshape(-1))

    rpb = np.zeros((LAYERS, HEADS, P, 3, GRID_ROWS, 16), np.float32)
    table = np.zeros((LAYERS, HEADS, 15, 31 + 64), np.float32)
    table[:, :, :, 32:63] = i["na_rpb_2"]
    for qr in range(GRID_ROWS):
        for qc in range(16):
            for dj in range(3):
                b = 32 + 16 * (dj - 1) - qc + 15
                rpb[:, :, qr * 16 + qc, dj] = table[:, :, 7 - qr:15 - qr, b:b + 16]

    def moe(w, cols):
        e, k, m = w.shape
        return np.ascontiguousarray(w.reshape(e, k // P, P, m).transpose(0, 2, 1, 3)).reshape(e, P, -1)

    return {
        "xT": np.ascontiguousarray(i["x"][0].T.reshape(DC, P, SEQ).transpose(1, 0, 2)),
        "wfirst": first, "wlayers": np.stack(layers), "consts": _constants(), "vectors": vectors,
        "brow": np.concatenate([i["b_group"][0], i["b_expert"][0]])[None, :],
        "lamv": i["diff_lambda_2"].reshape(1, -1),
        "rpb": rpb.reshape(LAYERS, HEADS, P, -1),
        "w1": moe(i["moe_w1"][0], 512), "w3": moe(i["moe_w3"][0], 512), "w2": moe(i["moe_w2"][0], 1024),
    }


def kernel(**inputs):
    import concourse.bacc as bacc
    from concourse.bass_utils import run_bass_kernel_spmd as run

    nc = bacc.Bacc("TRN2", target_bir_lowering=False, num_devices=1)
    arrays = _arrays(inputs)
    args = {name: nc.dram_tensor(name, a.shape, mybir.dt.from_np(a.dtype), kind="ExternalInput").ap() for name, a in arrays.items()}
    args["out"] = nc.dram_tensor("out", (P, DC, SEQ), F32, kind="ExternalOutput").ap()
    build(nc, **args)
    got = run(nc, [arrays], core_ids=[0]).results[0]["out"]
    got = got.transpose(2, 1, 0).reshape(NA_TILES, GRID_ROWS, 16, D).transpose(1, 0, 2, 3)
    return np.ascontiguousarray(got).reshape(1, SEQ, D)
```

```python
from contextlib import ExitStack
import math

import numpy as np

import concourse.bass as bass
from concourse import mybir

P = 128
SEQ = 512
D = 1024
DC = D // P
NQB = SEQ // P
D_RNN = 1280
RC = D_RNN // P
CONV_W = 4
LRU_C = 8.0
HEADS = 8
KV_RANK = 256
KVC = KV_RANK // P
IDX_HEADS = 8
IDX_DIM = 64
IDX_SCALE = IDX_DIM ** -0.5 * IDX_HEADS ** -0.5
TOPK = min(256, SEQ // 4)
DSA_SCALE = P ** -0.5
GROUPS = 4
PER_GROUP = 8
EXPERTS = GROUPS * PER_GROUP
D_EXPERT = 512
EPS = 1e-6
LN_EPS = 1e-5
MOE_BLOCKS = 40
MOE_SURE = 32

LAYERS = 2
D_FF = 2816
FFC = D_FF // P
GRID_W = 64
GRID_ROWS = SEQ // GRID_W
NA_TILES = 4
DN_ALPHA = (2 * LAYERS) ** 0.25
ROPE_THETA = 500000.0
MQ_RANK = 384
MQC = MQ_RANK // P
MLA_QK = 96
NA_SCALE = 64 ** -0.5
DIFF_SCALE = 64 ** -0.5
MLA_SCALE = MLA_QK ** -0.5
NA_KEYS = [(0, 2), (0, 3), (1, 4), (2, 4)]

CHUNKS = 16
SLOTS = 5
HI_SLOTS = 3
MOD_FIRST = 2 * D // P
MOD_SLOTS = 4 * D // P // 2
MG_SLOTS = 2 * D * D // (CHUNKS * P * P)

OUT_OF_SIGHT = -3.3e38
TAKEN = -3.0e38
LN2_HI = 0.693145751953125
HALF_INVERSE = 0x7E7127EA
MASKED = -1.0e30

ALU = mybir.AluOpType
ACT = mybir.ActivationFunctionType
AX_X = mybir.AxisListType.X
F32 = mybir.dt.float32
I32 = mybir.dt.int32
F32R = mybir.dt.float32r


def stream_plan():
    gates = [(f"{name}{m}", n * CHUNKS) for m in range(MG_SLOTS) for name, n in (("mg", 1), ("mod", MOD_SLOTS // MG_SLOTS))]
    first = [("xr", RC * DC), ("rg", 2 * RC), ("ckv", KVC * DC), ("qi", 4 * DC), ("ki", DC),
             ("wi", 1), ("gr", RC * DC)] + gates + [("q", HEADS * DC),
             ("rnn_out", DC * RC), ("uk", HEADS * KVC), ("uv", 4 * 2 * KVC), ("att_out", DC * DC),
             ("out", DC * DC), ("router", 3)]
    layer = [("na_v", 4 * DC), ("na_qk", 8 * DC), ("na_gb", DC * (DC + 4)),
             ("df_v", 4 * DC), ("df_qk", 8 * DC), ("cq", MQC * DC), ("mckv", KVC * DC), ("kr", DC),
             ("df_gb", DC * (DC + 4)), ("qb", HEADS * MQC), ("kvb_k", 4 * KVC),
             ("kvb_v", 4 * KVC), ("ml_gb", DC * (DC + 4)),
             ("out2", DC * DC), ("ffn_in", 2 * FFC * DC), ("ffn_out", DC * FFC)]
    blocks = {"uv": 16, "na_v": 16, "df_v": 16, "qb": 16, "kvb_v": 8, "ml_gb": 16, "rg": 16, "ckv": 16, "gr": 16, "mg0": 16,
              "rnn_out": 16, "att_out": 16, "router": 16}

    def place(parts, at):
        found = {}
        for name, n in parts:
            if name in blocks:
                at += -at % blocks[name]
            found[name] = at
            at += n
        return found, at + -at % CHUNKS

    one, end = place(first, 0)
    two, size = place(layer, 0)
    return one, end, two, size


def const_plan():
    widths = [("ident", P), ("tri", P), ("ones", P), ("cos_d", SEQ), ("sin_d", SEQ), ("cos_m", SEQ), ("sin_m", SEQ),
              ("perm_d", P), ("perm_m", P), ("dist", 7 * P), ("na_mask", 160), ("causal", P),
              ("block", MOE_BLOCKS), ("first", PER_GROUP), ("token", NQB)]
    at, found = 0, {}
    for name, n in widths:
        found[name] = (at, at + n)
        at += n
    return found, at


def vector_plan():
    widths = [("b_mod", 48), ("norm1_g", 8), ("conv_w", 4 * RC), ("conv_b", RC), ("b_rg_a", RC), ("b_rg_x", RC),
              ("lam", RC), ("kv_g", KVC), ("norm2_g", 8), ("final_g", 8), ("ln_in_g", 8), ("ln_in_b", 8)]
    for l in range(LAYERS):
        widths += [(f"b_gate{l}", 24), (f"subln{l}", 1), (f"mq_g{l}", MQC), (f"mkv_g{l}", KVC), (f"ln1_g{l}", 8),
                   (f"ln1_b{l}", 8), (f"ln2_g{l}", 8), (f"ln2_b{l}", 8)]
    at, found = 0, {}
    for name, n in widths:
        found[name] = (at, at + n)
        at += n
    return found, at


class Bank:

    def __init__(self, ps, banks, full, free):
        self.ps, self.banks, self.full, self.free = ps, banks, full, free
        self.made, self.took = 0, 0

    def claim(self, pe):
        if self.made >= 2:
            pe.wait_ge(self.free, self.made - 1)
        b = self.banks[self.made % 2]
        self.made += 1
        return self.ps[:, b, :]

    def take(self, eng):
        b = self.banks[self.took % 2]
        self.took += 1
        eng.wait_ge(self.full, self.took)
        return self.ps[:, b, :]


def build(nc, xT, crow, wmod, wfirst, wlayers, consts, vectors, brow, lamv, rpb, w1, w3, w2, out):
    one, end1, two, size2 = stream_plan()
    cst, NCONST = const_plan()
    vcol, NVEC = vector_plan()
    n_slots1, n_slots2 = end1 // CHUNKS, size2 // CHUNKS
    unsplit = [("rg", "ckv"), ("uk", "att_out"), ("rnn_out", "uk")] + [(f"mod{m}", f"mg{m + 1}") for m in range(MG_SLOTS - 1)] + [(f"mod{MG_SLOTS - 1}", "q")]
    plain1 = {s for a, b in unsplit for s in range(one[a] // CHUNKS, one[b] // CHUNKS)} | {one["router"] // CHUNKS}
    plain2 = set(range(two["qb"] // CHUNKS, two["ml_gb"] // CHUNKS))
    split = [s for s in range(n_slots1) if s not in plain1]
    split += [n_slots1 + l * n_slots2 + s for l in range(LAYERS) for s in range(n_slots2) if s not in plain2]
    order = {slot: q for q, slot in enumerate(split)}

    def split_no(slot):
        return order.get(slot)

    with ExitStack() as ctx:

        def at(name, kb, shape, dt=F32):
            return nc.alloc_sbuf_tensor_at(name, shape, dt, offset=(nc.sbuf_base + 31) // 32 * 32 + int(kb * 1024))

        def sem(name):
            return ctx.enter_context(nc.semaphore(name))

        hT = at("hT", 0, [P, DC, SEQ])
        uT = at("uT", 16, [P, DC, SEQ])
        wring = at("wring", 32, [P, SLOTS, CHUNKS * P])
        w_hi = at("w_hi", 72, [P, HI_SLOTS, CHUNKS * P], F32R)
        w_lo = at("w_lo", 32, [P, SLOTS, CHUNKS * P], F32R)
        cs = at("cs", 189, [P, NCONST])
        vec = at("vec", 204.5, [P, NVEC])
        small = at("small", 206, [P, 384])

        def K(name, n=P):
            a, b = cst[name]
            return cs[0:n, a:b]

        def V(name):
            a, b = vcol[name]
            return vec[:, a:b]

        ident, ones = K("ident"), K("ones")
        late = cst["cos_d"][0], cst["sin_d"][1]
        csil = cs[:, late[0]:late[1]]
        wmodS = at("wmodS", 96, [P, MOD_FIRST, D])
        used = [0]

        def sm(n):
            a = used[0]
            used[0] += n
            assert used[0] <= 384
            return small[:, a:a + n]

        mod = sm(48)
        a1, a2, s_abs, s_z, s_zz, hsp, hbx = sm(8), sm(8), sm(RC), sm(RC), sm(RC), sm(RC), sm(RC)
        wi_s = sm(NQB * IDX_HEADS)
        n_var, n_rec, n_inv = sm(NQB), sm(NQB), sm(NQB)
        negmax, rsum, rinv = sm(8), sm(8), sm(8)
        lam_prod, lam_two, lam_neg = sm(64), sm(4), sm(2)
        subg, rinv2 = sm(2), sm(8)
        max8 = sm(24)
        s_int = sm(RC).bitcast(I32)
        gate12 = sm(2 * NQB)
        browS = sm(GROUPS + EXPERTS)[0:1, :]
        zeros = at("zeros", 116.5, [P, MOE_BLOCKS + 1], I32)
        xr = at("xr", 96, [P, RC, SEQ + CONV_W])
        rnn = at("rnn", 117, [P, RC, SEQ])
        lru_a = at("lru_a", 137, [P, RC, SEQ])
        lru_t = at("lru_t", 157, [P, 2, 3, SEQ])
        qi = at("qi", 169, [P, 4, SEQ])
        ki = at("ki", 177, [P, SEQ])
        ckv = at("ckv", 179, [P, KVC, SEQ])
        sqb = at("sqb", 183, [P, 2, SEQ])
        acc = at("acc", 187, [P, SEQ])
        qT = at("qT", 96, [P, HEADS, SEQ])
        sel = at("sel", 112, [P, 10, P])
        kT = at("kT", 117, [P, HEADS, SEQ])
        Lb = at("Lb", 133, [P, 2, SEQ])
        mixT = at("mixT", 137, [P, DC, SEQ])
        gb = at("gb", 153, [P, DC, SEQ])
        PT = at("PT", 169, [P, NQB, SEQ])
        Bb = at("Bb", 177, [P, SEQ])
        Pb = at("Pb", 183, [P, 3, SEQ])
        vS = at("vS", 16, [P, NQB, HEADS * P])
        rel = sqb

        mring = at("mring", 32, [P, 6, 2 * D])
        mring_lo = at("mring_lo", 32, [P, 6, 2 * D], F32R)
        mring_hi = at("mring_hi", 80, [P, 6, 2 * D], F32R)
        u_tok = at("u_tok", 128, [P, NQB, D])
        gt = at("gt", 144, [P, 2048])
        big = at("big", 152, [P, MOE_BLOCKS * EXPERTS])
        tixI = at("tixI", 157, [P, 2 * NQB], I32)
        destI = at("destI", 157.125, [P, 2 * NQB], I32)
        tokI = at("tokI", 157.25, [P, NQB], I32)
        bexpI = at("bexpI", 157.5, [P, MOE_BLOCKS], I32)
        overI = at("overI", 157.75, [P, 1], I32)
        ids = at("ids", 158, [P, MOE_BLOCKS + 1], I32)
        xs = at("xs", 160, [P, 2, D])
        xsT_hi = at("xsT_hi", 136, [P, 2, DC, P], F32R)
        xsT_lo = at("xsT_lo", 168, [P, 2, DC, P], F32R)
        sil = at("sil", 176, [P, D_EXPERT])
        hid = at("hid", 178, [P, D_EXPERT])
        hidT_hi = at("hidT_hi", 180, [P, 4, P], F32R)
        hidT_lo = at("hidT_lo", 184, [P, 4, P], F32R)
        ysb = at("ysb", 128, [P, 2, D])
        y_tok = at("y_tok", 96, [P, 2, NQB, D])
        qk2 = at("qk2", 96, [P, 8, SEQ])
        v2 = at("v2", 112, [P, NQB, SEQ])
        near = at("near", 120, [P, 2, 10 * P])
        rp = at("rp", 130, [P, 2, 3 * P])
        P2 = at("P2", 137, [P, 4, SEQ])
        PT2 = at("PT2", 145, [P, NQB, SEQ])
        o2 = at("o2", 153, [P, 4, SEQ])
        sg = at("sg", 161, [P, 2, SEQ])
        a_hi = at("a_hi", 0, [P, HEADS, SEQ], F32R)
        a_lo = at("a_lo", 96, [P, HEADS, SEQ], F32R)
        mix_hi = at("mix_hi", 153, [P, DC, SEQ], F32R)
        mix_lo = at("mix_lo", 137, [P, DC, SEQ], F32R)
        xS = at("xS", 117, [P, DC, SEQ])
        cq = at("cq", 137, [P, MQC, SEQ])
        ckv2 = at("ckv2", 143, [P, KVC, SEQ])
        krT = at("krT", 147, [P, SEQ])
        raw = at("raw", 149, [P, 2, SEQ])
        q96 = at("q96", 96, [P, HEADS, SEQ])
        k96 = at("k96", 112, [P, HEADS, SEQ])
        vM = at("vM", 128, [P, NQB, SEQ])
        x_hi = at("x_hi", 0, [P, DC, SEQ], F32R)
        x_lo = [at("xa_lo", 165, [P, DC, SEQ], F32R), at("xf_lo", 16, [P, DC, SEQ], F32R)]
        x_lo_f = [at("xa_lo_f", 165, [P, DC, SEQ]), uT]
        o_hi = at("o_hi", 96, [P, 4, SEQ], F32R)
        o_lo = at("o_lo", 153, [P, 4, SEQ], F32R)
        m_hi = at("m_hi", 104, [P, DC, SEQ], F32R)
        m_lo = at("m_lo", 16, [P, DC, SEQ], F32R)
        g_hi = at("g_hi", 96, [P, FFC, SEQ], F32R)
        g_lo = at("g_lo", 140, [P, FFC, SEQ], F32R)
        g_f = at("g_f", 140, [P, FFC, SEQ])
        lamS = at("lamS", 161, [P, LAYERS * 4 * 64])
        table = nc.dram_tensor("table", (P * (MOE_BLOCKS + 1), 1), I32, kind="Internal").ap()
        u_rows = nc.dram_tensor("u_rows", (SEQ, D), F32, kind="Internal").ap()
        y_rows = nc.dram_tensor("y_rows", (MOE_BLOCKS * P, D), F32, kind="Internal").ap()

        ps = ctx.enter_context(nc.psum_tensor("ps", [P, 8, SEQ], F32))

        const_in, late_in, vec_in, x_in, c_in = (sem(n) for n in ("const_in", "late_in", "vec_in", "x_in", "c_in"))
        rest_in = sem("rest_in")
        x_back, a_lo_rdy = sem("x_back"), sem("a_lo_rdy")
        w_in = [sem(f"w_in{i}") for i in range(SLOTS)]
        w_used, hi_rdy, lo_rdy, t_rdy, y_hi_rdy, o2_rdy = (sem(n) for n in ("w_used", "hi_rdy", "lo_rdy", "t_rdy", "y_hi_rdy", "o2_rdy"))
        A = Bank(ps, (0, 1), sem("a_full"), sem("a_free"))
        B = Bank(ps, (2, 3), sem("b_full"), sem("b_free"))
        dve_step, pool_step = sem("dve_step"), sem("pool_step")
        c_silu, mod_used, pad_rdy = (sem(n) for n in ("c_silu", "mod_used", "pad_rdy"))
        mod_in = [sem(f"mod_in{q}") for q in range(4)]
        squared, sq_added, norm_var, norm_rstd, u_rdy = sem("squared"), sem("sq_added"), sem("norm_var"), sem("norm_rstd"), sem("u_rdy")
        inv_rdy = sem("inv_rdy")
        a_coef, sp_rdy = sem("a_coef"), sem("sp_rdy")
        conv_rdy, gate_s, gate_t, gated_x, decay_rdy = (sem(n) for n in ("conv_rdy", "gate_s", "gate_t", "gated_x", "decay_rdy"))
        root_sq, half_inv, root_fixed, pool_fix = (sem(n) for n in ("root_sq", "half_inv", "root_fixed", "pool_fix"))
        lru_sqrt, h_rdy, gelu_rdy, gh_rdy = (sem(n) for n in ("lru_sqrt", "h_rdy", "gelu_rdy", "gh_rdy"))
        ckv_raw, qik_rdy, wi_rdy, ckv_rdy = (sem(n) for n in ("ckv_raw", "qik_rdy", "wi_rdy", "ckv_rdy"))
        g_rdy, q_rdy, k_rdy, v_rdy, mix2_rdy = (sem(n) for n in ("g_rdy", "q_rdy", "k_rdy", "v_rdy", "mix2_rdy"))
        ix_score, ix_rel, ix_acc, sel_rdy = (sem(n) for n in ("ix_score", "ix_rel", "ix_acc", "sel_rdy"))
        sc_rdy, mx_rdy, exp_done, p_norm, turned, pt_rdy, att_rdy = (
            sem(n) for n in ("sc_rdy", "mx_rdy", "exp_done", "p_norm", "turned", "pt_rdy", "att_rdy"))
        h1_rdy = sem("h1_rdy")
        table_clear, brow_in, u_stored, logit_in, ohot, gl_diff, gl_exp, e_diff, e_exp, route_rdy = (sem(n) for n in (
            "table_clear", "brow_in", "u_stored", "logit_in", "ohot", "gl_diff", "gl_exp", "e_diff", "e_exp", "route_rdy"))
        tix_rdy, table_set, ids_in, moe_go = (sem(n) for n in ("tix_rdy", "table_set", "ids_in", "moe_go"))
        xs_in = [sem(f"xs_in{j}") for j in range(2)]
        part_in = [sem(f"part_in{k}") for k in range(6)]
        part_hi, part_lo, xs_hi, xs_lo, ht_hi, ht_lo = (sem(n) for n in ("part_hi", "part_lo", "xs_hi", "xs_lo", "ht_hi", "ht_lo"))
        xt_full, gate_full, up_full, sil_done, hid_done = (sem(n) for n in (
            "xt_full", "gate_full", "up_full", "sil_done", "hid_done"))
        ht_full, y0_full, y1_full, y0_rdy, y1_rdy = (sem(n) for n in (
            "ht_full", "y0_full", "y1_full", "y0_rdy", "y1_rdy"))
        y_stored = [sem(f"y_stored{j}") for j in range(2)]
        rows_back = [sem(f"rows_back{r}") for r in range(NQB)]
        mixed_rows, h2_rdy, b1_rdy, summed, centered, x_rdy = (sem(n) for n in (
            "mixed_rows", "h2_rdy", "b1_rdy", "summed", "centered", "x_rdy"))
        lam_in, lam_sum, lam_exp, sub_rdy = (sem(n) for n in ("lam_in", "lam_sum", "lam_exp", "sub_rdy"))
        rp_in, near_rdy, roped, vals_rdy, keys_rdy = (sem(n) for n in ("rp_in", "near_rdy", "roped", "vals_rdy", "keys_rdy"))
        pair_exp, pair_norm, pair_turned, pair_pt = (sem(n) for n in ("pair_exp", "pair_norm", "pair_turned", "pair_pt"))
        pair_sc, pair_mx, o_rdy, sg_rdy, sg_used, merged_rdy = (sem(n) for n in ("pair_sc", "pair_mx", "o_rdy", "sg_rdy", "sg_used", "merged_rdy"))
        lat_rdy, kr_rdy, hid_rdy = (sem(n) for n in ("lat_rdy", "kr_rdy", "hid_rdy"))
        stored = sem("stored")

        n_norm = {"act": 0, "dve": 0, "pe": 0, "i": 0}
        cnt = {"hi": 0, "t_a": 0, "t_d": 0, "sq_a": 0, "sq_d": 0, "sq_p": 0, "nv_a": 0, "nv_d": 0, "nv_p": 0, "dv": 0, "av": 0, "pv": 0}
        plan = {"at": -1, "owed": 0, "mod": 0}

        def after(eng, ins, s, key):
            ins.then_inc(s, 1)
            cnt[key] += 1
            eng.wait_ge(s, cnt[key])

        def chunk(pe, c, n=1):
            slot = c // CHUNKS
            if slot != plan["at"]:
                assert not plan["owed"]
                passed = slot - plan["at"] - 1 if plan["at"] >= 0 else 0
                if passed:
                    plan["mod"] += passed
                    pe.wait_ge(mod_used, 1 + plan["mod"])
                plan["owed"] = 1 + passed if plan["at"] >= 0 else 0
                plan["at"] = slot
                q = split_no(slot)
                if q is None:
                    pe.wait_ge(w_in[slot % SLOTS], 16 * (slot // SLOTS + 1))
                else:
                    pe.wait_ge(lo_rdy, q + 1)
            return views(c, n)

        def views(c, n=1):
            slot, o = c // CHUNKS, (c % CHUNKS) * P
            q = split_no(slot)
            if q is None:
                return wring[:, slot % SLOTS, o:o + n * P]
            return w_hi[:, q % HI_SLOTS, o:o + n * P], w_lo[:, slot % SLOTS, o:o + n * P]

        def said(ins):
            if plan["owed"]:
                ins.then_inc(w_used, 1)
                plan["owed"] -= 1

        def tile(pe, bank, c0, rhs, nk, m=P, wait=None):
            for k in range(nk):
                w = chunk(pe, c0 + k)
                if wait is not None:
                    wait(k)
                ins = pe.matmul(bank, w[:, 0:m], rhs[:, k, :], start=(k == 0), stop=(k == nk - 1))
                if k < nk - 1:
                    said(ins)
            return ins

        def tile3(pe, bank, c0, hi, lo, nk, m=P, wait=None):
            for k in range(nk):
                wh, wl = chunk(pe, c0 + k)
                if wait is not None:
                    wait(k)
                said(pe.matmul(bank, wh[:, 0:m], hi[:, k, :], start=(k == 0), stop=False))
                pe.matmul(bank, wh[:, 0:m], lo[:, k, :], start=False, stop=False)
                ins = pe.matmul(bank, wl[:, 0:m], hi[:, k, :], start=False, stop=(k == nk - 1))
            return ins

        def squares_pe(pe, n):
            cnt["sq_p"] += n
            pe.wait_ge(sq_added, cnt["sq_p"])
            b = B.claim(pe)
            for s in range(NQB):
                ins = pe.matmul(b[:, s:s + 1], acc[:, s * P:(s + 1) * P], ones[:, 0:1], start=True, stop=True)
            ins.then_inc(B.full, 1)

        def spread_pe(pe):
            cnt["nv_p"] += 1
            pe.wait_ge(inv_rdy, cnt["nv_p"])
            b = B.claim(pe)
            for s in range(NQB):
                ins = pe.matmul(b[:, s * P:(s + 1) * P], n_inv[:, s:s + 1].broadcast_to((P, P)), ident, start=True, stop=True)
            ins.then_inc(B.full, 1)

        def norm_pe(pe, n):
            squares_pe(pe, n)
            spread_pe(pe)

        def squares(act, X, n, wait=None):
            for c in range(n):
                if wait is not None:
                    wait(c)
                k = cnt["sq_a"]
                if k >= 2:
                    act.wait_ge(sq_added, k - 1)
                act.activation(sqb[:, k % 2, :], X[:, c, :], ACT.Square).then_inc(squared, 1)
                cnt["sq_a"] += 1

        def weights_hi(act, c, ahead=2):
            slot = c // CHUNKS
            end = n_slots1 if slot < n_slots1 else n_slots1 + LAYERS * n_slots2
            upto = sum(g <= slot for g in split) + ahead
            while cnt["hi"] < min(upto, len(split)) and split[cnt["hi"]] < min(slot + SLOTS - 1, end):
                q, g = cnt["hi"], split[cnt["hi"]]
                act.wait_ge(w_in[g % SLOTS], 16 * (g // SLOTS + 1))
                if q >= HI_SLOTS:
                    act.wait_ge(w_used, split[q - HI_SLOTS] + 1)
                act.activation(w_hi[:, q % HI_SLOTS, :], wring[:, g % SLOTS, :], ACT.Copy).then_inc(hi_rdy, 1)
                cnt["hi"] += 1

        def weights_lo(pool, slot):
            q = split_no(slot)
            if q is not None:
                pool.wait_ge(hi_rdy, q + 1)
                pool.tensor_tensor(w_lo[:, slot % SLOTS, :], wring[:, slot % SLOTS, :], w_hi[:, q % HI_SLOTS, :].bitcast(F32),
                                   ALU.subtract).then_inc(lo_rdy, 1)

        def norm_hi(act, b):
            for c in range(DC):
                cnt["t_a"] += 1
                act.wait_ge(t_rdy, cnt["t_a"])
                act.activation(x_hi[:, c, :], x_lo_f[b[1]][:, c, :], ACT.Identity, bias=b[0][:, c:c + 1]).then_inc(y_hi_rdy, 1)

        def root(act):
            cnt["nv_a"] += 1
            act.wait_ge(norm_var, cnt["nv_a"])
            act.activation(n_inv, n_rec, ACT.Sqrt).then_inc(norm_rstd, 1)

        def sum_squares(dve, n):
            for c in range(n):
                k = cnt["sq_d"]
                dve.wait_ge(squared, k + 1)
                if c == 0:
                    ins = dve.tensor_copy(acc[:], sqb[:, k % 2, :])
                else:
                    ins = dve.tensor_tensor(acc[:], acc[:], sqb[:, k % 2, :], ALU.add)
                ins.then_inc(sq_added, 1)
                cnt["sq_d"] += 1
                dve.wait_ge(sq_added, k + 1)

        def inverse_root(dve, width, eps):
            b = B.take(dve)
            dve.tensor_scalar(n_var, b[:, 0:NQB], 1.0 / width, eps, ALU.mult, ALU.add).then_inc(B.free, 1)
            dve.wait_ge(B.free, B.took)
            dve.reciprocal(n_rec, n_var).then_inc(norm_var, 1)
            cnt["nv_d"] += 1
            dve.wait_ge(norm_rstd, cnt["nv_d"])
            after(dve, dve.tensor_tensor(n_var, n_var, n_inv, ALU.mult), dve_step, "dstep")
            after(dve, dve.tensor_tensor(n_var, n_var, n_inv, ALU.mult), dve_step, "dstep")
            after(dve, dve.tensor_scalar(n_var, n_var, -0.5, 1.5, ALU.mult, ALU.add), dve_step, "dstep")
            dve.tensor_tensor(n_inv, n_inv, n_var, ALU.mult).then_inc(inv_rdy, 1)

        def spread(dve):
            dve.tensor_copy(rstd, B.take(dve)).then_inc(B.free, 1)
            dve.wait_ge(B.free, B.took)

        def inverse_var(dve, width, eps):
            inverse_root(dve, width, eps)
            spread(dve)

        rstd = acc[:]

        def free_bank_b(dve):
            dve.engine_nop().then_inc(B.free, 1)

        def add_up(dve, X, c):
            dve.tensor_tensor(acc[:], X[:, 0, :] if c == 1 else acc[:], X[:, c, :], ALU.add).then_inc(summed, 1)
            cnt["sum"] = cnt.get("sum", 0) + 1
            dve.wait_ge(summed, cnt["sum"])

        def center(dve, X):
            b = B.take(dve)
            dve.tensor_scalar(acc[:], b, 1.0 / D, None, ALU.mult).then_inc(B.free, 1)
            dve.wait_ge(B.free, B.took)
            for c in range(DC):
                dve.tensor_tensor(X[:, c, :], X[:, c, :], acc[:], ALU.subtract).then_inc(centered, 1)
            cnt["cen"] = cnt.get("cen", 0) + DC
            dve.wait_ge(centered, cnt["cen"])

        def mean_pe(pe):
            cnt["sum_p"] = cnt.get("sum_p", 0) + DC - 1
            pe.wait_ge(summed, cnt["sum_p"])
            pe.matmul(B.claim(pe), ones, acc[:], start=True, stop=True).then_inc(B.full, 1)

        def normed(dve, X, Y, g, b, turn=False):
            sum_squares(dve, DC)
            inverse_var(dve, D, LN_EPS)
            for c in range(DC):
                after(dve, dve.scalar_tensor_tensor(out=X[:, c, :], in0=X[:, c, :], scalar=g[:, c:c + 1], in1=rstd,
                                                    op0=ALU.mult, op1=ALU.mult), dve_step, "dstep")
                x, y = X[:, c, :], Y[:, c, :]
                if turn:
                    x = x.rearrange("p (r j c) -> p r j c", r=GRID_ROWS, j=NA_TILES)
                    y = y.rearrange("p (j r c) -> p r j c", r=GRID_ROWS, j=NA_TILES)
                dve.tensor_scalar(y, x, b[:, c:c + 1], None, ALU.add).then_inc(x_rdy, 1)

        def normed_split(dve, X, to, g, b, turn=False):
            sum_squares(dve, DC)
            inverse_var(dve, D, LN_EPS)
            scale_split(dve, X, to, g, b, x_rdy, turn)

        def scale_split(dve, X, to, g, b, rdy, turn=False):
            def low(c):
                t = x_lo_f[to][:, c, :]
                dve.wait_ge(y_hi_rdy, cnt["t_d"] + c + 1)
                dve.scalar_tensor_tensor(out=x_lo[to][:, c, :], in0=t, scalar=b[:, c:c + 1], in1=x_hi[:, c, :].bitcast(F32),
                                         op0=ALU.add, op1=ALU.subtract).then_inc(rdy, 1)
            for c in range(DC):
                y = x_lo_f[to][:, c, :]
                ins = dve.scalar_tensor_tensor(out=X[:, c, :] if turn else y, in0=X[:, c, :], scalar=g[:, c:c + 1], in1=rstd, op0=ALU.mult, op1=ALU.mult)
                if turn:
                    after(dve, ins, dve_step, "dstep")
                    ins = dve.tensor_copy(y.rearrange("p (j r c) -> p r j c", r=GRID_ROWS, j=NA_TILES),
                                          X[:, c, :].rearrange("p (r j c) -> p r j c", r=GRID_ROWS, j=NA_TILES))
                ins.then_inc(t_rdy, 1)
                if c >= 1:
                    low(c - 1)
            low(DC - 1)
            cnt["t_d"] += DC

        names = {"lg": 144, "gmax": 4, "w": 32, "wm": 4, "goh": 16, "gd": 16, "ge": 16, "es": 32, "m1": 4, "m2": 4,
                 "oh1": 32, "oh2": 32, "d": 4, "ex": 4, "gw": 4, "p1": 4, "M1": 128, "M2": 128, "M": 128, "pos": 128,
                 "cts": 32, "nb": 32, "cum": 32, "st": 32, "bq": 128, "tix": 128, "ix": 4, "be": MOE_BLOCKS}
        starts = dict(zip(names, np.cumsum([0] + list(names.values())).tolist()))

        def T(name):
            return gt[:, starts[name]:starts[name] + names[name]]

        A_ATT = A_ROWS = RC + 2 * RC + KVC + 4 + 1 + 1 + RC + 2 * DC + HEADS + HEADS + 2 * NQB + HEADS

        def units_pe(pe, units, ready, Pb=Pb):
            U = len(units)
            for i in range(U + 3):
                if i < U:
                    u = units[i]
                    k = cnt["pv"] + i
                    ready(i)
                    if k >= 2:
                        pe.wait_ge(exp_done, k - 1)
                    ins = pe.matmul(ps[:, 4 + k % 2, 0:u["nk"] * P], u["q"], u["k"], start=True, stop=True)
                    ins.then_inc(sc_rdy, 1)
                if 2 <= i < U + 2:
                    u = units[i - 2]
                    k = cnt["pv"] + i - 2
                    pe.wait_ge(p_norm, k + 1)
                    if k >= 2:
                        pe.wait_ge(pt_rdy, k - 1)
                    for j in range(u["nk"]):
                        ins = pe.transpose(ps[:, 6 + k % 2, j * P:(j + 1) * P], Pb[:, k % 3, j * P:(j + 1) * P], ident)
                    ins.then_inc(turned, 1)
                if i >= 3 and "sum" in units[i - 3]:
                    pe.wait_ge(pt_rdy, cnt["pv"] + i - 2)
                    units[i - 3]["sum"](pe)
            cnt["pv"] += U

        def units_dve(dve, units, Pb=Pb):
            U = len(units)

            def norm(i):
                k = cnt["dv2"] + i
                n = units[i]["nk"] * P
                dve.wait_ge(exp_done, k + 1)
                after(dve, dve.reciprocal(rinv[:, k % 4:k % 4 + 1], rsum[:, k % 4:k % 4 + 1]), dve_step, "dstep")
                dve.tensor_scalar(Pb[:, k % 3, 0:n], Pb[:, k % 3, 0:n], rinv[:, k % 4:k % 4 + 1], None, ALU.mult).then_inc(p_norm, 1)

            for i, u in enumerate(units):
                k = cnt["dv2"] + i
                n = u["nk"] * P
                dve.wait_ge(sc_rdy, k + 1)
                s = ps[:, 4 + k % 2, 0:n]
                m = negmax[:, k % 4:k % 4 + 1]
                if "bias" in u:
                    b = u["bias"](dve)
                    if k >= 2:
                        dve.wait_ge(exp_done, k - 1)
                    after(dve, dve.scalar_tensor_tensor(out=Lb[:, k % 2, 0:n], in0=s, scalar=u["scale"], in1=b,
                                                        op0=ALU.mult, op1=ALU.add), dve_step, "dstep")
                    dve.reduce_max(m, Lb[:, k % 2, 0:n], AX_X, negate=True).then_inc(mx_rdy, 1)
                else:
                    after(dve, dve.reduce_max(m, s, AX_X, negate=True), dve_step, "dstep")
                    dve.tensor_scalar(m, m, u["scale"], None, ALU.mult).then_inc(mx_rdy, 1)
                if i >= 1:
                    norm(i - 1)
            norm(U - 1)
            cnt["dv2"] += U

        def units_act(act, units, sums, Pb=Pb, PT=PT):
            U = len(units)
            for i in range(U + 3):
                if i < U:
                    u = units[i]
                    k = cnt["av2"] + i
                    n = u["nk"] * P
                    act.wait_ge(mx_rdy, k + 1)
                    if k >= 3:
                        act.wait_ge(turned, k - 2)
                    src, sc = (Lb[:, k % 2, 0:n], 1.0) if "bias" in u else (ps[:, 4 + k % 2, 0:n], u["scale"])
                    act.activation(Pb[:, k % 3, 0:n], src, ACT.Exp, bias=negmax[:, k % 4:k % 4 + 1], scale=sc,
                                   accum_out=rsum[:, k % 4:k % 4 + 1]).then_inc(exp_done, 1)
                if i >= 3 and "sum" in units[i - 3]:
                    sums(units[i - 3])
                if 2 <= i < U + 2:
                    u = units[i - 2]
                    k = cnt["av2"] + i - 2
                    act.wait_ge(turned, k + 1)
                    t = ps[:, 6 + k % 2, 0:u["nk"] * P].rearrange("p (j q) -> p j q", q=P)
                    act.activation(PT[:, 0:u["nk"], u["qb"] * P:(u["qb"] + 1) * P], t, ACT.Copy).then_inc(pt_rdy, 1)
            cnt["av2"] += U

        cnt.update({"dv2": 0, "av2": 0, "dstep": 0, "astep": 0, "pfix": 0})

        def na_units():
            units, i0 = [], 0
            for h in range(HEADS):
                r, i0 = 64 * (h % 2), 0
                for n, (lo, hi) in enumerate(NA_KEYS):
                    units.append({"nk": hi - lo, "qb": n, "h": h, "scale": NA_SCALE,
                                  "q": qk2[r:r + 64, h // 2, n * P:(n + 1) * P], "k": qk2[r:r + 64, 4 + h // 2, lo * P:hi * P],
                                  "bias": lambda dve, h=h, a=i0, b=i0 + hi - lo, n=n: (
                                      wait_near(dve, h) if n == 0 else None, near[:, h % 2, a * P:b * P])[1]})
                    i0 += hi - lo

                def total(pe, h=h, r=r):
                    b = A.claim(pe)
                    for n, (lo, hi) in enumerate(NA_KEYS):
                        for j in range(lo, hi):
                            ins = pe.matmul(b[r:r + 64, n * P:(n + 1) * P], v2[:, j, h * 64:(h + 1) * 64],
                                            PT2[:, j - lo, n * P:(n + 1) * P], start=(j == lo), stop=(j == hi - 1))
                    ins.then_inc(A.full, 1)
                units[-1]["sum"] = total
            return units

        def wait_near(dve, h):
            cnt["near"] = cnt.get("near", 0) + 1
            dve.wait_ge(near_rdy, cnt["near"])

        def mla_units():
            units = []
            for h in range(HEADS):
                r = 64 * (h % 2)
                for qb in range(NQB):
                    units.append({"nk": NQB, "qb": qb, "h": h, "scale": MLA_SCALE,
                                  "q": q96[0:MLA_QK, h, qb * P:(qb + 1) * P], "k": k96[0:MLA_QK, h, :]})

                def total(pe, h=h, r=r):
                    b = A.claim(pe)
                    for j in range(NQB):
                        ins = pe.matmul(b[r:r + 64, :], vM[:, j, h * 64:(h + 1) * 64], PT2[:, j, :], start=(j == 0), stop=(j == NQB - 1))
                    ins.then_inc(A.full, 1)
                units[-1]["sum"] = total
            return units

        pairs = [(h, qb) for h in range(4) for qb in range(NQB)]
        pair_banks = ((4, 5), (2, 3))

        dsa = []
        for h in range(HEADS):
            for qb in range(NQB):
                dsa.append({"nk": qb + 1, "qb": qb, "h": h, "scale": DSA_SCALE,
                            "q": qT[:, h, qb * P:(qb + 1) * P], "k": kT[:, h, 0:(qb + 1) * P]})

                def bias(dve, h=h, qb=qb):
                    n = (qb + 1) * P
                    o = qb * (qb + 1) // 2
                    d = K("dist")[:, (NQB - 1 - qb) * P:(NQB - 1 - qb) * P + n]
                    after(dve, dve.scalar_tensor_tensor(
                        out=Bb[:, 0:n], in0=d, scalar=-(2.0 ** (-8.0 * (h + 1) / HEADS)),
                        in1=sel[:, o:o + qb + 1, :].rearrange("p j q -> p (j q)"), op0=ALU.mult, op1=ALU.add),
                        dve_step, "dstep")
                    return Bb[:, 0:n]
                dsa[-1]["bias"] = bias

            def total(pe, h=h):
                b = A.claim(pe)
                for j in range(NQB):
                    ins = pe.matmul(b[:, j * P:SEQ], vS[:, j, h * P:(h + 1) * P], PT[:, j, j * P:SEQ],
                                    start=(j == 0), stop=(j == NQB - 1))
                ins.then_inc(A.full, 1)
            dsa[-1]["sum"] = total

        U_DSA = HEADS * NQB
        U_LAYER = 2 * HEADS * NQB

        def layer_pe(pe, l):
            base = {name: end1 + l * size2 + c for name, c in two.items()}
            xa, xf = (x_hi, x_lo[0]), (x_hi, x_lo[1])

            def gated(c0, branch, between=None):
                for m in range(DC):
                    tile3(pe, A.claim(pe), c0 + m * (DC + 4), *xa, DC).then_inc(A.full, 1)
                    tile3(pe, B.claim(pe), c0 + m * (DC + 4) + DC, o_hi, o_lo, 4,
                          wait=(lambda k: pe.wait_ge(o2_rdy, 4 * (3 * l + branch) + k + 1)) if m == 0 else None).then_inc(B.full, 1)
                    if between is not None:
                        between(m)

            def values(c0, wait=None):
                for j in range(NQB):
                    b = A.claim(pe)
                    for k in range(DC):
                        c = c0 + 4 * k
                        if k < DC // 2 or j == NQB - 1:
                            wh, wl = chunk(pe, c, 4)
                        else:
                            if j == 0 and k == DC // 2:
                                pe.wait_ge(lo_rdy, split_no(c // CHUNKS) + 1)
                            wh, wl = views(c, 4)
                        if j == 0 and wait is not None:
                            wait(k)
                        xh, xl = (x[:, k, j * P:(j + 1) * P] for x in xa)
                        said(pe.matmul(b, xh, wh, start=(k == 0), stop=False))
                        pe.matmul(b, xh, wl, start=False, stop=False)
                        ins = pe.matmul(b, xl, wh, start=False, stop=(k == DC - 1))
                    ins.then_inc(A.full, 1)

            values(base["na_v"], lambda k: pe.wait_ge(x_rdy, 2 * DC * l + k + 1))
            for m in range(8):
                tile3(pe, A.claim(pe), base["na_qk"] + m * DC, *xa, DC).then_inc(A.full, 1)
            units_pe(pe, na_units(), lambda i: pe.wait_ge(A.free, A.made) if i == 0 else None, P2)
            gated(base["na_gb"], 0)

            values(base["df_v"])

            def turn(perm, m, n=P):
                pe.wait_ge(A.free, m)
                pe.matmul(B.claim(pe)[0:n, :], perm[0:n, 0:n], raw[0:n, (cnt["rp"]) % 2, :], start=True, stop=True).then_inc(B.full, 1)
                cnt["rp"] += 1
            for m in range(8):
                tile3(pe, A.claim(pe), base["df_qk"] + m * DC, *xa, DC).then_inc(A.full, 1)
                if m >= 1:
                    turn(K("perm_d"), A.made - 1)
            turn(K("perm_d"), A.made)
            pe.wait_ge(B.free, B.made)
            pe.wait_ge(roped, l * 16 + 8)
            U = len(pairs)
            for i in range(U + 3):
                if i < U:
                    h, qb = pairs[i]
                    k = l * U + i
                    if k >= 2:
                        pe.wait_ge(pair_exp, 2 * (k - 1))
                    for a in range(2):
                        r = 64 * a
                        pe.matmul(ps[:, pair_banks[k % 2][a], :], qk2[r:r + 64, h, qb * P:(qb + 1) * P], qk2[r:r + 64, 4 + h, :],
                                  start=True, stop=True).then_inc(pair_sc, 1)
                if 2 <= i < U + 2:
                    k = l * U + i - 2
                    pe.wait_ge(pair_norm, k + 1)
                    if k >= 2:
                        pe.wait_ge(pair_pt, k - 1)
                    for j in range(NQB):
                        ins = pe.transpose(ps[:, 6 + k % 2, j * P:(j + 1) * P], P2[:, 2 * (k % 2), j * P:(j + 1) * P], ident)
                    ins.then_inc(pair_turned, 1)
                if i >= 3 and pairs[i - 3][1] == NQB - 1:
                    h = pairs[i - 3][0]
                    pe.wait_ge(pair_pt, l * U + i - 2)
                    b = A.claim(pe)
                    for j in range(NQB):
                        ins = pe.matmul(b, v2[:, j, h * P:(h + 1) * P], PT2[:, j, :], start=(j == 0), stop=(j == NQB - 1))
                    ins.then_inc(A.full, 1)
            for m in range(MQC + KVC):
                tile3(pe, A.claim(pe), base["cq"] + m * DC, *xa, DC).then_inc(A.full, 1)
                if m >= 1:
                    spread_pe(pe)
                if m < 4:
                    squares_pe(pe, 1)
            tile3(pe, A.claim(pe)[0:MLA_QK, :], base["kr"], *xa, DC, MLA_QK).then_inc(A.full, 1)
            kr_copied = A.made

            def latent_norms(m):
                if m in (1, 3):
                    squares_pe(pe, (MQC, KVC)[m // 2])
                elif m in (2, 4):
                    spread_pe(pe)
                elif m == 5:
                    pe.wait_ge(A.free, kr_copied)
                    pe.matmul(B.claim(pe)[0:MLA_QK, :], K("perm_m")[0:MLA_QK, 0:MLA_QK], krT[0:MLA_QK, :], start=True, stop=True).then_inc(B.full, 1)
            gated(base["df_gb"], 1, latent_norms)

            pe.wait_ge(lat_rdy, (l + 1) * (MQC + KVC))
            for h in range(HEADS):
                tile(pe, A.claim(pe)[0:MLA_QK, :], base["qb"] + h * MQC, cq, MQC, MLA_QK).then_inc(A.full, 1)
                if h >= 1:
                    turn(K("perm_m"), A.made - 1, MLA_QK)
            turn(K("perm_m"), A.made, MLA_QK)
            for h in range(HEADS):
                b = A.claim(pe)
                for k in range(KVC):
                    w = chunk(pe, base["kvb_k"] + (h // 2) * KVC + k)
                    ins = pe.matmul(b[0:64, :], w[:, 64 * (h % 2):64 * (h % 2) + 64], ckv2[:, k, :], start=(k == 0), stop=(k == KVC - 1))
                    if k < KVC - 1:
                        said(ins)
                ins.then_inc(A.full, 1)
            for s_ in range(NQB):
                b = A.claim(pe)
                for k in range(KVC):
                    ins = pe.matmul(b, ckv2[:, k, s_ * P:(s_ + 1) * P], chunk(pe, base["kvb_v"] + 4 * k, 4), start=(k == 0), stop=(k == KVC - 1))
                    if k < KVC - 1:
                        said(ins)
                ins.then_inc(A.full, 1)
            pe.wait_ge(roped, l * 16 + 16)
            pe.wait_ge(keys_rdy, l + 1)
            units_pe(pe, mla_units(), lambda i: pe.wait_ge(A.free, A.made) if i == 0 else None, P2)
            gated(base["ml_gb"], 2)

            pe.wait_ge(merged_rdy, (l + 1) * 3 * DC)
            for m in range(DC):
                tile3(pe, B.claim(pe), base["out2"] + m * DC, m_hi, m_lo, DC).then_inc(B.full, 1)
            mean_pe(pe)
            norm_pe(pe, DC)
            for m in range(FFC):
                tile3(pe, A.claim(pe), base["ffn_in"] + 2 * m * DC, *xf, DC,
                     wait=(lambda k: pe.wait_ge(x_rdy, 2 * DC * l + DC + k + 1)) if m == 0 else None).then_inc(A.full, 1)
                tile3(pe, B.claim(pe), base["ffn_in"] + (2 * m + 1) * DC, *xf, DC).then_inc(B.full, 1)
            for m in range(DC):
                tile3(pe, B.claim(pe), base["ffn_out"] + m * FFC, g_hi, g_lo, FFC,
                     wait=(lambda k: pe.wait_ge(hid_rdy, l * FFC + k + 1)) if m == 0 else None).then_inc(B.full, 1)
            mean_pe(pe)
            norm_pe(pe, DC)

        def layer_act(act, l):
            def copy(to, n=P):
                act.activation(to, A.take(act)[0:n, :], ACT.Copy).then_inc(A.free, 1)

            def gates(branch, between=None):
                bg = V(f"b_gate{l}")
                for m in range(DC):
                    weights_hi(act, end1 + l * size2 + two[("na_gb", "df_gb", "ml_gb")[branch]] + m * (DC + 4))
                    k = (3 * l + branch) * DC + m
                    if k >= 2:
                        act.wait_ge(sg_used, k - 1)
                    act.activation(sg[:, k % 2, :], A.take(act), ACT.Sigmoid, bias=bg[:, branch * DC + m:branch * DC + m + 1]).then_inc(A.free, 1)
                    if between is not None:
                        between(m)

            for j in range(NA_TILES):
                weights_hi(act, end1 + l * size2 + two["na_v"] + (CHUNKS if j == NA_TILES - 1 else 0))
                copy(v2[:, j, :])
            for m in range(8):
                weights_hi(act, end1 + l * size2 + two["na_qk"] + m * DC)
                copy(qk2[:, m, :])

            def na_out(u):
                r = 64 * (u["h"] % 2)
                act.activation(o2[r:r + 64, u["h"] // 2, :], A.take(act)[r:r + 64, :], ACT.Copy).then_inc(A.free, 1)
            units_act(act, na_units(), na_out, P2, PT2)
            gates(0)

            for s_ in range(NQB):
                weights_hi(act, end1 + l * size2 + two["df_v"] + (CHUNKS if s_ == NQB - 1 else 0))
                copy(v2[:, s_, :])
            for m in range(8):
                weights_hi(act, end1 + l * size2 + two["df_qk"] + m * DC)
                if m >= 2:
                    act.wait_ge(roped, l * 16 + m - 1)
                copy(raw[:, m % 2, :])
            U = len(pairs)
            for i in range(U + 3):
                if i < U:
                    k = l * U + i
                    if k >= 2:
                        act.wait_ge(pair_turned, k - 1)
                    for a in range(2):
                        act.wait_ge(pair_mx, 2 * k + a + 1)
                        act.activation(P2[:, 2 * (k % 2) + a, :], ps[:, pair_banks[k % 2][a], :], ACT.Exp,
                                       bias=negmax[:, 2 * (k % 2) + a:2 * (k % 2) + a + 1], scale=DIFF_SCALE,
                                       accum_out=rsum[:, 2 * (k % 2) + a:2 * (k % 2) + a + 1]).then_inc(pair_exp, 1)
                if i >= 3 and pairs[i - 3][1] == NQB - 1:
                    copy(o2[:, pairs[i - 3][0], :])
                if 2 <= i < U + 2:
                    k = l * U + i - 2
                    act.wait_ge(pair_turned, k + 1)
                    qb = pairs[i - 2][1]
                    act.activation(PT2[:, :, qb * P:(qb + 1) * P], ps[:, 6 + k % 2, :].rearrange("p (j q) -> p j q", q=P),
                                   ACT.Copy).then_inc(pair_pt, 1)
            act.wait_ge(A.free, A.took)
            squares(act, o2[:, 0:1, :], 1)
            for h in range(4):
                if h + 1 < 4:
                    squares(act, o2[:, h + 1:h + 2, :], 1)
                weights_hi(act, end1 + l * size2 + two["cq"] + h * DC)
                copy(cq[:, h, :] if h < MQC else ckv2[:, h - MQC, :])
                root(act)
            for m in range(4 - MQC, KVC):
                weights_hi(act, end1 + l * size2 + two["mckv"] + m * DC)
                copy(ckv2[:, m, :])
            copy(krT[0:MLA_QK, :], MLA_QK)
            latents_copied = A.took

            def latent_norms(m):
                if m == 1:
                    act.wait_ge(A.free, latents_copied)
                    act.wait_ge(o_rdy, 4 * (l + 1))
                    squares(act, cq, MQC)
                    root(act)
                elif m == 3:
                    squares(act, ckv2, KVC)
                    root(act)
            gates(1, latent_norms)
            act.wait_ge(kr_rdy, l + 1)
            for h in range(HEADS):
                if h >= 2:
                    act.wait_ge(roped, l * 16 + 8 + h - 1)
                copy(raw[0:MLA_QK, h % 2, :], MLA_QK)
            for h in range(HEADS):
                copy(k96[0:64, h, :], 64)
            for s_ in range(NQB):
                copy(vM[:, s_, :])

            def mla_out(u):
                r = 64 * (u["h"] % 2)
                act.activation(o2[r:r + 64, u["h"] // 2, :], A.take(act)[r:r + 64, :], ACT.Copy).then_inc(A.free, 1)
            units_act(act, mla_units(), mla_out, P2, PT2)
            gates(2)

            for m in range(DC):
                weights_hi(act, end1 + l * size2 + two["out2"] + m * DC)
            squares(act, hT, DC, lambda c: act.wait_ge(centered, DC + 2 * DC * l + c + 1))
            root(act)
            norm_hi(act, (V(f"ln1_b{l}"), 1))
            for m in range(FFC):
                weights_hi(act, end1 + l * size2 + two["ffn_in"] + 2 * m * DC)
                act.activation(g_f[:, m, :], A.take(act), ACT.Silu).then_inc(A.free, 1)
            for c in range(0, DC * FFC, CHUNKS):
                weights_hi(act, end1 + l * size2 + two["ffn_out"] + c)
            squares(act, hT, DC, lambda c: act.wait_ge(centered, 2 * DC + 2 * DC * l + c + 1))
            root(act)
            if l < LAYERS - 1:
                norm_hi(act, (V(f"ln2_b{l}"), 0))

        def layer_dve(dve, l):
            step = lambda ins: after(dve, ins, dve_step, "dstep")
            TT, TS, STT = dve.tensor_tensor, dve.tensor_scalar, dve.scalar_tensor_tensor

            def branch(n, a_free, between=None):
                for m in range(DC):
                    k = (3 * l + n) * DC + m
                    dve.wait_ge(A.free, a_free + m + 1)
                    if n == 0:
                        TT(uT[:, m, :], B.take(dve), sg[:, k % 2, :], ALU.mult).then_inc(B.free, 1)
                        dve.wait_ge(B.free, B.took)
                        dve.engine_nop().then_inc(sg_used, 1)
                        dve.engine_nop().then_inc(merged_rdy, 1)
                    else:
                        TT(sg[:, k % 2, :], B.take(dve), sg[:, k % 2, :], ALU.mult).then_inc(B.free, 1)
                        dve.wait_ge(B.free, B.took)
                        TT(uT[:, m, :], uT[:, m, :], sg[:, k % 2, :], ALU.add).then_inc(sg_used, 1)
                        if n == 2:
                            dve.wait_ge(sg_used, k + 1)
                            step(dve.tensor_copy(m_hi[:, m, :], uT[:, m, :]))
                            TT(m_lo[:, m, :], uT[:, m, :], m_hi[:, m, :].bitcast(F32), ALU.subtract).then_inc(merged_rdy, 1)
                        else:
                            dve.engine_nop().then_inc(merged_rdy, 1)
                    if between is not None:
                        between(m)

            def heads_split():
                for c in range(4):
                    step(dve.tensor_copy(o_hi[:, c, :], o2[:, c, :]))
                    TT(o_lo[:, c, :], o2[:, c, :], o_hi[:, c, :].bitcast(F32), ALU.subtract).then_inc(o2_rdy, 1)

            def rope(x, to, cos, sin, n=P):
                step(TT(to, x, cos, ALU.mult))
                TT(x, B.take(dve)[0:n, :] if n != 32 else B.take(dve)[64:MLA_QK, :], sin, ALU.mult).then_inc(B.free, 1)
                dve.wait_ge(B.free, B.took)
                return TT(to, to, x, ALU.add)

            a = A2 + l * A_LAYER
            units_dve(dve, na_units(), P2)
            a += 4 + 8 + HEADS
            dve.wait_ge(A.free, a)
            heads_split()
            branch(0, a)
            a += DC + 4
            for m in range(8):
                dve.wait_ge(A.free, a + m + 1)
                rope(raw[:, m % 2, :], qk2[:, m, :], K("cos_d"), K("sin_d")).then_inc(roped, 1)
            a += 8
            U = len(pairs)

            def pair(i):
                k = l * U + i
                c = 2 * (k % 2)
                dve.wait_ge(pair_exp, 2 * (k + 1))
                step(dve.reciprocal(rinv[:, c:c + 2], rsum[:, c:c + 2]))
                step(TT(rinv[:, c + 1:c + 2], rinv[:, c + 1:c + 2], lam_neg[:, l:l + 1], ALU.mult))
                step(TS(P2[:, c + 1, :], P2[:, c + 1, :], rinv[:, c + 1:c + 2], None, ALU.mult))
                STT(out=P2[:, c, :], in0=P2[:, c, :], scalar=rinv[:, c:c + 1], in1=P2[:, c + 1, :], op0=ALU.mult, op1=ALU.add).then_inc(pair_norm, 1)

            for i in range(U):
                k = l * U + i
                for q in range(2):
                    c = 2 * (k % 2) + q
                    dve.wait_ge(pair_sc, 2 * k + q + 1)
                    step(dve.reduce_max(negmax[:, c:c + 1], ps[:, pair_banks[k % 2][q], :], AX_X, negate=True))
                    TS(negmax[:, c:c + 1], negmax[:, c:c + 1], DIFF_SCALE, None, ALU.mult).then_inc(pair_mx, 1)
                if i >= 1:
                    pair(i - 1)
            pair(U - 1)
            a += 4
            for h in range(4):
                if h >= 1:
                    dve.wait_ge(o_rdy, 4 * l + h)
                sum_squares(dve, 1)
                inverse_var(dve, P, EPS)
                STT(out=o2[:, h, :], in0=o2[:, h, :], scalar=subg[:, l:l + 1], in1=rstd, op0=ALU.mult, op1=ALU.mult).then_inc(o_rdy, 1)
            a += MQC + KVC + 1
            dve.wait_ge(o_rdy, 4 * (l + 1))
            heads_split()

            def latent_norms(m):
                if m in (1, 3):
                    sum_squares(dve, (MQC, KVC)[m // 2])
                    inverse_root(dve, (MQ_RANK, KV_RANK)[m // 2], EPS)
                elif m in (2, 4):
                    X, n, g = ((cq, MQC, V(f"mq_g{l}")), (ckv2, KVC, V(f"mkv_g{l}")))[m // 4]
                    spread(dve)
                    for c in range(n):
                        STT(out=X[:, c, :], in0=X[:, c, :], scalar=g[:, c:c + 1], in1=rstd, op0=ALU.mult, op1=ALU.mult).then_inc(lat_rdy, 1)
                elif m == 5:
                    x = krT[64:MLA_QK, :]
                    t = raw[64:MLA_QK, 0, :]
                    TT(t, B.take(dve)[64:MLA_QK, :], K("sin_m")[64:MLA_QK, :], ALU.mult).then_inc(B.free, 1)
                    step(TT(x, x, K("cos_m")[64:MLA_QK, :], ALU.mult))
                    dve.wait_ge(B.free, B.took)
                    TT(x, x, t, ALU.add).then_inc(kr_rdy, 1)
                    dve.wait_ge(kr_rdy, l + 1)
                    dve.tensor_copy(k96[64:MLA_QK, :, :], krT[64:MLA_QK, :].unsqueeze(1).broadcast_to((32, HEADS, SEQ))).then_inc(keys_rdy, 1)
            branch(1, a, latent_norms)
            a += DC
            for h in range(HEADS):
                dve.wait_ge(A.free, a + h + 1)
                rope(raw[0:MLA_QK, h % 2, :], q96[0:MLA_QK, h, :], K("cos_m")[0:MLA_QK, :], K("sin_m")[0:MLA_QK, :], MLA_QK).then_inc(roped, 1)
            a += HEADS + HEADS + NQB
            units_dve(dve, mla_units(), P2)
            a += HEADS
            dve.wait_ge(A.free, a)
            heads_split()
            branch(2, a)
            a += DC

            def residual(where):
                for m in range(DC):
                    STT(out=hT[:, m, :], in0=x_hi[:, m, :].bitcast(F32), scalar=DN_ALPHA, in1=B.take(dve), op0=ALU.mult, op1=ALU.add).then_inc(B.free, 1)
                    dve.wait_ge(B.free, B.took)
                    step(STT(out=hT[:, m, :], in0=x_lo[where][:, m, :].bitcast(F32), scalar=DN_ALPHA, in1=hT[:, m, :], op0=ALU.mult, op1=ALU.add))
                    if m >= 1:
                        add_up(dve, hT, m)
            residual(0)
            center(dve, hT)
            normed_split(dve, hT, 1, V(f"ln1_g{l}"), V(f"ln1_b{l}"))
            for m in range(FFC):
                dve.wait_ge(A.free, a + m + 1)
                TT(g_f[:, m, :], B.take(dve), g_f[:, m, :], ALU.mult).then_inc(B.free, 1)
                dve.wait_ge(B.free, B.took)
                step(dve.tensor_copy(g_hi[:, m, :], g_f[:, m, :]))
                TT(g_lo[:, m, :], g_f[:, m, :], g_hi[:, m, :].bitcast(F32), ALU.subtract).then_inc(hid_rdy, 1)
            a += FFC
            assert a == A2 + (l + 1) * A_LAYER, (a, A2, A_LAYER)
            residual(1)
            center(dve, hT)
            if l < LAYERS - 1:
                normed_split(dve, hT, 0, V(f"ln2_g{l}"), V(f"ln2_b{l}"))
            else:
                normed(dve, hT, hT, V(f"ln2_g{l}"), V(f"ln2_b{l}"))

        A2 = RC + 2 * RC + KVC + 4 + 1 + 1 + RC + 2 * DC + HEADS + HEADS + 2 * NQB + HEADS + 2 * NQB
        A_LAYER = 4 + 8 + HEADS + DC + 4 + 8 + 4 + DC + MQC + KVC + 1 + HEADS + HEADS + NQB + HEADS + DC + FFC
        cnt["rp"] = 0
        block = ctx.enter_context(nc.Block())

        @block.sync
        def _(sp):
            for q in range(4):
                if q == 1:
                    sp.dma_start(vec[:], vectors).then_inc(vec_in, 16)
                    sp.dma_start(cs[:, 0:late[0]], consts[:, 0:late[0]]).then_inc(const_in, 16)
                if q == 2:
                    sp.dma_start(hT[:], xT).then_inc(x_in, 16)
                sp.dma_start(wmodS[:, 4 * q:4 * q + 4, :], wmod[:, 4 * q:4 * q + 4, :]).then_inc(mod_in[q], 16)
            for s in range(n_slots1):
                if s == SLOTS:
                    sp.dma_start(cs[:, late[1]:], consts[:, late[1]:]).then_inc(rest_in, 16)
                if s >= SLOTS:
                    sp.wait_ge(w_used, s - SLOTS + 1)
                if s == one["out"] // CHUNKS + 1:
                    sp.dma_start(xS[:], xT).then_inc(x_back, 16)
                sp.dma_start(wring[:, s % SLOTS, :], wfirst[s]).then_inc(w_in[s % SLOTS], 16)

            for r in range(NQB):
                sp.wait_ge(A.free, A_ROWS + 2 * r + 2)
                sp.dma_start(u_rows[r * P:(r + 1) * P, :], u_tok[:, r, :]).then_inc(u_stored, 16)

            sp.wait_ge(moe_go, 1)
            sp.dma_start(cs[:, late[0]:late[1]], consts[:, late[0]:late[1]]).then_inc(late_in, 16)
            sp.wait_ge(route_rdy, 1)

            def expert(b):
                e = sp.value_load(bexpI[0:1, bass.ds(b, 1)], min_val=0, max_val=EXPERTS - 1)
                first = isinstance(b, int) and b == 0
                for k, (w, done) in enumerate(((w1, gate_full), (w3, up_full), (w2, y1_full))):
                    if not first:
                        sp.wait_ge(done, b)
                    elif k == 1:
                        sp.wait_ge(xs_in[0], 16)
                    for h in range(2):
                        sp.dma_start(mring[:, 2 * k + h, :], w[bass.ds(e, 1)].rearrange("e p n -> (e p) n")[:, h * 2 * D:(h + 1) * 2 * D]
                                     ).then_inc(part_in[2 * k + h], 16)

            expert(0)
            with sp.Fori(1, MOE_SURE) as b:
                expert(b)
            over = sp.value_load(overI[0:1, 0:1], min_val=0, max_val=1)
            with sp.If(over):
                with sp.Fori(MOE_SURE, MOE_BLOCKS) as b:
                    expert(b)
                sp.wait_ge(y1_full, MOE_BLOCKS)
            sp.wait_ge(y1_full, MOE_SURE)
            for r in range(NQB):
                sp.wait_ge(rows_back[r], 32)
            for l in range(LAYERS):
                for s in range(n_slots2):
                    g = n_slots1 + l * n_slots2 + s
                    sp.wait_ge(w_used, g - SLOTS + 1)
                    sp.dma_start(wring[:, g % SLOTS, :], wlayers[l, s]).then_inc(w_in[g % SLOTS], 16)
            sp.wait_ge(x_rdy, DC + 2 * DC * LAYERS)
            sp.dma_start(out, hT[:]).then_inc(stored, 16)
            sp.wait_ge(stored, 16)

        @block.gpsimd
        def _(pool):
            pool.dma_start(csil, crow.partition_broadcast(P)).then_inc(c_in, 16)
            pool.wait_ge(mod_used, 1)
            pool.memset(xr[:, :, 0:CONV_W - 1], 0.0).then_inc(pad_rdy, 1)
            pool.memset(zeros[:], 0).then_inc(pool_step, 1)
            pool.wait_ge(pool_step, 1)
            pool.dma_start(table.rearrange("(p b) o -> p (b o)", p=P), zeros[:]).then_inc(table_clear, 16)
            pool.dma_start(browS, brow).then_inc(brow_in, 16)
            def better_root(n):
                step = lambda ins: after(pool, ins, pool_fix, "pfix")
                r, e = lru_t[:, n % 2, 0, :], lru_t[:, n % 2, 1, :]
                pool.wait_ge(root_sq, n + 1)
                step(pool.tensor_tensor(e, xr[:, n, 0:SEQ], e, ALU.subtract))
                pool.wait_ge(half_inv, n + 1)
                step(pool.tensor_tensor(e, e, sqb[:, n % 2, :], ALU.mult))
                pool.tensor_tensor(r, r, e, ALU.add).then_inc(root_fixed, 1)
            between = one["ckv"] // CHUNKS + 2
            for slot in range(n_slots1):
                for n in {between: (0, 1), between + 1: (2, 3), between + 2: (4, 5, 6), between + 3: (7, 8), between + 4: (9,)}.get(slot, ()):
                    better_root(n)
                weights_lo(pool, slot)
            pool.wait_ge(tix_rdy, 1)
            pool.wait_ge(table_clear, 16)
            for k in range(2):
                for r in range(NQB):
                    c = k * NQB + r
                    pool.indirect_dma_start(table, bass.IndirectOffsetOnAxis(ap=tixI[:, c:c + 1], axis=0),
                                            tokI[:, r:r + 1], None).then_inc(table_set, 16)
            pool.wait_ge(table_set, 16 * 2 * NQB)
            pool.dma_start(ids[:], table.rearrange("(p b) o -> p (b o)", p=P)).then_inc(ids_in, 16)
            pool.wait_ge(ids_in, 16)
            pool.wait_ge(u_stored, 16 * NQB)
            def rows_in(blocks):
                for j in range(2):
                    pool.wait_ge(y_stored[j], 16 * (blocks // 2))
                for r in range(NQB):
                    for k in range(2):
                        c = k * NQB + r
                        pool.indirect_dma_start(y_tok[:, k, r, :], None, y_rows[0:blocks * P, :],
                                                bass.IndirectOffsetOnAxis(ap=destI[:, c:c + 1], axis=0)).then_inc(rows_back[r], 16)

            def gather(b):
                if b >= 2:
                    pool.wait_ge(xt_full, b - 1)
                pool.indirect_dma_start(xs[:, b % 2, :], None, u_rows, bass.IndirectOffsetOnAxis(ap=ids[:, b:b + 1], axis=0)
                                        ).then_inc(xs_in[b % 2], 16)

            for b in range(MOE_SURE):
                gather(b)
            pool.wait_ge(route_rdy, 1)
            over = pool.value_load(overI[0:1, 0:1], min_val=0, max_val=1)
            with pool.If(over):
                for b in range(MOE_SURE, MOE_BLOCKS):
                    gather(b)
                rows_in(MOE_BLOCKS)
            with pool.Else():
                rows_in(MOE_SURE)
            pool.wait_ge(h2_rdy, DC)
            pool.dma_start(lamS[:], lamv.partition_broadcast(P)).then_inc(lam_in, 16)
            for l in range(LAYERS):
                def table_in(h):
                    k = l * HEADS + h
                    if h >= 2:
                        pool.wait_ge(near_rdy, k - 1)
                    pool.dma_start(rp[:, h % 2, :], rpb[l, h]).then_inc(rp_in, 16)

                def near_bias(h):
                    k = l * HEADS + h
                    pool.wait_ge(rp_in, 16 * (k + 1))
                    if h + 1 < HEADS:
                        table_in(h + 1)
                    if h >= 2:
                        pool.wait_ge(mx_rdy, U_DSA + l * U_LAYER + 4 * (h - 1))
                    m = K("na_mask").rearrange("p (t c) -> p t c", c=16)
                    i0 = 0
                    for n, (lo, hi) in enumerate(NA_KEYS):
                        w = hi - lo
                        ins = pool.tensor_tensor(
                            near[:, h % 2, i0 * P:(i0 + w) * P].rearrange("p (t r c) -> p t r c", r=GRID_ROWS, c=16),
                            rp[:, h % 2, (lo - n + 1) * P:(hi - n + 1) * P].rearrange("p (t r c) -> p t r c", r=GRID_ROWS, c=16),
                            m[:, i0:i0 + w, :].unsqueeze(2).broadcast_to((P, w, GRID_ROWS, 16)), ALU.add)
                        i0 += w
                    ins.then_inc(near_rdy, 1)

                attention = two["na_gb"] // CHUNKS
                for slot in range(n_slots2):
                    if slot == 3:
                        pool.wait_ge(x_rdy, DC + 2 * DC * l)
                        table_in(0)
                    if slot in (4, 5):
                        near_bias(slot - 4)
                    if slot == attention + 2:
                        for h in range(2, HEADS):
                            near_bias(h)
                    weights_lo(pool, n_slots1 + l * n_slots2 + slot)

        @block.scalar
        def _(act):
            act.wait_ge(c_in, 16)
            act.activation(csil, csil, ACT.Silu).then_inc(c_silu, 1)
            act.wait_ge(vec_in, 16)
            act.activation(s_abs, V("lam"), ACT.Abs).then_inc(sp_rdy, 1)
            act.wait_ge(x_in, 16)
            squares(act, hT, DC)
            weights_hi(act, one["xr"], 0)
            root(act)
            norm_hi(act, (mod, 1))
            for n in range(RC):
                weights_hi(act, one["xr"] + n * DC)
                act.activation(xr[:, n, CONV_W - 1:CONV_W - 1 + SEQ], A.take(act), ACT.Copy).then_inc(A.free, 1)
            def decay(n):
                act.wait_ge(gate_s, n + 1)
                act.activation(xr[:, n, 0:SEQ], lru_a[:, n, :], ACT.Tanh, scale=0.5).then_inc(gate_t, 1)
            for n in range(RC):
                weights_hi(act, one["rg"] + 2 * n)
                if n >= 2:
                    act.wait_ge(gated_x, n - 1)
                act.activation(lru_t[:, n % 2, 0, :], A.take(act), ACT.Sigmoid, bias=V("b_rg_a")[:, n:n + 1]).then_inc(A.free, 1)
                act.activation(lru_t[:, n % 2, 1, :], A.take(act), ACT.Tanh, scale=0.5, bias=hbx[:, n:n + 1]).then_inc(A.free, 1)
                if n >= 1:
                    decay(n - 1)
            decay(RC - 1)
            act.wait_ge(gate_t, RC)
            for n in range(RC):
                act.activation(lru_a[:, n, :], lru_a[:, n, :], ACT.Exp, scale=-1.0).then_inc(decay_rdy, 1)
            def square_root(n):
                act.wait_ge(gated_x, RC)
                if n >= 2:
                    act.wait_ge(h_rdy, n - 1)
                act.activation(lru_t[:, n % 2, 0, :], xr[:, n, 0:SEQ], ACT.Sqrt).then_inc(lru_sqrt, 1)
                act.wait_ge(lru_sqrt, n + 1)
                act.activation(lru_t[:, n % 2, 1, :], lru_t[:, n % 2, 0, :], ACT.Square).then_inc(root_sq, 1)

            def gelu(n):
                weights_hi(act, one["gr"] + n * DC)
                if n >= 2:
                    act.wait_ge(gh_rdy, n - 1)
                act.activation(lru_t[:, n % 2, 2, :], A.take(act), ACT.Gelu_apprx_tanh).then_inc(A.free, 1)
            parts = [(ckv[:, c, :], SEQ, 1.0) for c in range(KVC)] + [(qi[:, m, :], SEQ, 1.0) for m in range(4)]
            parts += [(ki[:], SEQ, 1.0), (wi_s, NQB * IDX_HEADS, IDX_SCALE)]
            for n, (to, width, scale) in enumerate(parts):
                square_root(n)
                weights_hi(act, one["ckv"] + n * DC)
                act.activation(to, A.take(act)[:, 0:width], ACT.Copy, scale=scale).then_inc(A.free, 1)
            act.wait_ge(A.free, A.took)
            for n in range(RC):
                if len(parts) + n < RC:
                    square_root(len(parts) + n)
                gelu(n)
            squares(act, ckv, KVC)
            root(act)
            act.wait_ge(gh_rdy, RC)
            for m in range(2 * DC):
                weights_hi(act, one[f"mg{m // 2}"] + (m % 2) * DC)
                to = mixT if m < DC else gb
                act.activation(to[:, m % DC, :], A.take(act), ACT.Sigmoid).then_inc(A.free, 1)
            act.wait_ge(ckv_rdy, KVC)
            k = 0
            for qb in range(NQB):
                for h in range(IDX_HEADS):
                    act.wait_ge(ix_score, k + 1)
                    if k >= 2:
                        act.wait_ge(ix_acc, k - 1)
                    n = (qb + 1) * P
                    act.activation(rel[:, k % 2, 0:n], ps[:, 4 + k % 2, 0:n], ACT.Relu).then_inc(ix_rel, 1)
                    k += 1
            for h in range(HEADS):
                weights_hi(act, one["q"] + h * DC)
                act.activation(qT[:, h, :], A.take(act), ACT.Copy).then_inc(A.free, 1)
            weights_hi(act, one["uk"])
            for h in range(HEADS):
                act.activation(kT[:, h, :], A.take(act), ACT.Copy).then_inc(A.free, 1)
            for s in range(NQB):
                for n in range(2):
                    act.activation(vS[:, s, n * SEQ:(n + 1) * SEQ], A.take(act), ACT.Copy).then_inc(A.free, 1)

            def att_out(u):
                b = A.take(act)
                act.activation(a_hi[:, u["h"], :], b, ACT.Copy)
                act.activation(qT[:, u["h"], :], b, ACT.Copy).then_inc(A.free, 1)
            units_act(act, dsa, att_out)
            for c in range(one["att_out"], one["router"], CHUNKS):
                weights_hi(act, c)
            squares(act, hT, DC, lambda c: act.wait_ge(h1_rdy, c + 1))
            root(act)
            for r in range(NQB):
                for n in range(2):
                    act.activation(u_tok[:, r, n * SEQ:(n + 1) * SEQ], A.take(act), ACT.Copy).then_inc(A.free, 1)
            act.wait_ge(gl_diff, 1)
            act.activation(T("ge"), T("gd"), ACT.Exp).then_inc(gl_exp, 1)
            act.wait_ge(e_diff, 1)
            act.activation(T("ex"), T("d"), ACT.Exp).then_inc(e_exp, 1)

            def part(b, k):
                act.wait_ge(part_in[k], 16 * b + 16)
                act.activation(mring_hi[:, k, :], mring[:, k, :], ACT.Copy).then_inc(part_hi, 1)

            def block_x(b, j):
                act.wait_ge(xt_full, b + 1)
                act.activation(xsT_hi[:, j, 0:4, :], ps[:, 0, :].rearrange("p (c n) -> p c n", n=P), ACT.Copy)
                act.activation(xsT_hi[:, j, 4:8, :], ps[:, 1, :].rearrange("p (c n) -> p c n", n=P), ACT.Copy).then_inc(xs_hi, 1)

            def block_act(i, j, last=False):
                b = 2 * i + j
                act.wait_ge(gate_full, b + 1)
                if not (isinstance(b, int) and b == 0):
                    act.wait_ge(hid_done, b)
                act.activation(sil[:], ps[:, 2, :], ACT.Silu).then_inc(sil_done, 1)
                part(b, 4)
                part(b, 5)
                act.wait_ge(ht_full, b + 1)
                act.activation(hidT_hi[:], ps[:, 4, :].rearrange("p (c n) -> p c n", n=P), ACT.Copy).then_inc(ht_hi, 1)
                if not last:
                    block_x(b + 1, 1 - j)
                    part(b + 1, 0)
                    part(b + 1, 1)
                act.wait_ge(y1_full, b + 1)
                if not (isinstance(i, int) and i == 0):
                    act.wait_ge(y_stored[j], 16 * i)
                act.activation(ysb[:, j, SEQ:], ps[:, 6, :], ACT.Copy).then_inc(y1_rdy, 1)
                act.wait_ge(y1_rdy, b + 1)
                act.wait_ge(y0_rdy, b + 1)
                act.dma_start(y_rows[bass.ds(b * P, P), :], ysb[:, j, :]).then_inc(y_stored[j], 16)
                if not last:
                    part(b + 1, 2)
                    part(b + 1, 3)

            part(0, 0)
            part(0, 1)
            block_x(0, 0)
            part(0, 2)
            part(0, 3)
            for j in range(2):
                block_act(0, j)
            with act.Fori(1, MOE_SURE // 2 - 1) as i:
                for j in range(2):
                    block_act(i, j)
            block_act(MOE_SURE // 2 - 1, 0)
            act.wait_ge(route_rdy, 1)
            over = act.value_load(overI[0:1, 0:1], min_val=0, max_val=1)
            with act.If(over):
                block_act(MOE_SURE // 2 - 1, 1)
                with act.Fori(MOE_SURE // 2, MOE_BLOCKS // 2 - 1) as i:
                    for j in range(2):
                        block_act(i, j)
                block_act(MOE_BLOCKS // 2 - 1, 0)
                block_act(MOE_BLOCKS // 2 - 1, 1, last=True)
            with act.Else():
                block_act(MOE_SURE // 2 - 1, 1, last=True)
            squares(act, hT, DC, lambda c: act.wait_ge(h2_rdy, c + 1))
            root(act)
            weights_hi(act, end1)
            squares(act, uT, DC, lambda c: act.wait_ge(centered, c + 1))
            root(act)
            norm_hi(act, (V("ln_in_b"), 0))
            act.wait_ge(lam_sum, 1)
            act.activation(lam_two[:, 0:4], lam_prod[:, 0:4], ACT.Exp).then_inc(lam_exp, 1)
            act.wait_ge(x_rdy, DC)
            for l in range(LAYERS):
                layer_act(act, l)

        @block.vector
        def _(dve):
            dve.wait_ge(vec_in, 16)
            step = lambda ins: after(dve, ins, dve_step, "dstep")
            dve.wait_ge(c_silu, 1)

            def mod_tile(w, m):
                return dve.scalar_tensor_tensor(out=w, in0=w, scalar=1.0, in1=csil, op0=ALU.mult, op1=ALU.mult, accum_out=mod[:, m:m + 1])
            for m in range(MOD_FIRST):
                if m == MOD_FIRST // 2:
                    sum_squares(dve, DC)
                if m % 4 == 0:
                    dve.wait_ge(mod_in[m // 4], 16)
                ins = mod_tile(wmodS[:, m, :], m)
            ins.then_inc(mod_used, 1)
            dve.wait_ge(mod_used, 1)
            step(dve.tensor_tensor(mod[:, 0:16], mod[:, 0:16], V("b_mod")[:, 0:16], ALU.add))
            dve.scalar_tensor_tensor(out=a1, in0=mod[:, 8:16], scalar=1.0, in1=V("norm1_g"), op0=ALU.add, op1=ALU.mult).then_inc(a_coef, 1)
            dve.wait_ge(a_coef, 1)
            inverse_var(dve, D, EPS)
            scale_split(dve, hT, 1, a1, mod, u_rdy)
            dve.tensor_scalar(hbx, V("b_rg_x"), 0.5, None, ALU.mult)
            after(dve, dve.tensor_scalar(hsp, V("lam"), -1.0, 0.0, ALU.mult, ALU.max), dve_step, "dstep")
            dve.wait_ge(sp_rdy, 1)
            step(dve.tensor_scalar(s_abs, s_abs, 87.0, None, ALU.min))
            step(dve.tensor_scalar(s_int, s_abs, 1.0 / math.log(2.0), None, ALU.mult))
            step(dve.tensor_copy(s_z, s_int))
            step(dve.scalar_tensor_tensor(out=s_abs, in0=s_z, scalar=-LN2_HI, in1=s_abs, op0=ALU.mult, op1=ALU.add))
            step(dve.scalar_tensor_tensor(out=s_abs, in0=s_z, scalar=LN2_HI - math.log(2.0), in1=s_abs, op0=ALU.mult, op1=ALU.add))
            step(dve.tensor_scalar(s_int, s_z, -float(2 ** 23), 127.0 * 2 ** 23, ALU.mult, ALU.add))
            step(dve.tensor_scalar(s_zz, s_abs, -1.0 / 10.0, 1.0, ALU.mult, ALU.add))
            for k in range(9, 0, -1):
                step(dve.scalar_tensor_tensor(out=s_zz, in0=s_abs, scalar=-1.0 / k, in1=s_zz, op0=ALU.mult, op1=ALU.mult))
                step(dve.tensor_scalar(s_zz, s_zz, 1.0, None, ALU.add))
            step(dve.tensor_tensor(s_abs, s_zz, s_int.bitcast(F32), ALU.mult))
            step(dve.tensor_scalar(s_z, s_abs, 2.0, None, ALU.add))
            step(dve.reciprocal(s_z, s_z))
            step(dve.tensor_tensor(s_z, s_z, s_abs, ALU.mult))
            step(dve.tensor_tensor(s_zz, s_z, s_z, ALU.mult))
            step(dve.tensor_scalar(s_abs, s_zz, 1.0 / 19.0, None, ALU.mult))
            for k in range(17, 1, -2):
                step(dve.scalar_tensor_tensor(out=s_abs, in0=s_abs, scalar=1.0 / k, in1=s_zz, op0=ALU.add, op1=ALU.mult))
            step(dve.scalar_tensor_tensor(out=s_abs, in0=s_abs, scalar=1.0, in1=s_z, op0=ALU.add, op1=ALU.mult))
            step(dve.scalar_tensor_tensor(out=hsp, in0=s_abs, scalar=2.0, in1=hsp, op0=ALU.mult, op1=ALU.add))
            after(dve, dve.tensor_scalar(hsp, hsp, LRU_C, None, ALU.mult), dve_step, "dstep")
            cw, cb = V("conv_w"), V("conv_b")
            dve.wait_ge(pad_rdy, 1)
            for n in range(RC):
                dve.wait_ge(A.free, n + 1)
                after(dve, dve.tensor_scalar(rnn[:, n, :], xr[:, n, 0:SEQ], cw[:, n:n + 1], cb[:, n:n + 1], ALU.mult, ALU.add), dve_step, "dstep")
                for w in range(1, CONV_W):
                    ins = dve.scalar_tensor_tensor(out=rnn[:, n, :], in0=xr[:, n, w:w + SEQ], scalar=cw[:, w * RC + n:w * RC + n + 1],
                                                   in1=rnn[:, n, :], op0=ALU.mult, op1=ALU.add)
                    if w < CONV_W - 1:
                        after(dve, ins, dve_step, "dstep")
                ins.then_inc(conv_rdy, 1)
            for n in range(RC):
                t = lru_t[:, n % 2]
                dve.wait_ge(A.free, RC + 2 * n + 2)
                dve.tensor_scalar(lru_a[:, n, :], t[:, 0, :], hsp[:, n:n + 1], 2e-30, ALU.mult, ALU.max).then_inc(gate_s, 1)
                after(dve, dve.tensor_scalar(t[:, 1, :], t[:, 1, :], 0.5, 0.5, ALU.mult, ALU.add), dve_step, "dstep")
                dve.tensor_tensor(rnn[:, n, :], rnn[:, n, :], t[:, 1, :], ALU.mult).then_inc(gated_x, 1)
            dve.wait_ge(gated_x, RC)
            a_free_gr = RC + 2 * RC + KVC + 4 + 1 + 1

            def gated_h(n):
                dve.wait_ge(A.free, a_free_gr + n + 1)
                dve.wait_ge(h_rdy, n + 1)
                dve.tensor_tensor(rnn[:, n, :], rnn[:, n, :], lru_t[:, n % 2, 2, :], ALU.mult).then_inc(gh_rdy, 1)

            def prepare(n):
                v, a, t = sqb[:, n % 2, :], lru_a[:, n, :], xr[:, n, 0:SEQ]
                dve.wait_ge(decay_rdy, n + 1)
                step(dve.scalar_tensor_tensor(out=v, in0=a, scalar=1.0, in1=t, op0=ALU.add, op1=ALU.mult))
                step(dve.scalar_tensor_tensor(out=v, in0=a, scalar=-1.0, in1=v, op0=ALU.add, op1=ALU.add))
                step(dve.scalar_tensor_tensor(out=v, in0=a, scalar=1.0, in1=v, op0=ALU.add, op1=ALU.mult))
                step(dve.scalar_tensor_tensor(out=a, in0=v, scalar=-0.5, in1=a, op0=ALU.mult, op1=ALU.add))
                dve.wait_ge(lru_sqrt, n + 1)
                dve.tensor_scalar(v.bitcast(I32), lru_t[:, n % 2, 0, :].bitcast(I32), -1.0, float(HALF_INVERSE), ALU.mult, ALU.add).then_inc(half_inv, 1)

            def scan(n):
                r, x = lru_t[:, n % 2, 0, :], xr[:, n, 0:SEQ]
                dve.wait_ge(root_fixed, n + 1)
                step(dve.scalar_tensor_tensor(out=r, in0=lru_a[:, n, :], scalar=1.0, in1=r, op0=ALU.add, op1=ALU.mult))
                step(dve.tensor_tensor(x, r, rnn[:, n, :], ALU.mult))
                dve.tensor_tensor_scan(rnn[:, n, :], lru_a[:, n, :], x, 0.0, ALU.mult, ALU.add).then_inc(h_rdy, 1)
            prepare(0)
            for n in range(1, RC):
                prepare(n)
                scan(n - 1)
            gated_h(0)
            scan(RC - 1)
            gated_h(1)
            for n in range(2, RC):
                gated_h(n)
            sum_squares(dve, KVC)
            inverse_var(dve, KV_RANK, EPS)
            for c in range(KVC):
                dve.scalar_tensor_tensor(out=ckv[:, c, :], in0=ckv[:, c, :], scalar=V("kv_g")[:, c:c + 1], in1=rstd,
                                         op0=ALU.mult, op1=ALU.mult).then_inc(ckv_rdy, 1)
            for n in range(MOD_SLOTS):
                g = one[f"mod{n // 2}"] // CHUNKS + n % 2
                dve.wait_ge(w_in[g % SLOTS], 16 * (g // SLOTS + 1))
                for h in range(2):
                    ins = mod_tile(wring[:, g % SLOTS, h * D:(h + 1) * D], MOD_FIRST + 2 * n + h)
                ins.then_inc(mod_used, 1)
            dve.wait_ge(mod_used, 1 + MOD_SLOTS)
            step(dve.tensor_tensor(mod[:, 16:48], mod[:, 16:48], V("b_mod")[:, 16:48], ALU.add))
            dve.scalar_tensor_tensor(out=a2, in0=mod[:, 32:40], scalar=1.0, in1=V("norm2_g"), op0=ALU.add, op1=ALU.mult).then_inc(a_coef, 1)
            dve.wait_ge(table_clear, 16)
            k = 0
            for qb in range(NQB):
                o, n = qb * (qb + 1) // 2, (qb + 1) * P
                w = sel[:, o:o + qb + 1, :].rearrange("p j q -> p (j q)")
                for h in range(IDX_HEADS):
                    wt = wi_s[:, qb * IDX_HEADS + h:qb * IDX_HEADS + h + 1]
                    dve.wait_ge(ix_rel, k + 1)
                    if h == 0:
                        ins = dve.tensor_scalar(w, rel[:, k % 2, 0:n], wt, None, ALU.mult)
                    else:
                        ins = dve.scalar_tensor_tensor(out=w, in0=rel[:, k % 2, 0:n], scalar=wt, in1=w, op0=ALU.mult, op1=ALU.add)
                    ins.then_inc(ix_acc, 1)
                    k += 1
                    dve.wait_ge(ix_acc, k)
            dve.wait_ge(rest_in, 16)
            c0 = K("causal")
            after(dve, dve.tensor_scalar(sel[:, 0, :], c0, MASKED / OUT_OF_SIGHT, None, ALU.mult), dve_step, "dstep")
            for qb in range(1, NQB):
                o = qb * (qb + 1) // 2
                ins = dve.tensor_tensor(sel[:, o + qb, :], sel[:, o + qb, :], c0, ALU.add)
            after(dve, ins, dve_step, "dstep")
            works = [sel[:, qb * (qb + 1) // 2:qb * (qb + 1) // 2 + qb + 1, :].rearrange("p j q -> p (j q)") for qb in range(NQB)]
            for r in range(TOPK // 8):
                for qb in range(1, NQB):
                    ins = dve.max(max8[:, 8 * (qb - 1):8 * qb], works[qb])
                after(dve, ins, dve_step, "dstep")
                for qb in range(1, NQB):
                    ins = dve.match_replace(works[qb], max8[:, 8 * (qb - 1):8 * qb], works[qb], TAKEN)
                after(dve, ins, dve_step, "dstep")
            for qb in range(1, NQB):
                ins = dve.tensor_scalar(works[qb], works[qb], TAKEN, -1.0, ALU.is_equal, ALU.add)
            after(dve, ins, dve_step, "dstep")
            for qb in range(1, NQB):
                ins = dve.tensor_scalar(works[qb], works[qb], -MASKED, None, ALU.mult)
            after(dve, ins, dve_step, "dstep")
            for m in range(DC):
                dve.wait_ge(A.free, a_free_gr + RC + m + 1)
                dve.tensor_tensor(mixT[:, m, :], B.take(dve), mixT[:, m, :], ALU.mult).then_inc(B.free, 1)
            units_dve(dve, dsa)
            dve.wait_ge(A.free, A_ATT)
            for h in range(HEADS):
                dve.tensor_tensor(a_lo[:, h, :], qT[:, h, :], a_hi[:, h, :].bitcast(F32), ALU.subtract).then_inc(a_lo_rdy, 1)
            for m in range(DC):
                dve.tensor_tensor(gb[:, m, :], B.take(dve), gb[:, m, :], ALU.mult).then_inc(B.free, 1)
                dve.wait_ge(B.free, B.took)
                after(dve, dve.tensor_tensor(mixT[:, m, :], mixT[:, m, :], gb[:, m, :], ALU.add), dve_step, "dstep")
                after(dve, dve.tensor_copy(mix_hi[:, m, :], mixT[:, m, :]), dve_step, "dstep")
                dve.tensor_tensor(mix_lo[:, m, :], mixT[:, m, :], mix_hi[:, m, :].bitcast(F32), ALU.subtract).then_inc(mix2_rdy, 1)
            for m in range(DC):
                if m == 0:
                    dve.wait_ge(x_back, 16)
                dve.scalar_tensor_tensor(out=hT[:, m, :], in0=B.take(dve), scalar=mod[:, 16 + m:17 + m], in1=xS[:, m, :],
                                         op0=ALU.mult, op1=ALU.add).then_inc(h1_rdy, 1)
                free_bank_b(dve)
            sum_squares(dve, DC)
            inverse_var(dve, D, EPS)
            for c in range(DC):
                after(dve, dve.scalar_tensor_tensor(out=uT[:, c, :], in0=hT[:, c, :], scalar=a2[:, c:c + 1], in1=rstd,
                                                    op0=ALU.mult, op1=ALU.mult), dve_step, "dstep")
                dve.tensor_scalar(uT[:, c, :], uT[:, c, :], mod[:, 24 + c:25 + c], None, ALU.add).then_inc(u_rdy, 1)
            step = lambda ins: after(dve, ins, dve_step, "dstep")
            TT, TS, STT = dve.tensor_tensor, dve.tensor_scalar, dve.scalar_tensor_tensor
            lg = T("lg").rearrange("p (s n) -> p s n", n=GROUPS + EXPERTS)
            dve.tensor_copy(T("lg"), B.take(dve)[:, 0:NQB * (GROUPS + EXPERTS)]).then_inc(B.free, 1)
            dve.wait_ge(B.free, B.took)
            gl, el = lg[:, :, 0:GROUPS], lg[:, :, GROUPS:]

            def four(t, n):
                return T(t)[:, 0:NQB * n].rearrange("p (s n) -> p s n", n=n)

            def best(values, n, m, pick):
                step(dve.reduce_max(T(m), values, AX_X))
                w = four("w", n)
                step(TT(w, values, T(m).unsqueeze(2).broadcast_to((P, NQB, n)), ALU.is_equal))
                step(TT(w, w, K("first")[:, 0:n].unsqueeze(1).broadcast_to((P, NQB, n)), ALU.mult))
                step(dve.reduce_max(T("wm"), w, AX_X))
                step(TT(four(pick, n), w, T("wm").unsqueeze(2).broadcast_to((P, NQB, n)), ALU.is_equal))

            best(gl, GROUPS, "gmax", "goh")
            TT(four("gd", GROUPS), gl, T("gmax").unsqueeze(2).broadcast_to((P, NQB, GROUPS)), ALU.subtract).then_inc(gl_diff, 1)
            prod = big[:, 0:NQB * EXPERTS].rearrange("p (s e g) -> p s e g", s=NQB, g=GROUPS)
            goh = four("goh", GROUPS)
            step(TT(prod, el.rearrange("p s (g e) -> p s e g", g=GROUPS), goh.unsqueeze(2).broadcast_to((P, NQB, PER_GROUP, GROUPS)), ALU.mult))
            es = four("es", PER_GROUP)
            step(dve.reduce_sum(es, prod, AX_X))
            best(es, PER_GROUP, "m1", "oh1")
            step(STT(out=es, in0=four("oh1", PER_GROUP), scalar=TAKEN, in1=es, op0=ALU.mult, op1=ALU.add))
            best(es, PER_GROUP, "m2", "oh2")
            TT(T("d"), T("m2"), T("m1"), ALU.subtract).then_inc(e_diff, 1)
            dve.wait_ge(gl_exp, 1)
            step(dve.reduce_sum(T("gw"), four("ge", GROUPS), AX_X))
            dve.wait_ge(e_exp, 1)
            step(TS(T("p1"), T("ex"), 1.0, None, ALU.add))
            step(TT(T("p1"), T("p1"), T("gw"), ALU.mult))
            step(dve.reciprocal(gate12[:, 0:NQB], T("p1")))
            TT(gate12[:, NQB:], gate12[:, 0:NQB], T("ex"), ALU.mult)
            for name, oh in (("M1", "oh1"), ("M2", "oh2")):
                ins = TT(T(name).rearrange("p (s g e) -> p s g e", s=NQB, e=PER_GROUP),
                         goh.unsqueeze(3).broadcast_to((P, NQB, GROUPS, PER_GROUP)),
                         four(oh, PER_GROUP).unsqueeze(2).broadcast_to((P, NQB, GROUPS, PER_GROUP)), ALU.mult)
            step(ins)
            TT(T("M"), T("M1"), T("M2"), ALU.add).then_inc(ohot, 1)
            b = B.take(dve)
            pos, cts = T("pos"), T("cts")
            dve.tensor_copy(pos, b[:, 0:NQB * EXPERTS])
            dve.tensor_copy(cts, b[:, NQB * EXPERTS:(NQB + 1) * EXPERTS]).then_inc(B.free, 1)
            dve.wait_ge(B.free, B.took)
            step(TS(T("nb"), cts, 0.0, None, ALU.is_gt))
            for lim in (P, 2 * P, 3 * P):
                step(STT(out=T("nb"), in0=cts, scalar=float(lim), in1=T("nb"), op0=ALU.is_gt, op1=ALU.add))
            step(dve.tensor_tensor_scan(T("cum"), ones[:, 0:EXPERTS], T("nb"), 0.0, ALU.mult, ALU.add))
            dve.tensor_tensor(T("st"), T("cum"), T("nb"), ALU.subtract)
            step(TS(T("bq"), pos, float(P), None, ALU.is_ge))
            for lim in (2 * P, 3 * P):
                step(STT(out=T("bq"), in0=pos, scalar=float(lim), in1=T("bq"), op0=ALU.is_ge, op1=ALU.add))
            step(STT(out=pos, in0=T("bq"), scalar=float(-P), in1=pos, op0=ALU.mult, op1=ALU.add))
            v3 = lambda t: T(t).rearrange("p (s e) -> p s e", e=EXPERTS)
            step(TT(v3("bq"), v3("bq"), T("st").unsqueeze(1).broadcast_to((P, NQB, EXPERTS)), ALU.add))
            TS(T("tix"), pos, float(MOE_BLOCKS + 1), None, ALU.mult)
            step(STT(out=pos, in0=T("bq"), scalar=float(P), in1=pos, op0=ALU.mult, op1=ALU.add))
            step(TT(T("tix"), T("tix"), T("bq"), ALU.add))
            for k, M in enumerate(("M1", "M2")):
                for t, to in (("tix", tixI), ("pos", destI)):
                    step(TT(T("bq"), T(M), T(t), ALU.mult))
                    step(dve.reduce_sum(T("ix"), v3("bq"), AX_X))
                    step(dve.tensor_copy(to[:, k * NQB:(k + 1) * NQB], T("ix")))
            dve.tensor_copy(tokI[:], K("token")).then_inc(tix_rdy, 1)
            bb = big[:].rearrange("p (b e) -> p b e", e=EXPERTS)
            step(TT(bb, T("cum").unsqueeze(1).broadcast_to((P, MOE_BLOCKS, EXPERTS)),
                    K("block").unsqueeze(2).broadcast_to((P, MOE_BLOCKS, EXPERTS)), ALU.is_le))
            step(dve.reduce_sum(T("be"), bb, AX_X))
            step(TS(T("be"), T("be"), float(EXPERTS - 1), None, ALU.min))
            step(TS(T("d")[:, 0:1], T("cum")[:, EXPERTS - 1:EXPERTS], float(MOE_SURE), None, ALU.is_gt))
            step(dve.tensor_copy(overI[:], T("d")[:, 0:1]))
            dve.tensor_copy(bexpI[:], T("be")).then_inc(route_rdy, 1)
            dve.wait_ge(route_rdy, 1)
            over = dve.value_load(overI[0:1, 0:1], min_val=0, max_val=1)

            def part(b, n):
                dve.wait_ge(part_hi, 6 * b + n + 1)
                dve.tensor_tensor(mring_lo[:, n, :], mring[:, n, :], mring_hi[:, n, :].bitcast(F32), ALU.subtract).then_inc(part_lo, 1)

            def block_x(b, j):
                dve.wait_ge(xs_hi, b + 1)
                dve.tensor_tensor(xsT_lo[:, j, :, :], ps[:, 0:2, :].rearrange("p a (c n) -> p (a c) n", n=P),
                                  xsT_hi[:, j, :, :].bitcast(F32), ALU.subtract).then_inc(xs_lo, 1)

            def block_dve(i, j, last=False):
                b = 2 * i + j
                part(b, 4)
                dve.wait_ge(up_full, b + 1)
                dve.wait_ge(sil_done, b + 1)
                dve.tensor_tensor(hid[:], ps[:, 3, :], sil[:], ALU.mult).then_inc(hid_done, 1)
                part(b, 5)
                dve.wait_ge(ht_hi, b + 1)
                dve.tensor_tensor(hidT_lo[:], ps[:, 4, :].rearrange("p (c n) -> p c n", n=P), hidT_hi[:].bitcast(F32),
                                  ALU.subtract).then_inc(ht_lo, 1)
                if not last:
                    block_x(b + 1, 1 - j)
                    part(b + 1, 0)
                    part(b + 1, 1)
                dve.wait_ge(y0_full, b + 1)
                if not (isinstance(i, int) and i == 0):
                    dve.wait_ge(y_stored[j], 16 * i)
                dve.tensor_copy(ysb[:, j, 0:SEQ], ps[:, 5, :]).then_inc(y0_rdy, 1)
                if not last:
                    part(b + 1, 2)
                    part(b + 1, 3)

            part(0, 0)
            part(0, 1)
            block_x(0, 0)
            part(0, 2)
            part(0, 3)
            for j in range(2):
                block_dve(0, j)
            with dve.Fori(1, MOE_SURE // 2 - 1) as i:
                for j in range(2):
                    block_dve(i, j)
            block_dve(MOE_SURE // 2 - 1, 0)
            with dve.If(over):
                block_dve(MOE_SURE // 2 - 1, 1)
                with dve.Fori(MOE_SURE // 2, MOE_BLOCKS // 2 - 1) as i:
                    for j in range(2):
                        block_dve(i, j)
                block_dve(MOE_BLOCKS // 2 - 1, 0)
                block_dve(MOE_BLOCKS // 2 - 1, 1, last=True)
            with dve.Else():
                block_dve(MOE_SURE // 2 - 1, 1, last=True)
            for r in range(NQB):
                dve.wait_ge(rows_back[r], 32)
                step(TS(y_tok[:, 0, r, :], y_tok[:, 0, r, :], gate12[:, r:r + 1], None, ALU.mult))
                STT(out=y_tok[:, 0, r, :], in0=y_tok[:, 1, r, :], scalar=gate12[:, NQB + r:NQB + r + 1], in1=y_tok[:, 0, r, :],
                    op0=ALU.mult, op1=ALU.add).then_inc(mixed_rows, 1)
            for c in range(DC):
                STT(out=hT[:, c, :], in0=B.take(dve), scalar=mod[:, 40 + c:41 + c], in1=hT[:, c, :],
                    op0=ALU.mult, op1=ALU.add).then_inc(h2_rdy, 1)
                free_bank_b(dve)
            sum_squares(dve, DC)
            inverse_var(dve, D, EPS)
            for c in range(DC):
                STT(out=uT[:, c, :], in0=hT[:, c, :], scalar=V("final_g")[:, c:c + 1], in1=rstd, op0=ALU.mult, op1=ALU.mult).then_inc(b1_rdy, 1)
            dve.wait_ge(b1_rdy, DC)
            for c in range(1, DC):
                add_up(dve, uT, c)
            center(dve, uT)
            normed_split(dve, uT, 0, V("ln_in_g"), V("ln_in_b"), turn=True)
            dve.wait_ge(late_in, 16)
            dve.wait_ge(lam_in, 16)
            lv = lamS[:].rearrange("p (l a d) -> p l a d", l=LAYERS, a=4)
            step(TT(lv[:, :, 0:4:2, :], lv[:, :, 0:4:2, :], lv[:, :, 1:4:2, :], ALU.mult))
            dve.reduce_sum(lam_prod[:, 0:4].rearrange("p (l a) -> p l a", a=2), lv[:, :, 0:4:2, :], AX_X).then_inc(lam_sum, 1)
            dve.wait_ge(lam_exp, 1)
            for l in range(LAYERS):
                init = 0.8 - 0.6 * math.exp(-0.3 * l)
                step(TT(lam_neg[:, l:l + 1], lam_two[:, 2 * l + 1:2 * l + 2], lam_two[:, 2 * l:2 * l + 1], ALU.subtract))
                step(TS(lam_neg[:, l:l + 1], lam_neg[:, l:l + 1], -init, None, ALU.add))
                step(TS(subg[:, l:l + 1], V(f"subln{l}"), 1.0 - init, None, ALU.mult))
            for l in range(LAYERS):
                layer_dve(dve, l)

        @block.tensor
        def _(pe):
            pe.wait_ge(const_in, 16)
            norm_pe(pe, DC)
            u = x_hi, x_lo[1]
            for n in range(RC):
                tile3(pe, A.claim(pe), one["xr"] + n * DC, *u, DC, wait=(lambda k: pe.wait_ge(u_rdy, k + 1)) if n == 0 else None).then_inc(A.full, 1)
            for n in range(RC):
                pe.wait_ge(conv_rdy, n + 1)
                for g in range(2):
                    b = A.claim(pe)
                    w = chunk(pe, one["rg"] + 2 * n + g)
                    said(pe.matmul(b[:, 0:SEQ // 2], w, rnn[:, n, 0:SEQ // 2], start=True, stop=True))
                    pe.matmul(b[:, SEQ // 2:], w, rnn[:, n, SEQ // 2:], start=True, stop=True).then_inc(A.full, 1)
            for m in range(KVC):
                tile3(pe, A.claim(pe), one["ckv"] + m * DC, *u, DC).then_inc(A.full, 1)
            for m in range(4):
                tile3(pe, A.claim(pe), one["qi"] + m * DC, *u, DC).then_inc(A.full, 1)
            tile3(pe, A.claim(pe), one["ki"], *u, DC).then_inc(A.full, 1)
            b = A.claim(pe)
            w = chunk(pe, one["wi"])
            for s in range(NQB):
                o = b[:, s * IDX_HEADS:(s + 1) * IDX_HEADS]
                for k in range(DC):
                    (xh, xl), (wh, wl) = (x[:, k, s * P:(s + 1) * P] for x in u), (x[:, k * IDX_HEADS:(k + 1) * IDX_HEADS] for x in w)
                    said(pe.matmul(o, xh, wh, start=(k == 0), stop=False))
                    pe.matmul(o, xh, wl, start=False, stop=False)
                    ins = pe.matmul(o, xl, wh, start=False, stop=(k == DC - 1))
            ins.then_inc(A.full, 1)
            for m in range(RC):
                tile3(pe, A.claim(pe), one["gr"] + m * DC, *u, DC).then_inc(A.full, 1)
            norm_pe(pe, KVC)
            for m in range(2 * DC):
                tile3(pe, A.claim(pe), one[f"mg{m // 2}"] + (m % 2) * DC, *u, DC).then_inc(A.full, 1)
            k = 0
            for qb in range(NQB):
                for h in range(IDX_HEADS):
                    r = 64 * (h % 2)
                    if k >= 2:
                        pe.wait_ge(ix_rel, k - 1)
                    pe.matmul(ps[:, 4 + k % 2, 0:(qb + 1) * P], qi[r:r + 64, h // 2, qb * P:(qb + 1) * P],
                              ki[r:r + 64, 0:(qb + 1) * P], start=True, stop=True).then_inc(ix_score, 1)
                    k += 1
            for m in range(HEADS):
                tile3(pe, A.claim(pe), one["q"] + m * DC, *u, DC).then_inc(A.full, 1)
            pe.wait_ge(gh_rdy, RC)
            for m in range(DC):
                tile(pe, B.claim(pe), one["rnn_out"] + m * RC, rnn, RC).then_inc(B.full, 1)
            pe.wait_ge(ckv_rdy, KVC)
            for m in range(HEADS):
                tile(pe, A.claim(pe), one["uk"] + m * KVC, ckv, KVC).then_inc(A.full, 1)
            for s in range(NQB):
                for n in range(2):
                    b = A.claim(pe)
                    for k in range(KVC):
                        w = chunk(pe, one["uv"] + (2 * k + n) * 4, 4)
                        ins = pe.matmul(b, ckv[:, k, s * P:(s + 1) * P], w, start=(k == 0), stop=(k == KVC - 1))
                        if k < KVC - 1:
                            said(ins)
                    ins.then_inc(A.full, 1)
            units_pe(pe, dsa, lambda i: (pe.wait_ge(ix_rel, NQB * IDX_HEADS), pe.wait_ge(A.free, A.made)) if i == 0 else None)
            for m in range(DC):
                tile3(pe, B.claim(pe), one["att_out"] + m * DC, a_hi, a_lo, DC,
                      wait=(lambda k: pe.wait_ge(a_lo_rdy, k + 1)) if m == 0 else None).then_inc(B.full, 1)
            pe.wait_ge(mix2_rdy, DC)
            for m in range(DC):
                tile3(pe, B.claim(pe), one["out"] + m * DC, mix_hi, mix_lo, DC).then_inc(B.full, 1)
            norm_pe(pe, DC)
            assert A.made == A_ROWS
            b = B.claim(pe)
            w = chunk(pe, one["router"], 3)
            N = GROUPS + EXPERTS
            pe.wait_ge(brow_in, 16)
            for r in range(NQB):
                for k in range(DC):
                    if r == 0:
                        pe.wait_ge(u_rdy, DC + k + 1)
                    said(pe.matmul(b[:, r * N:(r + 1) * N], uT[:, k, r * P:(r + 1) * P], w[:, k * N:(k + 1) * N], start=(k == 0), stop=False))
                ins = pe.matmul(b[:, r * N:(r + 1) * N], ones[0:1, :], browS, start=False, stop=True)
            ins.then_inc(B.full, 1)
            for r in range(NQB):
                for n in range(2):
                    b = A.claim(pe)
                    for c in range(4):
                        ins = pe.transpose(b[:, c * P:(c + 1) * P], uT[:, 4 * n + c, r * P:(r + 1) * P], ident)
                    ins.then_inc(A.full, 1)
            pe.wait_ge(ohot, 1)
            b = B.claim(pe)
            M = T("M").rearrange("p (s e) -> p s e", e=EXPERTS)
            for r in range(NQB):
                pe.matmul(b[:, r * EXPERTS:(r + 1) * EXPERTS], K("tri"), M[:, r, :], start=True, stop=(r == 0))
                for q in range(r):
                    pe.matmul(b[:, r * EXPERTS:(r + 1) * EXPERTS], ones, M[:, q, :], start=False, stop=(q == r - 1))
            for q in range(NQB):
                ins = pe.matmul(b[:, NQB * EXPERTS:(NQB + 1) * EXPERTS], ones, M[:, q, :], start=(q == 0), stop=(q == NQB - 1))
            ins.then_inc(B.full, 1)
            pe.wait_ge(A.free, A.made)
            pe.wait_ge(B.free, B.made)
            pe.transpose(ps[:, 7, 0:P], ident, ident).then_inc(moe_go, 1)

            def block_x(i, b, j):
                pe.wait_ge(xs_in[j], 16 * i + 16)
                if not (isinstance(b, int) and b == 0):
                    pe.wait_ge(xs_lo, b)
                for c in range(DC):
                    ins = pe.transpose(ps[:, c // 4, (c % 4) * P:(c % 4 + 1) * P], xs[:, j, c * P:(c + 1) * P], ident)
                ins.then_inc(xt_full, 1)

            def three(out, xh, xl, wh, wl, first, last):
                pe.matmul(out, xh, wh, start=first, stop=False)
                pe.matmul(out, xh, wl, start=False, stop=False)
                return pe.matmul(out, xl, wh, start=False, stop=last)

            def block_pe(i, j, last=False):
                b = 2 * i + j
                pe.wait_ge(xs_lo, b + 1)
                for w, full in enumerate((gate_full, up_full)):
                    for k in range(DC):
                        h, o = 2 * w + k // 4, (k % 4) * SEQ
                        if k % 4 == 0:
                            pe.wait_ge(part_lo, 6 * b + h + 1)
                        ins = three(ps[:, 2 + w, :], xsT_hi[:, j, k, :], xsT_lo[:, j, k, :], mring_hi[:, h, o:o + SEQ],
                                    mring_lo[:, h, o:o + SEQ], k == 0, k == DC - 1)
                    ins.then_inc(full, 1)
                pe.wait_ge(hid_done, b + 1)
                for c in range(4):
                    ins = pe.transpose(ps[:, 4, c * P:(c + 1) * P], hid[:, c * P:(c + 1) * P], ident)
                ins.then_inc(ht_full, 1)
                if not last:
                    block_x(i + j, b + 1, 1 - j)
                pe.wait_ge(ht_lo, b + 1)
                for n, full in enumerate((y0_full, y1_full)):
                    if not (isinstance(b, int) and b == 0):
                        pe.wait_ge((y0_rdy, y1_rdy)[n], b)
                    for k in range(4):
                        h, o = 4 + k // 2, (k % 2) * D + n * SEQ
                        if n == 0 and k % 2 == 0:
                            pe.wait_ge(part_lo, 6 * b + h + 1)
                        ins = three(ps[:, 5 + n, :], hidT_hi[:, k, :], hidT_lo[:, k, :], mring_hi[:, h, o:o + SEQ],
                                    mring_lo[:, h, o:o + SEQ], k == 0, k == 3)
                    ins.then_inc(full, 1)

            block_x(0, 0, 0)
            for j in range(2):
                block_pe(0, j)
            with pe.Fori(1, MOE_SURE // 2 - 1) as i:
                for j in range(2):
                    block_pe(i, j)
            block_pe(MOE_SURE // 2 - 1, 0)
            pe.wait_ge(route_rdy, 1)
            over = pe.value_load(overI[0:1, 0:1], min_val=0, max_val=1)
            with pe.If(over):
                block_pe(MOE_SURE // 2 - 1, 1)
                with pe.Fori(MOE_SURE // 2, MOE_BLOCKS // 2 - 1) as i:
                    for j in range(2):
                        block_pe(i, j)
                block_pe(MOE_BLOCKS // 2 - 1, 0)
                block_pe(MOE_BLOCKS // 2 - 1, 1, last=True)
            with pe.Else():
                block_pe(MOE_SURE // 2 - 1, 1, last=True)
            pe.wait_ge(mixed_rows, NQB)
            for c in range(DC):
                b = B.claim(pe)
                for r in range(NQB):
                    ins = pe.transpose(b[:, r * P:(r + 1) * P], y_tok[:, 0, r, c * P:(c + 1) * P], ident)
                ins.then_inc(B.full, 1)
            norm_pe(pe, DC)
            mean_pe(pe)
            norm_pe(pe, DC)
            for l in range(LAYERS):
                layer_pe(pe, l)


def _columns(v):
    return v.reshape(-1, P).T


def _chunks(w, nk=None):
    k, m = w.shape
    return w.reshape(k // P, P, m // P, P).transpose(2, 0, 1, 3).reshape(-1, P, P)


def _blocks(w):
    k, m = w.shape
    return w.reshape(k // P, P, m // 512, 4, P).transpose(0, 2, 3, 1, 4).reshape(-1, P, P)


def _wide(w, width=P):
    out = np.zeros((w.shape[0], width), w.dtype)
    out[:, :w.shape[1]] = w
    return out


def _pack(w, n):
    k, m = w.shape
    a = _wide(w.reshape(k // P, P, m).transpose(1, 0, 2).reshape(P, -1), n * P)
    return a.reshape(P, n, P).transpose(1, 0, 2)


def _stream(found, size, parts):
    s = np.zeros((size, P, P), np.float32)
    for name, chunks in parts.items():
        s[found[name]:found[name] + len(chunks)] = chunks
    return np.ascontiguousarray(s.reshape(-1, CHUNKS, P, P).transpose(0, 2, 1, 3)).reshape(-1, P, CHUNKS * P)


def _constants():
    cst, n = const_plan()
    t = np.zeros((P, n), np.float32)

    def put(name, v):
        a, b = cst[name]
        t[:v.shape[0], a:b] = v.reshape(v.shape[0], -1)

    p = np.arange(P)
    put("ident", np.eye(P))
    put("ones", np.ones((P, P)))
    put("tri", p[:, None] < p[None, :])
    pos = np.arange(SEQ).reshape(GRID_ROWS, NA_TILES, 16).transpose(1, 0, 2).reshape(-1).astype(np.float32)

    def rotary(base, half, group, rows):
        cos, sin, perm = np.ones((rows, SEQ)), np.zeros((rows, SEQ)), np.zeros((rows, P))
        inv = np.exp(np.float32(-math.log(ROPE_THETA)) * np.arange(half, dtype=np.float32) / np.float32(half)).astype(np.float32)
        ang = (pos[:, None] * inv[None, :]).astype(np.float32)
        for g in range(base, rows, group):
            for j in range(half):
                cos[g + j] = cos[g + half + j] = np.cos(ang[:, j])
                sin[g + j] = sin[g + half + j] = np.sin(ang[:, j])
                perm[g + half + j, g + j] = -1.0
                perm[g + j, g + half + j] = 1.0
        return cos, sin, perm

    c, s, m = rotary(0, 8, 64, P)
    put("cos_d", c), put("sin_d", s), put("perm_d", m)
    c, s, m = rotary(64, 16, 64, MLA_QK)
    put("cos_m", c), put("sin_m", s), put("perm_m", m)
    put("dist", p[:, None] - np.arange(7 * P)[None, :] + 3 * P)
    put("causal", np.where(p[None, :] <= p[:, None], 0.0, OUT_OF_SIGHT))
    mask = np.zeros((P, 10, 16))
    i = 0
    for n_, (lo, hi) in enumerate(NA_KEYS):
        for j in range(lo, hi):
            qc = n_ * 16 + p % 16
            kc = j * 16 + np.arange(16)
            w = np.clip(qc - 8, 0, GRID_W - 16)
            mask[:, i] = np.where((kc[None] >= w[:, None]) & (kc[None] < w[:, None] + 16), 0.0, MASKED)
            i += 1
    put("na_mask", mask)
    put("block", np.broadcast_to(np.arange(MOE_BLOCKS), (P, MOE_BLOCKS)))
    put("first", np.broadcast_to(PER_GROUP - np.arange(PER_GROUP), (P, PER_GROUP)))
    put("token", np.arange(SEQ).reshape(NQB, P).T)
    return t


def _arrays(i):
    one, end1, two, size2 = stream_plan()
    w_in = i["w_in"][0]
    cut = np.cumsum([0, D_RNN, D_RNN, D, KV_RANK, 512, IDX_DIM, IDX_HEADS, 2 * D])
    part = dict(zip(["xr", "gr", "q", "ckv", "qi", "ki", "wi", "mg"], [w_in[:, a:b] for a, b in zip(cut[:-1], cut[1:])]))
    parts = {n: _chunks(part[n]) for n in ("xr", "gr", "q", "ckv", "qi", "mg")}
    mg = parts.pop("mg")
    wmod = i["w_mod"][0].T.reshape(-1, P, D)
    rest = wmod[MOD_FIRST:].reshape(-1, P, DC, P).transpose(0, 2, 1, 3).reshape(-1, P, P)
    for n in range(MG_SLOTS):
        parts[f"mg{n}"] = mg[n * CHUNKS:(n + 1) * CHUNKS]
        parts[f"mod{n}"] = rest[2 * n * CHUNKS:2 * (n + 1) * CHUNKS]
    parts["rg"] = np.stack([i["w_rg_a"][0], i["w_rg_x"][0]], 1).reshape(-1, P, P)
    parts["ki"] = _chunks(np.concatenate([part["ki"], part["ki"]], 1))
    parts["wi"] = _pack(part["wi"], 1)
    parts["rnn_out"] = _chunks(i["w_rnn_out"][0])
    parts["uk"] = _chunks(i["w_uk"][0].reshape(KV_RANK, -1))
    parts["uv"] = _blocks(i["w_uv"][0].reshape(KV_RANK, -1))
    parts["att_out"] = _chunks(i["w_att_out"][0])
    parts["out"] = _chunks(i["w_out"][0])
    parts["router"] = _pack(np.concatenate([i["w_group"][0], i["w_expert"][0]], 1), 3)
    first = _stream(one, end1, parts)

    layers = []
    for l in range(LAYERS):
        w = i["w_in_2"][l]
        cut = np.cumsum([0, 1024, 512, 1024, 512, MQ_RANK, 256, 32, 3 * D])
        part = dict(zip(["na_qk", "na_v", "df_qk", "df_v", "cq", "mckv", "kr", "gate"], [w[:, a:b] for a, b in zip(cut[:-1], cut[1:])]))
        parts = {n: _chunks(part[n]) for n in ("na_qk", "df_qk", "cq", "mckv")}
        parts["na_v"], parts["df_v"] = _blocks(part["na_v"]), _blocks(part["df_v"])
        parts["kr"] = _chunks(_wide(np.concatenate([part["mckv"][:, 192:], part["kr"]], 1)))
        for b, name in enumerate(("na_gb", "df_gb", "ml_gb")):
            g = _chunks(part["gate"][:, b * D:(b + 1) * D]).reshape(DC, DC, P, P)
            o = _chunks(i["w_branch_2"][l, b]).reshape(DC, 4, P, P)
            parts[name] = np.concatenate([g, o], 1).reshape(-1, P, P)
        qb = i["w_mla_qb_2"][l].reshape(MQ_RANK, HEADS, MLA_QK)
        parts["qb"] = np.concatenate([_chunks(_wide(qb[:, h])) for h in range(HEADS)])
        kvb = i["w_mla_kvb_2"][l].reshape(256, HEADS, 2, 64)
        parts["kvb_k"] = _chunks(kvb[:, :, 0].reshape(256, 512))
        parts["kvb_v"] = _blocks(kvb[:, :, 1].reshape(256, 512))
        parts["out2"] = _chunks(i["w_out_2"][l])
        gu = i["w_ffn_in_2"][l].reshape(D, 2, FFC, P).transpose(0, 2, 1, 3).reshape(D, 2 * D_FF)
        parts["ffn_in"] = _chunks(gu)
        parts["ffn_out"] = _chunks(i["w_ffn_out_2"][l])
        layers.append(_stream(two, size2, parts))

    vcol, n = vector_plan()
    names = {"b_mod": "b_mod", "norm1_g": "norm1_g", "conv_w": "conv_w", "conv_b": "conv_b", "b_rg_a": "b_rg_a",
             "b_rg_x": "b_rg_x", "lam": "lru_lambda", "kv_g": "kv_norm_g", "norm2_g": "norm2_g", "final_g": "final_g",
             "ln_in_g": "ln_in_g_2", "ln_in_b": "ln_in_b_2"}
    per = {"b_gate": "b_gate_2", "subln": "diff_subln_g_2", "mq_g": "mla_q_norm_g_2", "mkv_g": "mla_kv_norm_g_2",
           "ln1_g": "ln1_g_2", "ln1_b": "ln1_b_2", "ln2_g": "ln2_g_2", "ln2_b": "ln2_b_2"}
    vectors = np.zeros((P, n), np.float32)
    for name, (a, b) in vcol.items():
        v = i[names[name]] if name in names else i[per[name[:-1]]][int(name[-1])]
        vectors[:, a:b] = _columns(np.asarray(v).reshape(-1))

    rpb = np.zeros((LAYERS, HEADS, P, 3, GRID_ROWS, 16), np.float32)
    table = np.zeros((LAYERS, HEADS, 15, 31 + 64), np.float32)
    table[:, :, :, 32:63] = i["na_rpb_2"]
    for qr in range(GRID_ROWS):
        for qc in range(16):
            for dj in range(3):
                b = 32 + 16 * (dj - 1) - qc + 15
                rpb[:, :, qr * 16 + qc, dj] = table[:, :, 7 - qr:15 - qr, b:b + 16]

    def moe(w, cols):
        e, k, m = w.shape
        return np.ascontiguousarray(w.reshape(e, k // P, P, m).transpose(0, 2, 1, 3)).reshape(e, P, -1)

    return {
        "xT": np.ascontiguousarray(i["x"][0].T.reshape(DC, P, SEQ).transpose(1, 0, 2)),
        "crow": i["c"], "wmod": np.ascontiguousarray(wmod[:MOD_FIRST].transpose(1, 0, 2)),
        "wfirst": first, "wlayers": np.stack(layers), "consts": _constants(), "vectors": vectors,
        "brow": np.concatenate([i["b_group"][0], i["b_expert"][0]])[None, :],
        "lamv": i["diff_lambda_2"].reshape(1, -1),
        "rpb": rpb.reshape(LAYERS, HEADS, P, -1),
        "w1": moe(i["moe_w1"][0], 512), "w3": moe(i["moe_w3"][0], 512), "w2": moe(i["moe_w2"][0], 1024),
    }


def kernel(**inputs):
    import concourse.bacc as bacc
    from concourse.bass_utils import run_bass_kernel_spmd as run

    nc = bacc.Bacc("TRN2", target_bir_lowering=False, num_devices=1)
    arrays = _arrays(inputs)
    args = {name: nc.dram_tensor(name, a.shape, mybir.dt.from_np(a.dtype), kind="ExternalInput").ap() for name, a in arrays.items()}
    args["out"] = nc.dram_tensor("out", (P, DC, SEQ), F32, kind="ExternalOutput").ap()
    build(nc, **args)
    got = run(nc, [arrays], core_ids=[0]).results[0]["out"]
    got = got.transpose(2, 1, 0).reshape(NA_TILES, GRID_ROWS, 16, D).transpose(1, 0, 2, 3)
    return np.ascontiguousarray(got).reshape(1, SEQ, D)
```
